# Optimizing a Trainium2 kernel written in Bass

```python
import jax, jax.numpy as jnp
from jax import lax
import numpy as np

D_MODEL = 1024
BATCH = 1
SEQ = 512
DEPTH = 2

MEM_LEN = 256
BRANCH_WIDTH = D_MODEL // 2
N_BRANCH = 4

RWKV_HEAD_DIM = 64
RWKV_HEADS = BRANCH_WIDTH // RWKV_HEAD_DIM
RWKV_LORA = 64
RWKV_GN_EPS = 64e-5

MLA_NOPE = 64
MLA_ROPE = 32
MLA_V = 64
MLA_HEADS = BRANCH_WIDTH // MLA_V
MLA_Q_LORA = 3 * D_MODEL // 8
MLA_KV_LORA = D_MODEL // 4
ROPE_THETA = 10000.0
Q_BLOCK = 128

CONV_KERNEL = 31

XATTN_HEADS = 4
XATTN_HEAD_DIM = BRANCH_WIDTH // XATTN_HEADS

DEEPNORM_ALPHA = (2.0 * DEPTH) ** 0.25
DEEPNORM_BETA = (8.0 * DEPTH) ** -0.25
LN_EPS = 1e-5
RMS_EPS = 1e-6
MASK_VALUE = -1e30

RWKV_SHIFT_COLS = 3 * BRANCH_WIDTH + 2 * RWKV_LORA
SPLIT_SIZES = (
    RWKV_SHIFT_COLS, BRANCH_WIDTH,
    MLA_Q_LORA, MLA_KV_LORA, MLA_ROPE, BRANCH_WIDTH,
    2 * BRANCH_WIDTH, BRANCH_WIDTH,
    BRANCH_WIDTH, BRANCH_WIDTH,
    N_BRANCH * D_MODEL,
)
SPLIT_POINTS = tuple(int(s) for s in np.cumsum(SPLIT_SIZES)[:-1])
IN_COLS = int(sum(SPLIT_SIZES))


def _layer_norm(x, g, b):
    xf = x.astype(jnp.float32)
    mu = jnp.mean(xf, -1, keepdims=True)
    var = jnp.mean(jnp.square(xf - mu), -1, keepdims=True)
    return ((xf - mu) * lax.rsqrt(var + LN_EPS)).astype(x.dtype) * g + b

def _rms_norm(x, g):
    xf = x.astype(jnp.float32)
    y = xf * lax.rsqrt(jnp.mean(jnp.square(xf), -1, keepdims=True) + RMS_EPS)
    return y.astype(x.dtype) * g

def _rope(x, cos, sin):
    half = x.shape[-1] // 2
    x1, x2 = x[..., :half], x[..., half:]
    return jnp.concatenate([x1 * cos - x2 * sin, x1 * sin + x2 * cos], axis=-1)

def _rwkv7_branch(p, gate, mu, w0, w2, a0, a2, k_k, k_a, r_k, lnx_g, lnx_b):
    B, S, _ = p.shape
    H, N, W = RWKV_HEADS, RWKV_HEAD_DIM, BRANCH_WIDTH
    p_prev = jnp.pad(p, ((0, 0), (1, 0), (0, 0)))[:, :-1]
    p = p + mu * (p_prev - p)
    r, k, v, wl, al = jnp.split(p, (W, 2 * W, 3 * W, 3 * W + RWKV_LORA), axis=-1)
    w_log = -jax.nn.softplus(-(w0 + jnp.tanh(wl) @ w2)) - 0.5
    decay = jnp.exp(-jnp.exp(w_log.astype(jnp.float32)))
    a = jax.nn.sigmoid(a0 + al @ a2)

    def heads(t):
        return t.reshape(B, S, H, N).astype(jnp.float32)

    kk = heads(k * k_k)
    kk = kk / jnp.maximum(jnp.linalg.norm(kk, axis=-1, keepdims=True), 1e-12)
    k = k * (1.0 + (a - 1.0) * k_a)
    r_h, k_h, v_h, a_h, w_h = heads(r), heads(k), heads(v), heads(a), heads(decay)
    xs = tuple(jnp.moveaxis(t, 1, 0) for t in (r_h, w_h, k_h, v_h, -kk, kk * a_h))

    def step(state, inp):
        r_t, w_t, k_t, v_t, a_t, b_t = inp
        sa = jnp.einsum('bhvk,bhk->bhv', state, a_t)
        state = (state * w_t[:, :, None, :] + sa[..., None] * b_t[:, :, None, :]
                 + v_t[..., None] * k_t[:, :, None, :])
        return state, jnp.einsum('bhvk,bhk->bhv', state, r_t)

    s0 = jnp.zeros((B, H, N, N), jnp.float32)
    _, y = lax.scan(step, s0, xs)
    y = jnp.moveaxis(y, 0, 1)
    y_mu = jnp.mean(y, -1, keepdims=True)
    y_var = jnp.mean(jnp.square(y - y_mu), -1, keepdims=True)
    y = ((y - y_mu) * lax.rsqrt(y_var + RWKV_GN_EPS)).reshape(B, S, W) * lnx_g + lnx_b
    bonus = jnp.sum(r_h * k_h * r_k, axis=-1, keepdims=True) * v_h
    y = y + bonus.reshape(B, S, W)
    return y.astype(gate.dtype) * jax.nn.silu(gate)

def _causal_block_attention(q, k, v, scale):
    B, S, H, Dq = q.shape
    nb = S // Q_BLOCK
    qb = jnp.moveaxis(q.reshape(B, nb, Q_BLOCK, H, Dq), 1, 0)
    key_idx = jnp.arange(S)

    def one_block(args):
        q_blk, i = args
        s = jnp.einsum('bqhd,bkhd->bhqk', q_blk, k).astype(jnp.float32) * scale
        q_idx = i * Q_BLOCK + jnp.arange(Q_BLOCK)
        s = jnp.where(key_idx[None, :] <= q_idx[:, None], s, MASK_VALUE)
        pr = jax.nn.softmax(s, axis=-1).astype(v.dtype)
        return jnp.einsum('bhqk,bkhd->bqhd', pr, v)

    o = lax.map(one_block, (qb, jnp.arange(nb)))
    return jnp.moveaxis(o, 0, 1).reshape(B, S, H, v.shape[-1])

def _mla_branch(q_lat, kv_lat, k_pe, gate, cos, sin, q_norm, w_uq, kv_norm, w_ukv):
    B, S, _ = q_lat.shape
    H = MLA_HEADS
    q = (_rms_norm(q_lat, q_norm) @ w_uq).reshape(B, S, H, MLA_NOPE + MLA_ROPE)
    kv = (_rms_norm(kv_lat, kv_norm) @ w_ukv).reshape(B, S, H, MLA_NOPE + MLA_V)
    q_nope, q_pe = q[..., :MLA_NOPE], q[..., MLA_NOPE:]
    k_nope, v = kv[..., :MLA_NOPE], kv[..., MLA_NOPE:]
    q_pe = _rope(q_pe, cos[:, :, None, :], sin[:, :, None, :])
    k_pe = _rope(k_pe, cos, sin)
    q_full = jnp.concatenate([q_nope, q_pe], axis=-1)
    k_full = jnp.concatenate(
        [k_nope, jnp.broadcast_to(k_pe[:, :, None, :], (B, S, H, MLA_ROPE))], axis=-1)
    o = _causal_block_attention(q_full, k_full, v, (MLA_NOPE + MLA_ROPE) ** -0.5)
    return o.reshape(B, S, BRANCH_WIDTH) * jax.nn.silu(gate)

def _conformer_conv_branch(u, gate, conv_w, conv_b, ln_g, ln_b):
    val, glu_gate = jnp.split(u, 2, axis=-1)
    h = val * jax.nn.sigmoid(glu_gate)
    h = lax.conv_general_dilated(
        h, conv_w[:, None, :], window_strides=(1,), padding=[(CONV_KERNEL - 1, 0)],
        dimension_numbers=('NWC', 'WIO', 'NWC'), feature_group_count=BRANCH_WIDTH) + conv_b
    h = jax.nn.silu(_layer_norm(h, ln_g, ln_b))
    return h * jax.nn.silu(gate)

def _memory_xattn_branch(q, gate, mem, w_mem_kv):
    B, S, _ = q.shape
    M = mem.shape[1]
    kv = mem @ w_mem_kv
    k = kv[..., :BRANCH_WIDTH].reshape(B, M, XATTN_HEADS, XATTN_HEAD_DIM)
    v = kv[..., BRANCH_WIDTH:].reshape(B, M, XATTN_HEADS, XATTN_HEAD_DIM)
    qh = q.reshape(B, S, XATTN_HEADS, XATTN_HEAD_DIM)
    s = jnp.einsum('bshd,bmhd->bhsm', qh, k).astype(jnp.float32) * XATTN_HEAD_DIM ** -0.5
    pr = jax.nn.softmax(s, axis=-1).astype(v.dtype)
    o = jnp.einsum('bhsm,bmhd->bshd', pr, v).reshape(B, S, BRANCH_WIDTH)
    return o * jax.nn.silu(gate)

def first_inputs(seed: int = 0) -> dict:
    key = jax.random.key(seed)
    ks = jax.random.split(key, 32)
    f32 = jnp.float32
    L, D, W = DEPTH, D_MODEL, BRANCH_WIDTH

    def nrm(k, shape, scale):
        return jax.random.normal(k, shape, f32) * scale

    x = jax.random.normal(ks[0], (BATCH, SEQ, D), f32)
    mem = jax.random.normal(ks[1], (BATCH, MEM_LEN, D), f32)
    start = jax.random.randint(ks[2], (BATCH, 1), 0, 4096, dtype=jnp.int32)
    positions = start + jnp.arange(SEQ, dtype=jnp.int32)[None, :]
    return {
        "x": x,
        "mem": mem,
        "positions": positions,
        "w_in": nrm(ks[3], (L, D, IN_COLS), D ** -0.5),
        "b_gate": nrm(ks[4], (L, N_BRANCH, D), 0.1),
        "rwkv_mu": jax.random.uniform(ks[5], (L, RWKV_SHIFT_COLS), f32),
        "rwkv_w0": jax.random.uniform(ks[6], (L, W), f32, -6.0, 0.0),
        "rwkv_w2": nrm(ks[7], (L, RWKV_LORA, W), 0.5 * RWKV_LORA ** -0.5),
        "rwkv_a0": nrm(ks[8], (L, W), 0.1),
        "rwkv_a2": nrm(ks[9], (L, RWKV_LORA, W), 0.5 * RWKV_LORA ** -0.5),
        "rwkv_k_k": 0.85 + nrm(ks[10], (L, W), 0.05),
        "rwkv_k_a": 1.0 + nrm(ks[11], (L, W), 0.05),
        "rwkv_r_k": nrm(ks[12], (L, RWKV_HEADS, RWKV_HEAD_DIM), 0.3),
        "rwkv_lnx_g": 1.0 + nrm(ks[13], (L, W), 0.02),
        "rwkv_lnx_b": nrm(ks[14], (L, W), 0.02),
        "mla_q_norm": 1.0 + nrm(ks[15], (L, MLA_Q_LORA), 0.02),
        "mla_w_uq": nrm(ks[16], (L, MLA_Q_LORA, MLA_HEADS * (MLA_NOPE + MLA_ROPE)), MLA_Q_LORA ** -0.5),
        "mla_kv_norm": 1.0 + nrm(ks[17], (L, MLA_KV_LORA), 0.02),
        "mla_w_ukv": nrm(ks[18], (L, MLA_KV_LORA, MLA_HEADS * (MLA_NOPE + MLA_V)), MLA_KV_LORA ** -0.5),
        "conv_w": nrm(ks[19], (L, CONV_KERNEL, W), CONV_KERNEL ** -0.5),
        "conv_b": nrm(ks[20], (L, W), 0.02),
        "conv_ln_g": 1.0 + nrm(ks[21], (L, W), 0.02),
        "conv_ln_b": nrm(ks[22], (L, W), 0.02),
        "xattn_w_mem_kv": nrm(ks[23], (L, D, 2 * W), D ** -0.5),
        "w_o_branch": nrm(ks[24], (L, N_BRANCH, W, D), DEEPNORM_BETA * W ** -0.5),
        "w_out": nrm(ks[25], (L, D, D), DEEPNORM_BETA * D ** -0.5),
        "ln_g": 1.0 + nrm(ks[26], (L, D), 0.02),
        "ln_b": nrm(ks[27], (L, D), 0.02),
    }

def first_block(x, mem, positions, w_in, b_gate, rwkv_mu, rwkv_w0, rwkv_w2, rwkv_a0, rwkv_a2,
              rwkv_k_k, rwkv_k_a, rwkv_r_k, rwkv_lnx_g, rwkv_lnx_b, mla_q_norm, mla_w_uq,
              mla_kv_norm, mla_w_ukv, conv_w, conv_b, conv_ln_g, conv_ln_b, xattn_w_mem_kv,
              w_o_branch, w_out, ln_g, ln_b):
    B, S, D = x.shape
    inv_freq = ROPE_THETA ** (-jnp.arange(0, MLA_ROPE, 2, dtype=jnp.float32) / MLA_ROPE)
    ang = positions.astype(jnp.float32)[..., None] * inv_freq
    cos = jnp.cos(ang).astype(x.dtype)
    sin = jnp.sin(ang).astype(x.dtype)
    for l in range(DEPTH):
        h = x @ w_in[l]
        (rw_p, rw_g, q_lat, kv_lat, k_pe, mla_g, conv_u, conv_g, xq, xg,
         merge) = jnp.split(h, SPLIT_POINTS, axis=-1)
        y_rwkv = _rwkv7_branch(rw_p, rw_g, rwkv_mu[l], rwkv_w0[l], rwkv_w2[l], rwkv_a0[l],
                               rwkv_a2[l], rwkv_k_k[l], rwkv_k_a[l], rwkv_r_k[l],
                               rwkv_lnx_g[l], rwkv_lnx_b[l])
        y_mla = _mla_branch(q_lat, kv_lat, k_pe, mla_g, cos, sin, mla_q_norm[l], mla_w_uq[l],
                            mla_kv_norm[l], mla_w_ukv[l])
        y_conv = _conformer_conv_branch(conv_u, conv_g, conv_w[l], conv_b[l], conv_ln_g[l],
                                        conv_ln_b[l])
        y_mem = _memory_xattn_branch(xq, xg, mem, xattn_w_mem_kv[l])
        branches = jnp.stack([y_rwkv, y_mla, y_conv, y_mem], axis=2)
        proj = jnp.einsum('bsnc,ncd->bsnd', branches, w_o_branch[l])
        gates = jax.nn.sigmoid(merge.reshape(B, S, N_BRANCH, D) + b_gate[l])
        merged = jnp.sum(gates * proj, axis=2)
        out = merged @ w_out[l]
        x = _layer_norm(DEEPNORM_ALPHA * x + out, ln_g[l], ln_b[l])
    return x


GRID_W = 64
CTX_LEN = 256
HEAD_DIM = 64
ATTN_WIDTH = D_MODEL // 2
N_Q_HEADS = ATTN_WIDTH // HEAD_DIM
N_KV_HEADS = N_Q_HEADS // 4
GQA_GROUP = N_Q_HEADS // N_KV_HEADS
KV_WIDTH = N_KV_HEADS * HEAD_DIM
POOL_WINDOWS = (2, 4, 8, 16)
N_POOL_GROUPS = len(POOL_WINDOWS)
POOL_WIDTH = D_MODEL // 4
POOL_GROUP = POOL_WIDTH // N_POOL_GROUPS
N_FOURIER_GROUPS = 4
FOURIER_WIDTH = D_MODEL // 4
FOURIER_GROUP = FOURIER_WIDTH // N_FOURIER_GROUPS
MIX_WIDTH = ATTN_WIDTH + POOL_WIDTH + FOURIER_WIDTH
Q_END = ATTN_WIDTH
K_END = Q_END + KV_WIDTH
KV_END = K_END + KV_WIDTH
POOL_END = KV_END + POOL_WIDTH
IN_WIDTH = POOL_END + FOURIER_WIDTH
D_FF = -(-8 * D_MODEL // (3 * 256)) * 256
EPS = 1e-6


def rms_norm(x, g):
    xf = x.astype(jnp.float32)
    y = xf * lax.rsqrt(jnp.mean(xf * xf, axis=-1, keepdims=True) + EPS)
    return (y * g.astype(jnp.float32)).astype(x.dtype)

def axial_rope_tables(length):
    rows = length // GRID_W
    row_ids = jnp.repeat(jnp.arange(rows), GRID_W).astype(jnp.float32)
    col_ids = jnp.tile(jnp.arange(GRID_W), rows).astype(jnp.float32)
    n_freq = HEAD_DIM // 4
    freqs = ROPE_THETA ** (-jnp.arange(n_freq, dtype=jnp.float32) / n_freq)
    ang = jnp.stack([row_ids[:, None] * freqs, col_ids[:, None] * freqs], axis=1)
    return jnp.cos(ang), jnp.sin(ang)

def apply_rope(x, cos, sin):
    n_freq = HEAD_DIM // 4
    xf = x.astype(jnp.float32).reshape(*x.shape[:-1], 2, 2, n_freq)
    x1, x2 = xf[..., 0, :], xf[..., 1, :]
    cb, sb = cos[None, :, None], sin[None, :, None]
    out = jnp.stack([x1 * cb - x2 * sb, x2 * cb + x1 * sb], axis=-2)
    return out.reshape(x.shape).astype(x.dtype)

def gqa_softmax(qg, k, v):
    s = jnp.einsum('bqgrd,bkgd->bgrqk', qg, k, preferred_element_type=jnp.float32) * (HEAD_DIM ** -0.5)
    p = jax.nn.softmax(s, axis=-1).astype(v.dtype)
    return jnp.einsum('bgrqk,bkgd->bqgrd', p, v)

def latent_attention(q, k, v, k_ctx, v_ctx):
    b, s = q.shape[:2]
    n_blk = s // Q_BLOCK
    k_all = jnp.concatenate([k_ctx, k], axis=1)
    v_all = jnp.concatenate([v_ctx, v], axis=1)
    qb = q.reshape(b, n_blk, Q_BLOCK, N_KV_HEADS, GQA_GROUP, HEAD_DIM).transpose(1, 0, 2, 3, 4, 5)
    o = lax.map(lambda qblk: gqa_softmax(qblk, k_all, v_all), qb)
    return o.transpose(1, 0, 2, 3, 4, 5).reshape(b, s, ATTN_WIDTH)

def context_attention(q, k, v):
    b, cl = q.shape[:2]
    qg = q.reshape(b, cl, N_KV_HEADS, GQA_GROUP, HEAD_DIM)
    return gqa_softmax(qg, k, v).reshape(b, cl, ATTN_WIDTH)

def pool_mix(u, w_pool, pool_scale):
    b, length, _ = u.shape
    ug = u.astype(jnp.float32).reshape(b, length, N_POOL_GROUPS, POOL_GROUP)
    cs = jnp.concatenate([jnp.zeros((b, 1, N_POOL_GROUPS, POOL_GROUP), jnp.float32),
                          jnp.cumsum(ug, axis=1)], axis=1)
    t = jnp.arange(length)
    means = []
    for gi, w in enumerate(POOL_WINDOWS):
        lo = jnp.clip(t - w // 2, 0, length)
        hi = jnp.clip(t + w - w // 2, 0, length)
        cs_g = cs[:, :, gi]
        cnt = (hi - lo).astype(jnp.float32)
        means.append((cs_g[:, hi] - cs_g[:, lo]) / cnt[None, :, None])
    d = jnp.stack(means, axis=2) - ug
    y = jnp.einsum('blgc,gcd->blgd', d, w_pool.astype(jnp.float32)).reshape(b, length, POOL_WIDTH)
    return (y * pool_scale.astype(jnp.float32)).astype(u.dtype)

def fourier_mix(u, w_four):
    b, length, _ = u.shape
    ug = u.astype(jnp.float32).reshape(b, length, N_FOURIER_GROUPS, FOURIER_GROUP)
    f = jnp.fft.fft2(ug, axes=(1, 3), norm='ortho').real
    y = jnp.einsum('blgc,gcd->blgd', f, w_four.astype(jnp.float32))
    return y.reshape(b, length, FOURIER_WIDTH).astype(u.dtype)

def head_rms(x, g):
    return rms_norm(x, g)

def swiglu(h, w_gate_up, w_down):
    gate, up = jnp.split(h @ w_gate_up, 2, axis=-1)
    return (jax.nn.silu(gate) * up) @ w_down

def second_inputs(seed: int = 0) -> dict:
    key = jax.random.key(seed)
    ks = jax.random.split(key, 18)
    f32 = jnp.float32

    def nrm(k, shape, s):
        return jax.random.normal(k, shape, f32) * s

    return {
        "x": nrm(ks[0], (BATCH, SEQ, D_MODEL), 1.0),
        "c": nrm(ks[1], (BATCH, D_MODEL), 1.0),
        "ctx": nrm(ks[2], (BATCH, CTX_LEN, D_MODEL), 1.0),
        "c_ctx": nrm(ks[3], (D_MODEL,), 1.0),
        "w_ada": nrm(ks[4], (DEPTH, D_MODEL, 6 * D_MODEL), D_MODEL ** -0.5),
        "b_ada": nrm(ks[5], (DEPTH, 6 * D_MODEL), 0.01),
        "g_mix": 1.0 + nrm(ks[6], (DEPTH, D_MODEL), 0.02),
        "g_ffn": 1.0 + nrm(ks[7], (DEPTH, D_MODEL), 0.02),
        "w_in": nrm(ks[8], (DEPTH, D_MODEL, IN_WIDTH), D_MODEL ** -0.5),
        "q_gain": 1.0 + nrm(ks[9], (DEPTH, HEAD_DIM), 0.02),
        "k_gain": 1.0 + nrm(ks[10], (DEPTH, HEAD_DIM), 0.02),
        "w_pool": nrm(ks[11], (DEPTH, N_POOL_GROUPS, POOL_GROUP, POOL_GROUP), POOL_GROUP ** -0.5),
        "pool_scale": 1.0 + nrm(ks[12], (DEPTH, POOL_WIDTH), 0.02),
        "w_four": nrm(ks[13], (DEPTH, N_FOURIER_GROUPS, FOURIER_GROUP, FOURIER_GROUP), FOURIER_GROUP ** -0.5),
        "w_out": nrm(ks[14], (DEPTH, MIX_WIDTH, D_MODEL), MIX_WIDTH ** -0.5),
        "w_gate_up": nrm(ks[15], (DEPTH, D_MODEL, 2 * D_FF), D_MODEL ** -0.5),
        "w_down": nrm(ks[16], (DEPTH, D_FF, D_MODEL), D_FF ** -0.5),
    }

def second_block(x, c, ctx, c_ctx, w_ada, b_ada, g_mix, g_ffn, w_in, q_gain, k_gain,
              w_pool, pool_scale, w_four, w_out, w_gate_up, w_down):
    b, s, _ = x.shape
    cl = ctx.shape[1]
    cos, sin = axial_rope_tables(s)
    sc, scc = jax.nn.silu(c), jax.nn.silu(c_ctx)
    for i in range(DEPTH):
        update_ctx = i < DEPTH - 1
        mod_x = (sc @ w_ada[i] + b_ada[i])[:, None, :]
        mod_c = scc @ w_ada[i] + b_ada[i]
        sh1, sc1, ga1, sh2, sc2, ga2 = jnp.split(mod_x, 6, axis=-1)
        csh1, csc1, cga1, csh2, csc2, cga2 = jnp.split(mod_c, 6, axis=-1)

        hx = rms_norm(x, g_mix[i]) * (1.0 + sc1) + sh1
        hc = rms_norm(ctx, g_mix[i]) * (1.0 + csc1) + csh1
        zx = hx @ w_in[i]
        if update_ctx:
            zc = hc @ w_in[i]
            zc_kv = zc[..., Q_END:KV_END]
        else:
            zc_kv = hc @ w_in[i][:, Q_END:KV_END]
        kc = head_rms(zc_kv[..., :KV_WIDTH].reshape(b, cl, N_KV_HEADS, HEAD_DIM), k_gain[i])
        vc = zc_kv[..., KV_WIDTH:].reshape(b, cl, N_KV_HEADS, HEAD_DIM)

        q = apply_rope(head_rms(zx[..., :Q_END].reshape(b, s, N_Q_HEADS, HEAD_DIM), q_gain[i]), cos, sin)
        k = apply_rope(head_rms(zx[..., Q_END:K_END].reshape(b, s, N_KV_HEADS, HEAD_DIM), k_gain[i]), cos, sin)
        v = zx[..., K_END:KV_END].reshape(b, s, N_KV_HEADS, HEAD_DIM)
        mx = jnp.concatenate([
            latent_attention(q, k, v, kc, vc),
            pool_mix(zx[..., KV_END:POOL_END], w_pool[i], pool_scale[i]),
            fourier_mix(zx[..., POOL_END:], w_four[i]),
        ], axis=-1)
        x = x + ga1 * (mx @ w_out[i])

        if update_ctx:
            qc = head_rms(zc[..., :Q_END].reshape(b, cl, N_Q_HEADS, HEAD_DIM), q_gain[i])
            mc = jnp.concatenate([
                context_attention(qc, kc, vc),
                pool_mix(zc[..., KV_END:POOL_END], w_pool[i], pool_scale[i]),
                fourier_mix(zc[..., POOL_END:], w_four[i]),
            ], axis=-1)
            ctx = ctx + cga1 * (mc @ w_out[i])

        fx = rms_norm(x, g_ffn[i]) * (1.0 + sc2) + sh2
        x = x + ga2 * swiglu(fx, w_gate_up[i], w_down[i])
        if update_ctx:
            fc = rms_norm(ctx, g_ffn[i]) * (1.0 + csc2) + csh2
            ctx = ctx + cga2 * swiglu(fc, w_gate_up[i], w_down[i])
    return x


def setup_inputs(seed=0):
    out = dict(first_inputs(seed))
    for name, value in second_inputs(seed + 1).items():
        if name != "x":
            out[name + "_2"] = value
    return out


def reference(
    x, mem, positions, w_in, b_gate, rwkv_mu, rwkv_w0, rwkv_w2, rwkv_a0, rwkv_a2, rwkv_k_k,
    rwkv_k_a, rwkv_r_k, rwkv_lnx_g, rwkv_lnx_b, mla_q_norm, mla_w_uq, mla_kv_norm, mla_w_ukv,
    conv_w, conv_b, conv_ln_g, conv_ln_b, xattn_w_mem_kv, w_o_branch, w_out, ln_g, ln_b, c_2,
    ctx_2, c_ctx_2, w_ada_2, b_ada_2, g_mix_2, g_ffn_2, w_in_2, q_gain_2, k_gain_2, w_pool_2,
    pool_scale_2, w_four_2, w_out_2, w_gate_up_2, w_down_2,
):
    x = first_block(
        x, mem, positions, w_in, b_gate, rwkv_mu, rwkv_w0, rwkv_w2, rwkv_a0, rwkv_a2, rwkv_k_k,
        rwkv_k_a, rwkv_r_k, rwkv_lnx_g, rwkv_lnx_b, mla_q_norm, mla_w_uq, mla_kv_norm,
        mla_w_ukv, conv_w, conv_b, conv_ln_g, conv_ln_b, xattn_w_mem_kv, w_o_branch, w_out,
        ln_g, ln_b,
    )
    return second_block(
        x, c_2, ctx_2, c_ctx_2, w_ada_2, b_ada_2, g_mix_2, g_ffn_2, w_in_2, q_gain_2, k_gain_2,
        w_pool_2, pool_scale_2, w_four_2, w_out_2, w_gate_up_2, w_down_2,
    )


_drawn_inputs = setup_inputs


def setup_inputs(seed=0):
    import zlib

    import numpy as np

    out = dict(_drawn_inputs(seed))
    spreads = {}
    factors = {'mem': 6.332,
     'b_gate': 8.0,
     'rwkv_w2': 8.0,
     'rwkv_a0': 8.0,
     'rwkv_a2': 2.762,
     'rwkv_k_k': 8.0,
     'rwkv_k_a': 8.0,
     'rwkv_lnx_g': 8.0,
     'rwkv_lnx_b': 8.0,
     'mla_q_norm': 8.0,
     'mla_w_uq': 5.014,
     'mla_kv_norm': 8.0,
     'mla_w_ukv': 3.745,
     'conv_b': 8.0,
     'conv_ln_g': 8.0,
     'conv_ln_b': 8.0,
     'xattn_w_mem_kv': 6.093,
     'ctx_2': 2.781,
     'b_ada_2': 2.886,
     'g_mix_2': 5.601,
     'g_ffn_2': 3.141,
     'q_gain_2': 8.0,
     'k_gain_2': 8.0,
     'pool_scale_2': 6.845}
    for name, (base, spread) in spreads.items():
        noise = np.random.default_rng([zlib.crc32(name.encode()), seed]).standard_normal(out[name].shape)
        drawn = base * np.exp(spread * noise) if base else spread * noise
        out[name] = __import__('jax').numpy.asarray(drawn.astype(out[name].dtype))
    for name, factor in factors.items():
        out[name] = (out[name] * factor).astype(out[name].dtype)
    return out
```

```python
from contextlib import ExitStack

import numpy as np

import concourse.bass as bass
from concourse import mybir
from concourse.alu_op_type import AluOpType as ALU

F32 = mybir.dt.float32
I32 = mybir.dt.int32
ACT = mybir.ActivationFunctionType
AX_X = mybir.AxisListType.X

P = 128
T = 512
D = 1024
DK = D // P
W = 512
WT = W // P
NB = 4
LAYERS = 2
MEM = 256
CTX = 256
HD = 64
CH = 64
NCH = T // CH
TAPS = 31
RW_TILES = 13
EXPH = float(np.exp(-0.5))
DEEP_ALPHA = (2.0 * LAYERS) ** 0.25
RING = 8
CW = 1024

PCOL = {}
_at = 0
for _name, _n in (("b_gate", 32), ("mu", 13), ("w0", 4), ("a0", 4), ("k_k", 4), ("k_a", 4), ("r_k", 4),
                  ("lnx_g", 4), ("lnx_b", 4), ("q_norm", 3), ("kv_norm", 2), ("conv_b", 4),
                  ("cln_g", 4), ("cln_b", 4), ("ln_g", 8), ("ln_b", 8), ("conv_w", WT * TAPS),
                  ("w2a2", 512)):
    PCOL[_name] = _at
    _at += _n
NPAR = _at

CCOL = {}
_at = 0
for _name, _n in (("ident", 128), ("head_ones", 128), ("ones", 128), ("tri", 256), ("m0", 128),
                  ("lev", 6 * 128), ("causal", 128), ("swap", 32), ("freq", 1), ("sign", 1),
                  ("eps", 4), ("reset", 512)):
    CCOL[_name] = _at
    _at += _n
NCST = _at

STAGE_CHUNKS = (("rwkv", RW_TILES), ("mla", 6 + 3 + 2), ("conv", 8), ("xattn", 4 + 8), ("gates", 16),
                ("merge", 6 * 8), ("out", 8))
FIRST = {}
_at = 0
for _name, _n in STAGE_CHUNKS:
    FIRST[_name] = _at
    _at += _n
NCHUNK1 = _at


class Names:

    def __init__(self, handles):
        self.handles, self.of = handles, {}

    def __call__(self, name):
        if name not in self.of:
            self.of[name] = self.handles[len(self.of)]
        return self.of[name]


class Stream:

    def __init__(self, ring, arrived, used, source):
        self.ring, self.arrived, self.used, self.source = ring, arrived, used, source
        self.sent = 0

    def send(self, sp, upto):
        for n in range(self.sent, upto):
            if n >= RING:
                sp.wait_ge(self.used, n - RING + 1)
            sp.dma_start(self.ring[:, n % RING, :], self.source(n)).then_inc(self.arrived[n % RING], 16)
        self.sent = max(self.sent, upto)

    def wait(self, pe, n):
        pe.wait_ge(self.arrived[n % RING], 16 * (n // RING + 1))

    def chunk(self, n):
        return self.ring[:, n % RING, :]


def tile_of(chunk, k, m=P):
    return chunk[:, k * m:(k + 1) * m]


def first_block(nc, ctx, A):
    pass


def build(nc, A, debug=None):
    with ExitStack() as ctx:
        def sb(name, shape, dt=F32):
            return ctx.enter_context(nc.sbuf_tensor(name, shape, dt))

        pools = [[nc.alloc_semaphore(f"stage{p}_{i}") for i in range(50)] for p in range(2)]
        arrived = [nc.alloc_semaphore(f"chunk_arrived{i}") for i in range(RING)]
        used = nc.alloc_semaphore("chunks_used")
        loaded = nc.alloc_semaphore("loaded")
        stored = nc.alloc_semaphore("stored")
        PS = ctx.enter_context(nc.psum_tensor("ps", [P, 8, 512], F32))
        turn = [0]

        def stage():
            turn[0] += 1
            return Names(pools[turn[0] % 2]), pools[(turn[0] + 1) % 2]

        xT = sb("xT", [P, DK, T])
        ring = sb("ring", [P, RING, CW])
        mods = sb("mods", [P, LAYERS, 96])
        with ExitStack() as one:
            first(nc, one, A, PS, xT, ring, mods, stage, arrived, used, loaded, debug)
        if debug is None or debug[0:2] == "mx":
            with ExitStack() as two:
                second(nc, two, A, PS, xT, ring, mods, stage, arrived, used, loaded, stored, debug)
        if debug is None or debug == "x1":
            with nc.Block() as block:
                @block.sync
                def _(sp):
                    sp.dma_start(A["out"], xT[:, :, :].rearrange("p k t -> p (k t)")).then_inc(stored, 16)
                    sp.wait_ge(stored, 16)


def clear(sp, sems):
    for s in sems:
        sp.sem_clear(s)


def attention(nc, stage, PS, ident, causal, heads, dv, rows, blocks, query, key, value, nkeys, scale, out,
              probs, probsT, small, part):
    S, other = stage()
    units = [(h, q) for h in range(heads) for q in range(blocks)]
    wide = max(nkeys) > 512
    nbuf = len(probs)

    def turns(q):
        return (nkeys[q] + 511) // 512

    before = [0]
    for h, q in units:
        before.append(before[-1] + turns(q))
    stats = small.rearrange("p (s u) -> p s u", s=4)

    def scores(i, q):
        a = 2 * (i % 2) if wide else i % 4
        return PS[:, a:a + 2, :].rearrange("p b n -> p (b n)")[:, 0:nkeys[q]] if wide else PS[:, a, 0:nkeys[q]]

    sbuf = 2 if wide else 4

    def finish(act, h):
        act.wait_ge(S("product"), h + 1)
        nc.scalar.activation(out(h), PS[part(h):part(h) + dv, 6 + h % 2, 0:blocks * P], ACT.Copy).then_inc(S("out"), 1)

    with nc.Block() as block:
        @block.sync
        def _(sp):
            clear(sp, other)

        @block.tensor
        def _(pe):
            def make_scores(i):
                h, q = units[i]
                if i >= sbuf:
                    pe.wait_ge(S("probs"), i - sbuf + 1)
                s = scores(i, q)
                for a in range(0, nkeys[q], 512):
                    b = min(a + 512, nkeys[q])
                    mm = nc.tensor.matmul(s[:, a:b], query(h)[:, q * P:(q + 1) * P], key(h)[:, a:b], start=True, stop=True)
                mm.then_inc(S("scores"), 1)

            def turn(i):
                h, q = units[i]
                pe.wait_ge(S("scaled"), i + 1)
                for j in range(turns(q)):
                    n = before[i] + j
                    if n >= 2:
                        pe.wait_ge(S("turned_out"), n - 1)
                    for kb in range(4 * j, min(4 * j + 4, nkeys[q] // P)):
                        mm = nc.tensor.transpose(PS[:, 4 + n % 2, (kb % 4) * P:(kb % 4 + 1) * P], probs[i % nbuf][:, kb * P:(kb + 1) * P], ident)
                    mm.then_inc(S("turned"), 1)

            def product(h):
                pe.wait_ge(S("turned_out"), before[blocks * (h + 1)])
                if h >= 2:
                    pe.wait_ge(S("out"), h - 1)
                top = nkeys[-1] // P
                for kb in range(top):
                    q0 = min(q for q in range(blocks) if nkeys[q] > kb * P)
                    mm = nc.tensor.matmul(PS[part(h):part(h) + dv, 6 + h % 2, q0 * P:blocks * P], value(h, kb), probsT[h % 2][:, kb, q0 * P:blocks * P],
                                          start=(kb == 0), stop=(kb == top - 1))
                mm.then_inc(S("product"), 1)

            lead = 2 if wide else 3
            for i in range(min(lead, len(units))):
                make_scores(i)
            for i in range(len(units)):
                if i + lead < len(units):
                    make_scores(i + lead)
                turn(i)
                if i % blocks == blocks - 1:
                    product(i // blocks)

        @block.scalar
        def _(act):
            for i, (h, q) in enumerate(units):
                act.wait_ge(S("negmax"), i + 1)
                if i >= nbuf:
                    act.wait_ge(S("turned"), before[i - nbuf + 1])
                nc.scalar.activation(probs[i % nbuf][:, 0:nkeys[q]], scores(i, q), ACT.Exp, scale=scale, bias=stats[:, 1, i:i + 1],
                                     accum_out=stats[:, 2, i:i + 1]).then_inc(S("probs"), 1)
                if i >= 1 and (i - 1) % blocks == blocks - 1:
                    finish(act, (i - 1) // blocks)
            finish(act, heads - 1)

        @block.vector
        def _(dve):
            v = nc.vector

            def maximum(i):
                h, q = units[i]
                dve.wait_ge(S("scores"), i + 1)
                s = scores(i, q)
                if causal is not None:
                    v.tensor_tensor(s[:, q * P:(q + 1) * P], s[:, q * P:(q + 1) * P], causal, ALU.add).then_inc(S("causal"), 1)
                    dve.wait_ge(S("causal"), i + 1)
                v.tensor_reduce(stats[:, 0, i:i + 1], s, AX_X, ALU.max).then_inc(S("max"), 1)
                dve.wait_ge(S("max"), i + 1)
                v.tensor_scalar(stats[:, 1, i:i + 1], stats[:, 0, i:i + 1], -scale, None, ALU.mult).then_inc(S("negmax"), 1)

            def normalise(i):
                h, q = units[i]
                dve.wait_ge(S("probs"), i + 1)
                v.reciprocal(stats[:, 3, i:i + 1], stats[:, 2, i:i + 1]).then_inc(S("inverse"), 1)
                dve.wait_ge(S("inverse"), i + 1)
                p = probs[i % nbuf][:, 0:nkeys[q]]
                v.tensor_scalar(p, p, stats[:, 3, i:i + 1], None, ALU.mult).then_inc(S("scaled"), 1)

            def turned_out(i):
                h, q = units[i]
                if q == 0 and h >= 2:
                    dve.wait_ge(S("product"), h - 1)
                for j in range(turns(q)):
                    n = before[i] + j
                    nb = min(4, nkeys[q] // P - 4 * j)
                    dve.wait_ge(S("turned"), n + 1)
                    v.tensor_copy(probsT[h % 2][:, 4 * j:4 * j + nb, q * P:(q + 1) * P],
                                  PS[:, 4 + n % 2, 0:nb * P].rearrange("p (k t) -> p k t", k=nb)).then_inc(S("turned_out"), 1)

            for i in range(len(units) + 2):
                if i < len(units):
                    maximum(i)
                if 1 <= i <= len(units):
                    normalise(i - 1)
                if i >= 2:
                    turned_out(i - 2)


def first(nc, ctx, A, PS, xT, ring, mods, stage, arrived, used, loaded, debug):
    def sb(name, shape, dt=F32):
        return ctx.enter_context(nc.sbuf_tensor(name, shape, dt))

    memT = sb("memT", [P, DK, MEM])
    cst = sb("cst", [P, NCST])
    par = sb("par", [P, NPAR])
    oneless = sb("oneless", [P, 4])
    rope = sb("rope", [P, 2, T])
    BR = sb("BR", [P, NB * WT, T])
    X = sb("X", [P, 44 * T])

    def C(name, n=1, k=0):
        a = CCOL[name] + k
        return cst[:, a:a + n]

    def par_col(name, k=0):
        a = PCOL[name] + k
        return par[:, a:a + 1]

    def XT(i, n=1):
        return X[:, i * T:(i + n) * T] if n == 1 else X[:, i * T:(i + n) * T].rearrange("p (n t) -> p n t", n=n)

    ident = C("ident", P)

    S, other = stage()
    with nc.Block() as block:
        @block.sync
        def _(sp):
            sp.dma_start(cst[:, :], A["cst1"]).then_inc(loaded, 16)
            sp.dma_start(xT[:, :, :].rearrange("p k t -> p (k t)"), A["xT"]).then_inc(loaded, 16)
            sp.dma_start(memT[:, :, :].rearrange("p k t -> p (k t)"), A["memT"]).then_inc(loaded, 16)
            sp.dma_start(X[64:96, 0:T].bitcast(I32), A["pos"].partition_broadcast(32)).then_inc(loaded, 16)
            sp.wait_ge(loaded, 64)

        @block.vector
        def _(dve):
            count = [0]

            def link(ins):
                count[0] += 1
                ins.then_inc(S("angle_step"), 1)
                dve.wait_ge(S("angle_step"), count[0])

            two_pi = 2.0 * np.pi
            c1 = float(np.float32(6.28125))
            c2 = float(np.float32(np.float32(two_pi - c1).view(np.uint32) & np.uint32(0xFFFFF000)) if False else np.float32(round((two_pi - c1) * 2 ** 19) / 2 ** 19))
            c3 = float(np.float32(two_pi - c1 - c2))
            magic = float(1.5 * 2 ** 23)
            pos, ang, turns, cosr = (X[64:96, i * T:(i + 1) * T] for i in range(4))
            rows = slice(64, 96)
            freq = cst[rows, CCOL["freq"]:CCOL["freq"] + 1]
            sgn = cst[rows, CCOL["sign"]:CCOL["sign"] + 1]
            dve.wait_ge(loaded, 64)
            v = nc.vector
            link(v.tensor_copy(turns, pos.bitcast(I32)))
            link(v.tensor_scalar(ang, turns, freq, None, ALU.mult))
            link(v.tensor_scalar(pos, ang, 1.0 / two_pi, None, ALU.mult))
            link(v.tensor_scalar(turns, pos, magic, None, ALU.add))
            link(v.tensor_scalar(turns, turns, magic, None, ALU.subtract))
            for c in (c1, c2, c3):
                link(v.scalar_tensor_tensor(out=ang, in0=turns, scalar=-c, in1=ang, op0=ALU.mult, op1=ALU.add))
            link(v.tensor_scalar(cosr, ang, float(np.pi / 2), None, ALU.add))
            link(v.tensor_scalar(pos, cosr, float(np.pi), None, ALU.is_gt))
            link(v.scalar_tensor_tensor(out=cosr, in0=pos, scalar=-two_pi, in1=cosr, op0=ALU.mult, op1=ALU.add))
            top = float(np.float32(3.1415925))
            link(v.tensor_scalar(cosr, cosr, top, -top, ALU.min, ALU.max))
            link(v.tensor_scalar(ang, ang, top, -top, ALU.min, ALU.max))
            v.memset(oneless[:, :], 0.0).then_inc(S("angles"), 1)
            dve.wait_ge(S("sines"), 2)
            v.tensor_scalar(rope[rows, 1, :], rope[rows, 1, :], sgn, None, ALU.mult).then_inc(S("signed"), 1)

        @block.scalar
        def _(act):
            act.wait_ge(S("angles"), 1)
            nc.scalar.activation(rope[64:96, 0, :], X[64:96, 3 * T:4 * T], ACT.Sin).then_inc(S("sines"), 1)
            nc.scalar.activation(rope[64:96, 1, :], X[64:96, T:2 * T], ACT.Sin).then_inc(S("sines"), 1)

    with nc.Fori(0, LAYERS if debug is None or debug[0:2] in ("x1", "mx") else 1) as layer:
        stream = Stream(ring, arrived, used,
                        lambda n: A["w1"][bass.ds(layer, 1), n, :, :].rearrange("l p c -> p (l c)"))

        def gemm(pe, bank, n, rhs, done, m=P, base=0, wait_bank=None):
            stream.wait(pe, n)
            for k in range(DK):
                mm = nc.tensor.matmul(PS[base:base + m, bank, 0:rhs.shape[2]], tile_of(stream.chunk(n), k)[:, 0:m],
                                      rhs[:, k, :], start=(k == 0), stop=(k == DK - 1))
                if k == 0 and n:
                    mm.then_inc(used, 1)
            mm.then_inc(done, 1)

        n0 = FIRST["rwkv"]
        P0 = 0
        praw = X[:, 30 * T:30 * T + 13 * 513].rearrange("p (c t) -> p c t", c=13)
        M = XT(0, 13)
        S, other = stage()
        with nc.Block() as block:
            @block.sync
            def _(sp):
                clear(sp, other)
                sp.dma_start(par[:, :], A["par1"][bass.ds(layer, 1), :, :].rearrange("l p c -> p (l c)")).then_inc(S("par"), 16)
                stream.send(sp, n0 + RW_TILES + RING - 1)
                sp.wait_ge(S("par"), 16)

            @block.tensor
            def _(pe):
                for t in range(RW_TILES):
                    if t >= 4:
                        pe.wait_ge(S("evicted"), t - 3)
                    gemm(pe, t % 4, n0 + t, xT[:, :, :], S("product"))

            @block.scalar
            def _(act):
                for t in range(RW_TILES):
                    act.wait_ge(S("product"), t + 1)
                    nc.scalar.activation(praw[:, t, 1:T + 1], PS[:, t % 4, :], ACT.Copy).then_inc(S("evicted"), 1)

            @block.vector
            def _(dve):
                v = nc.vector
                v.memset(praw[:, :, 0:1], 0.0).then_inc(S("zeroed"), 1)
                dve.wait_ge(S("zeroed"), 1)
                dve.wait_ge(S("par"), 16)
                v.tensor_scalar(oneless[:, :], par[:, PCOL["k_a"]:PCOL["k_a"] + 4], -1.0, 1.0, ALU.mult, ALU.add).then_inc(S("oneless"), 1)
                for t in range(RW_TILES):
                    dve.wait_ge(S("evicted"), t + 1)
                    v.tensor_tensor(XT(13 + t % 4), praw[:, t, 0:T], praw[:, t, 1:T + 1], ALU.subtract).then_inc(S("diff"), 1)
                    dve.wait_ge(S("diff"), t + 1)
                    v.scalar_tensor_tensor(out=M[:, t, :], in0=XT(13 + t % 4), scalar=par_col("mu", t),
                                           in1=praw[:, t, 1:T + 1], op0=ALU.mult, op1=ALU.add).then_inc(S("mixed"), 1)

        if debug == "mix":
            dump(nc, A, M, stage, loaded)
            return

        SG, LC = XT(13, 4), XT(17, 4)
        AA, TH = XT(21, 4), XT(25)
        PP = X[:, 26 * T:26 * T + 4 * NCH * 65].rearrange("p (c j t) -> p c j t", c=4, j=NCH)
        PI = XT(31, 4)
        KK, TMP = XT(35, 4), XT(39, 4)
        AR = BR[:, 0:8, :].rearrange("p a t -> p (a t)").rearrange("p (c q x t) -> p c q x t", c=4, q=4, x=2)
        BT, KT = BR[:, 8:12, :], BR[:, 12:16, :]
        S, other = stage()
        with nc.Block() as block:
            @block.sync
            def _(sp):
                clear(sp, other)

            @block.tensor
            def _(pe):
                w2a2 = par[:, PCOL["w2a2"]:PCOL["w2a2"] + 512]
                pe.wait_ge(S("tanh"), 1)
                for c in range(4):
                    nc.tensor.matmul(PS[:, c, :], w2a2[0:64, c * P:(c + 1) * P], TH[0:64, :], start=True, stop=True).then_inc(S("lora"), 1)
                for c in range(4):
                    nc.tensor.matmul(PS[:, 4 + c, :], w2a2[64:128, c * P:(c + 1) * P], M[64:128, 12, :], start=True, stop=True).then_inc(S("lora"), 1)
                for c in range(4):
                    pe.wait_ge(S("ksq"), c + 1)
                    pe.wait_ge(S("gates"), 4)
                    nc.tensor.matmul(PS[:, c, :], C("head_ones", P), TMP[:, c, :], start=True, stop=True).then_inc(S("knorm2"), 1)
                for c in range(4):
                    pe.wait_ge(S("rkr"), c + 1)
                    pe.wait_ge(S("gates"), 8)
                    nc.tensor.matmul(PS[:, 4 + c, :], C("head_ones", P), TMP[:, c, :], start=True, stop=True).then_inc(S("bonus_sum"), 1)

            @block.scalar
            def _(act):
                a = nc.scalar
                a.activation(TH[0:64, :], M[0:64, 12, :], ACT.Tanh).then_inc(S("tanh"), 1)
                for c in range(4):
                    act.wait_ge(S("lora"), c + 1)
                    a.activation(SG[:, c, :], PS[:, c, :], ACT.Sigmoid, bias=par_col("w0", c)).then_inc(S("gates"), 1)
                for c in range(4):
                    act.wait_ge(S("lora"), 4 + c + 1)
                    a.activation(AA[:, c, :], PS[:, 4 + c, :], ACT.Sigmoid, bias=par_col("a0", c)).then_inc(S("gates"), 1)
                for c in range(4):
                    act.wait_ge(S("kraw"), c + 1)
                    a.activation(TMP[:, c, :], KK[:, c, :], ACT.Square).then_inc(S("ksq"), 1)
                for c in range(4):
                    act.wait_ge(S("knorm2"), c + 1)
                    a.activation(TMP[:, c, :], PS[:, c, :], ACT.Sqrt).then_inc(S("knorm"), 1)
                for c in range(4):
                    act.wait_ge(S("cum"), c + 1)
                    a.activation(PP[:, c, :, 1:65], LC[:, c, :].rearrange("p (j t) -> p j t", j=NCH), ACT.Exp, scale=-EXPH).then_inc(S("decays"), 1)
                    a.activation(PI[:, c, :], LC[:, c, :], ACT.Exp, scale=EXPH).then_inc(S("decays"), 1)

            @block.vector
            def _(dve):
                v = nc.vector
                v.memset(PP[:, :, :, 0:1], 1.0).then_inc(S("first_decay"), 1)
                for c in range(4):
                    v.tensor_scalar(KK[:, c, :], M[:, 4 + c, :], par_col("k_k", c), None, ALU.mult).then_inc(S("kraw"), 1)
                for c in range(4):
                    dve.wait_ge(S("gates"), c + 1)
                    v.tensor_tensor_scan(LC[:, c, :], C("reset", T), SG[:, c, :], 0.0, ALU.mult, ALU.add).then_inc(S("cum"), 1)
                for c in range(4):
                    dve.wait_ge(S("gates"), 4 + c + 1)
                    dve.wait_ge(S("cum"), c + 1)
                    v.tensor_scalar(SG[:, c, :], AA[:, c, :], par_col("k_a", c), oneless[:, c:c + 1], ALU.mult, ALU.add).then_inc(S("kscale"), 1)
                for c in range(4):
                    dve.wait_ge(S("kscale"), c + 1)
                    v.tensor_tensor(M[:, 4 + c, :], M[:, 4 + c, :], SG[:, c, :], ALU.mult).then_inc(S("kmod"), 1)
                for c in range(4):
                    dve.wait_ge(S("knorm"), c + 1)
                    v.tensor_scalar(TMP[:, c, :], TMP[:, c, :], 1e-12, None, ALU.max).then_inc(S("kfloor"), 1)
                for c in range(4):
                    dve.wait_ge(S("kfloor"), c + 1)
                    dve.wait_ge(S("kmod"), c + 1)
                    v.reciprocal(SG[:, c, :], TMP[:, c, :]).then_inc(S("kinv"), 1)
                for c in range(4):
                    dve.wait_ge(S("kinv"), c + 1)
                    v.tensor_tensor(KK[:, c, :], KK[:, c, :], SG[:, c, :], ALU.mult).then_inc(S("kk"), 1)
                for c in range(4):
                    dve.wait_ge(S("kinv"), 4)
                    dve.wait_ge(S("kmod"), c + 1)
                    v.scalar_tensor_tensor(out=TMP[:, c, :], in0=M[:, c, :], scalar=par_col("r_k", c), in1=M[:, 4 + c, :],
                                           op0=ALU.mult, op1=ALU.mult).then_inc(S("rkr"), 1)
                for c in range(4):
                    dve.wait_ge(S("kk"), c + 1)
                    v.tensor_tensor(AA[:, c, :], AA[:, c, :], KK[:, c, :], ALU.mult).then_inc(S("b0"), 1)
                for c in range(4):
                    dve.wait_ge(S("decays"), 2 * c + 2)
                    dve.wait_ge(S("first_decay"), 1)
                    dve.wait_ge(S("b0"), c + 1)
                    for q in range(4):
                        before = PP[:, c, 2 * q:2 * q + 2, 0:64]
                        upto = PP[:, c, 2 * q:2 * q + 2, 1:65]
                        sl = slice(q * P, (q + 1) * P)
                        v.scalar_tensor_tensor(out=AR[:, c, q, 0, :].rearrange("p (j t) -> p j t", j=2),
                                               in0=KK[:, c, sl].rearrange("p (j t) -> p j t", j=2), scalar=-1.0,
                                               in1=before, op0=ALU.mult, op1=ALU.mult).then_inc(S("done"), 1)
                        v.tensor_tensor(AR[:, c, q, 1, :].rearrange("p (j t) -> p j t", j=2),
                                        M[:, c, sl].rearrange("p (j t) -> p j t", j=2), upto, ALU.mult).then_inc(S("done"), 1)
                    v.tensor_tensor(BT[:, c, :], AA[:, c, :], PI[:, c, :], ALU.mult).then_inc(S("done"), 1)
                    v.tensor_tensor(KT[:, c, :], M[:, 4 + c, :], PI[:, c, :], ALU.mult).then_inc(S("done"), 1)
                for c in range(4):
                    dve.wait_ge(S("bonus_sum"), c + 1)
                    dve.wait_ge(S("done"), 10 * (c + 1))
                    v.tensor_tensor(M[:, c, :], PS[:, 4 + c, :], M[:, 8 + c, :], ALU.mult).then_inc(S("bonus"), 1)

        if debug == "prep":
            dump(nc, A, M, stage, loaded)
            return

        BON = M[:, 0:4, :]
        VF = M[:, 8:12, :]
        TB, TK, TV = XT(12, 4), XT(16, 4), XT(4, 4)
        GB, GK = X[:, 20 * T:24 * T].rearrange("p (h x t) -> p h x t", h=8, x=2), X[:, 32 * T:36 * T].rearrange("p (h x t) -> p h x t", h=8, x=2)
        DT = X[:, 36 * T:38 * T].rearrange("p (h t) -> p h t", h=8)
        DD = X[:, 38 * T:40 * T].rearrange("p (h t) -> p h t", h=8)
        XX = X[:, 40 * T:42 * T].rearrange("p (h t) -> p h t", h=8)
        MK = X[:, 42 * T:44 * T].rearrange("p (h t) -> p h t", h=8)
        PC = X[:, 31 * T + 0:31 * T + 32].rearrange("p (c j) -> p c j", c=4)
        ST, SN, PCM = (XT(i).rearrange("p (c v) -> p c v", c=4) for i in (24, 30, 9))
        ZS, US = XT(25), XT(8)
        S, other = stage()
        with nc.Block() as block:
            @block.sync
            def _(sp):
                clear(sp, other)

            @block.tensor
            def _(pe):
                for i in range(12):
                    src = (BT, KT, VF)[i // 4]
                    if i >= 4:
                        pe.wait_ge(S("tok"), i - 3)
                    for c in range(4):
                        mm = nc.tensor.transpose(PS[:, i % 4, c * P:(c + 1) * P], src[:, c, (i % 4) * P:(i % 4 + 1) * P], ident)
                    mm.then_inc(S("turned"), 1)

            @block.scalar
            def _(act):
                for i in range(12):
                    act.wait_ge(S("turned"), i + 1)
                    dst = (TB, TK, TV)[i // 4]
                    nc.scalar.activation(dst[:, i % 4, :], PS[:, i % 4, :], ACT.Copy).then_inc(S("tok"), 1)

            @block.vector
            def _(dve):
                nc.vector.tensor_copy(PC, PP[:, :, :, 64]).then_inc(S("pc"), 1)
                nc.vector.memset(XT(24), 0.0).then_inc(S("pc"), 1)
                nc.vector.memset(ZS, 0.0).then_inc(S("pc"), 1)

        YY = XT(26, 4)
        for q in range(4):
            S, other = stage()
            GR = slice(q * P, (q + 1) * P)
            with nc.Block() as block:
                @block.sync
                def _(sp):
                    clear(sp, other)

                @block.tensor
                def _(pe):
                    for g in range(2):
                        for which, src in ((0, BT), (1, KT)):
                            for half in range(2):
                                i = 4 * g + 2 * which + half
                                if i >= 4:
                                    pe.wait_ge(S("masked"), i - 3)
                                for hh in range(2):
                                    h = 4 * g + 2 * hh + half
                                    c, b = h // 2, 64 * (h % 2)
                                    mm = nc.tensor.matmul(PS[:, i % 4, hh * 256:(hh + 1) * 256], src[b:b + 64, c, GR],
                                                          AR[b:b + 64, c, q, :, :], start=True, stop=True)
                                mm.then_inc(S("gram"), 1)
                    for g in range(2):
                        for hh in range(4):
                            h = 2 * hh + g
                            c, b = h // 2, 64 * (h % 2)
                            mm = nc.tensor.matmul(PS[:, 4 + g, hh * P:(hh + 1) * P], AR[b:b + 64, c, q, 0, :], BT[b:b + 64, c, GR], start=True, stop=True)
                        mm.then_inc(S("gramM"), 1)
                    for lv in range(1, 6):
                        for g in range(2):
                            i = 2 * (lv - 1) + g
                            pe.wait_ge(S("level_mask"), i + 1)
                            pe.wait_ge(S("inv"), i + 1)
                            pe.wait_ge(S("invT"), i + 1)
                            pe.wait_ge(S("masked"), 8)
                            for hh in range(4):
                                h = 2 * hh + g
                                mm = nc.tensor.matmul(PS[:, g, hh * P:(hh + 1) * P], MK[:, h, :], DD[:, h, :], start=True, stop=True)
                            mm.then_inc(S("md"), 1)
                        for g in range(2):
                            i = 2 * (lv - 1) + g
                            pe.wait_ge(S("x_out"), i + 1)
                            for hh in range(4):
                                h = 2 * hh + g
                                mm = nc.tensor.matmul(PS[:, 2 + g, hh * P:(hh + 1) * P], XX[:, h, :], DT[:, h, :], start=True, stop=True)
                            mm.then_inc(S("dxT"), 1)
                            if lv < 5:
                                for hh in range(4):
                                    h = 2 * hh + g
                                    mm = nc.tensor.matmul(PS[:, 4 + g, hh * P:(hh + 1) * P], DT[:, h, :], XX[:, h, :], start=True, stop=True)
                                mm.then_inc(S("dx"), 1)
                    for j in range(2):
                        b = 64 * j
                        tt = slice(b, b + 64)
                        R = slice(b, b + 64)
                        pe.wait_ge(S("invT"), 12)
                        if j:
                            pe.wait_ge(S("state"), 1)
                        for c in range(4):
                            pv = slice(c * P, (c + 1) * P)
                            nc.tensor.matmul(PS[R, 6, pv], AR[:, c, q, 0, tt], ST[:, c, :], start=True, stop=False)
                            for h in (2 * c, 2 * c + 1):
                                hv = slice(h * 64, (h + 1) * 64)
                                mm = nc.tensor.matmul(PS[R, 6, hv], GK[:, h, 0, tt], TV[:, q, hv], start=False, stop=(h % 2 == 1))
                        mm.then_inc(S("z"), 1)
                        pe.wait_ge(S("z_out"), j + 1)
                        for h in range(8):
                            hv = slice(h * 64, (h + 1) * 64)
                            mm = nc.tensor.matmul(PS[R, 7, hv], DT[:, h, tt], ZS[:, hv], start=True, stop=True)
                        mm.then_inc(S("u"), 1)
                        pe.wait_ge(S("u_out"), j + 1)
                        if j:
                            pe.wait_ge(S("y_out"), 1)
                        for c in range(4):
                            pv = slice(c * P, (c + 1) * P)
                            nc.tensor.matmul(PS[:, 0, pv], TB[R, q, pv], US[R, pv], start=True, stop=False)
                            mm = nc.tensor.matmul(PS[:, 0, pv], TK[R, q, pv], TV[R, q, pv], start=False, stop=True)
                        mm.then_inc(S("s_new"), 1)
                        for c in range(4):
                            nc.tensor.matmul(PS[:, 1, c * 64:(c + 1) * 64], ST[:, c, :], AR[:, c, q, 1, tt], start=True, stop=False)
                            for h in (2 * c, 2 * c + 1):
                                hb = 64 * (h % 2)
                                hv = slice(h * 64, (h + 1) * 64)
                                o = PS[hb:hb + 64, 1, c * 64:(c + 1) * 64]
                                nc.tensor.matmul(o, US[:, hv], GB[:, h, 1, tt], start=False, stop=False)
                                mm = nc.tensor.matmul(o, TV[:, q, hv], GK[:, h, 1, tt], start=False, stop=True)
                        mm.then_inc(S("y"), 1)

                @block.scalar
                def _(act):
                    for lv in range(1, 6):
                        for g in range(2):
                            i = 2 * (lv - 1) + g
                            act.wait_ge(S("md"), i + 1)
                            if lv > 1:
                                act.wait_ge(S("dxT"), i - 1)
                                act.wait_ge(S("dx"), i - 1)
                            nc.scalar.activation(XX[:, g::2, :], PS[:, g, :].rearrange("p (h t) -> p h t", h=4), ACT.Copy).then_inc(S("x_out"), 1)
                    for j in range(2):
                        R = slice(64 * j, 64 * j + 64)
                        act.wait_ge(S("y"), j + 1)
                        nc.scalar.activation(YY[:, :, q * P + 64 * j:q * P + 64 * j + 64],
                                             PS[:, 1, 0:256].rearrange("p (c t) -> p c t", c=4), ACT.Copy).then_inc(S("y_out"), 1)

                @block.vector
                def _(dve):
                    v = nc.vector
                    tri = C("tri", 256)[:, None, :].to_broadcast([P, 2, 256])

                    def level(k):
                        return C("lev", P, k * P)[:, None, :].to_broadcast([P, 4, P])

                    for g in range(2):
                        for which, dst in ((0, GB), (1, GK)):
                            for half in range(2):
                                i = 4 * g + 2 * which + half
                                h = 4 * g + half
                                dve.wait_ge(S("gram"), i + 1)
                                v.tensor_tensor(dst[:, h:h + 3:2, :, :].rearrange("p h x t -> p h (x t)"),
                                                PS[:, i % 4, :].rearrange("p (h x) -> p h x", h=2), tri, ALU.mult).then_inc(S("masked"), 1)
                    if q == 0:
                        v.memset(US, 0.0).then_inc(S("u_zero"), 1)
                        dve.wait_ge(S("u_zero"), 1)
                    idb = ident[:, None, :].to_broadcast([P, 4, P])
                    for g in range(2):
                        hs = slice(g, 8, 2)
                        dve.wait_ge(S("gramM"), g + 1)
                        dve.wait_ge(S("masked"), 5 + g)
                        v.tensor_tensor(DD[:, hs, :], PS[:, 4 + g, :].rearrange("p (h t) -> p h t", h=4), C("m0", P)[:, None, :].to_broadcast([P, 4, P]), ALU.mult).then_inc(S("d_low"), 1)
                        v.tensor_tensor(DT[:, hs, :], GB[:, hs, 0, :], level(0), ALU.mult).then_inc(S("dT_low"), 1)
                        v.tensor_tensor(MK[:, hs, :], GB[:, hs, 0, :], level(1), ALU.mult).then_inc(S("level_mask"), 1)
                        dve.wait_ge(S("dT_low"), g + 1)
                        v.tensor_tensor(DD[:, hs, :], DD[:, hs, :], idb, ALU.add).then_inc(S("inv"), 1)
                        v.tensor_tensor(DT[:, hs, :], DT[:, hs, :], idb, ALU.add).then_inc(S("invT"), 1)
                    for lv in range(1, 6):
                        if lv < 5:
                            for g in range(2):
                                i = 2 * (lv - 1) + g
                                hs = slice(g, 8, 2)
                                dve.wait_ge(S("md"), i + 1)
                                v.tensor_tensor(MK[:, hs, :], GB[:, hs, 0, :], level(lv + 1), ALU.mult).then_inc(S("level_mask"), 1)
                        for g in range(2):
                            i = 2 * (lv - 1) + g
                            hs = slice(g, 8, 2)
                            dve.wait_ge(S("dxT"), i + 1)
                            if lv < 5:
                                dve.wait_ge(S("dx"), i + 1)
                            v.tensor_tensor(DT[:, hs, :], DT[:, hs, :], PS[:, 2 + g, :].rearrange("p (h t) -> p h t", h=4), ALU.add).then_inc(S("invT"), 1)
                            if lv < 5:
                                v.tensor_tensor(DD[:, hs, :], DD[:, hs, :], PS[:, 4 + g, :].rearrange("p (h t) -> p h t", h=4), ALU.add).then_inc(S("inv"), 1)
                    for j in range(2):
                        R = slice(64 * j, 64 * j + 64)
                        dve.wait_ge(S("z"), j + 1)
                        if j:
                            dve.wait_ge(S("state"), 1)
                        v.tensor_copy(ZS[R, :], PS[R, 6, :]).then_inc(S("z_out"), 1)
                        dve.wait_ge(S("u"), j + 1)
                        v.tensor_copy(US[R, :], PS[R, 7, :]).then_inc(S("u_out"), 1)
                        v.tensor_tensor(PCM, C("head_ones", P)[:, None, :].to_broadcast([P, 4, P]),
                                        PC[:, :, 2 * q + j:2 * q + j + 1].to_broadcast([P, 4, P]), ALU.mult).then_inc(S("decay_mask"), 1)
                        dve.wait_ge(S("s_new"), j + 1)
                        v.tensor_tensor(SN, PS[:, 0, :].rearrange("p (c v) -> p c v", c=4), ST, ALU.add).then_inc(S("s_sum"), 1)
                        dve.wait_ge(S("s_sum"), j + 1)
                        dve.wait_ge(S("y"), j + 1)
                        dve.wait_ge(S("decay_mask"), j + 1)
                        v.tensor_tensor(ST, SN, PCM, ALU.mult).then_inc(S("state"), 1)

        if debug == "scan":
            dump(nc, A, YY, stage, loaded)
            return

        Y0, SQ, RV = XT(30, 4), XT(34, 4), XT(38, 4)
        S, other = stage()
        with nc.Block() as block:
            @block.sync
            def _(sp):
                clear(sp, other)

            @block.tensor
            def _(pe):
                for c in range(4):
                    nc.tensor.matmul(PS[:, c, :], C("head_ones", P), YY[:, c, :], start=True, stop=True).then_inc(S("sum"), 1)
                for c in range(4):
                    pe.wait_ge(S("sq"), c + 1)
                    nc.tensor.matmul(PS[:, 4 + c, :], C("head_ones", P), SQ[:, c, :], start=True, stop=True).then_inc(S("sumsq"), 1)

            @block.scalar
            def _(act):
                for c in range(4):
                    act.wait_ge(S("centred"), c + 1)
                    nc.scalar.activation(SQ[:, c, :], Y0[:, c, :], ACT.Square).then_inc(S("sq"), 1)
                for c in range(4):
                    act.wait_ge(S("sumsq"), c + 1)
                    nc.scalar.activation(SQ[:, c, :], PS[:, 4 + c, :], ACT.Sqrt, scale=1.0 / HD, bias=C("eps", 1, 0)).then_inc(S("std"), 1)
                for c in range(4):
                    act.wait_ge(S("normed"), c + 1)
                    nc.scalar.activation(YY[:, c, :], Y0[:, c, :], ACT.Identity, scale=par_col("lnx_g", c), bias=par_col("lnx_b", c)).then_inc(S("affine"), 1)

            @block.vector
            def _(dve):
                v = nc.vector
                for c in range(4):
                    dve.wait_ge(S("sum"), c + 1)
                    v.scalar_tensor_tensor(out=Y0[:, c, :], in0=PS[:, c, :], scalar=-1.0 / HD, in1=YY[:, c, :], op0=ALU.mult, op1=ALU.add).then_inc(S("centred"), 1)
                for c in range(4):
                    dve.wait_ge(S("std"), c + 1)
                    v.reciprocal(RV[:, c, :], SQ[:, c, :]).then_inc(S("rstd"), 1)
                for c in range(4):
                    dve.wait_ge(S("rstd"), c + 1)
                    v.tensor_tensor(Y0[:, c, :], Y0[:, c, :], RV[:, c, :], ALU.mult).then_inc(S("normed"), 1)
                for c in range(4):
                    dve.wait_ge(S("affine"), c + 1)
                    v.tensor_tensor(BR[:, c, :], YY[:, c, :], BON[:, c, :], ALU.add).then_inc(S("branch"), 1)

        if debug == "rwkv":
            dump(nc, A, BR[:, 0:4, :], stage, loaded)
            return

        n0 = FIRST["mla"]
        QL, QN = XT(0, 5), XT(5, 5)
        SQ, KP, RST = XT(10, 5), XT(15), XT(16, 2)
        KPR, ROT = XT(18), XT(19, 2)
        QH, KH, VV = XT(24, 8), XT(32, 8), XT(40, 4)
        pe_rows = slice(64, 96)
        S, other = stage()
        with nc.Block() as block:
            @block.sync
            def _(sp):
                clear(sp, other)
                stream.send(sp, n0 + 11 + RING - 1)

            @block.tensor
            def _(pe):
                for t in range(5):
                    gemm(pe, t, n0 + t, xT[:, :, :], S("latent"))
                gemm(pe, 5, n0 + 5, xT[:, :, :], S("latent"), m=32, base=64)
                pe.wait_ge(S("kpe"), 1)
                nc.tensor.matmul(PS[64:96, 6, :], cst[64:96, CCOL["swap"]:CCOL["swap"] + 32], KP[pe_rows, :], start=True, stop=True).then_inc(S("swapped"), 1)
                for t in range(5):
                    pe.wait_ge(S("sq"), t + 1)
                    pe.wait_ge(S("evicted"), t + 1)
                    bank = 0 if t < 3 else 1
                    mm = nc.tensor.matmul(PS[:, bank, :], C("ones", P), SQ[:, t, :], start=t in (0, 3), stop=t in (2, 4))
                    if t in (2, 4):
                        mm.then_inc(S("sumsq"), 1)
                pe.wait_ge(S("normed"), 5)
                for h in range(8):
                    n = n0 + 6 + h // 3
                    if h % 3 == 0:
                        stream.wait(pe, n)
                    if h >= 2:
                        pe.wait_ge(S("q_out"), h - 1)
                    for k in range(3):
                        mm = nc.tensor.matmul(PS[0:96, 2 + h % 2, :], stream.chunk(n)[:, (h % 3) * 288 + k * 96:(h % 3) * 288 + (k + 1) * 96],
                                              QN[:, k, :], start=(k == 0), stop=(k == 2))
                        if h % 3 == 0 and k == 0:
                            mm.then_inc(used, 1)
                    mm.then_inc(S("q"), 1)
                for h in range(8):
                    pe.wait_ge(S("q_out"), h + 1)
                    if h >= 2:
                        pe.wait_ge(S("q_rot"), h - 1)
                    nc.tensor.matmul(PS[pe_rows, 6 + h % 2, :], cst[64:96, CCOL["swap"]:CCOL["swap"] + 32], QH[pe_rows, h, :],
                                     start=True, stop=True).then_inc(S("q_swapped"), 1)
                n = n0 + 9
                stream.wait(pe, n)
                for h in range(8):
                    pe.wait_ge(S("k_out"), h - 1) if h >= 2 else None
                    for k in range(2):
                        mm = nc.tensor.matmul(PS[0:64, 4 + h % 2, :], stream.chunk(n)[:, h * 128 + k * 64:h * 128 + (k + 1) * 64],
                                              QN[:, 3 + k, :], start=(k == 0), stop=(k == 1))
                        if h == 0 and k == 0:
                            mm.then_inc(used, 1)
                    mm.then_inc(S("k"), 1)
                n = n0 + 10
                stream.wait(pe, n)
                pe.wait_ge(S("rms"), 2)
                for q in range(4):
                    if q >= 2:
                        pe.wait_ge(S("v_out"), q - 1)
                    for k in range(2):
                        mm = nc.tensor.matmul(PS[:, q % 2, :], QN[:, 3 + k, q * P:(q + 1) * P], stream.chunk(n)[:, k * 512:(k + 1) * 512],
                                              start=(k == 0), stop=(k == 1))
                        if q == 0 and k == 0:
                            mm.then_inc(used, 1)
                    mm.then_inc(S("v"), 1)

            @block.scalar
            def _(act):
                a = nc.scalar
                for t in range(5):
                    act.wait_ge(S("latent"), t + 1)
                    a.activation(QL[:, t, :], PS[:, t, :], ACT.Copy).then_inc(S("evicted"), 1)
                    a.activation(SQ[:, t, :], PS[:, t, :], ACT.Square).then_inc(S("sq"), 1)
                act.wait_ge(S("latent"), 6)
                a.activation(KP[pe_rows, :], PS[pe_rows, 5, :], ACT.Copy).then_inc(S("kpe"), 1)
                for i, width in enumerate((384, 256)):
                    act.wait_ge(S("sumsq"), i + 1)
                    a.activation(RST[:, i, :], PS[:, i, :], ACT.Ln, scale=1.0 / width, bias=C("eps", 1, 1)).then_inc(S("log"), 1)
                for i in range(2):
                    act.wait_ge(S("log"), i + 1)
                    a.activation(RST[:, i, :], RST[:, i, :], ACT.Exp, scale=-0.5).then_inc(S("rms"), 1)
                for h in range(8):
                    act.wait_ge(S("q"), h + 1)
                    a.activation(QH[0:96, h, :], PS[0:96, 2 + h % 2, :], ACT.Copy).then_inc(S("q_out"), 1)
                for h in range(8):
                    act.wait_ge(S("k"), h + 1)
                    a.activation(KH[0:64, h, :], PS[0:64, 4 + h % 2, :], ACT.Copy).then_inc(S("k_out"), 1)
                for q in range(4):
                    act.wait_ge(S("v"), q + 1)
                    a.activation(VV[:, q, :], PS[:, q % 2, :], ACT.Copy).then_inc(S("v_out"), 1)

            @block.vector
            def _(dve):
                v = nc.vector
                cos, sin = rope[pe_rows, 0, :], rope[pe_rows, 1, :]
                dve.wait_ge(S("kpe"), 1)
                v.tensor_tensor(KPR[pe_rows, :], KP[pe_rows, :], cos, ALU.mult).then_inc(S("kp_cos"), 1)
                dve.wait_ge(S("swapped"), 1)
                v.tensor_tensor(ROT[pe_rows, 0, :], PS[pe_rows, 6, :], sin, ALU.mult).then_inc(S("kp_sin"), 1)
                dve.wait_ge(S("kp_sin"), 1)
                v.tensor_tensor(KPR[pe_rows, :], KPR[pe_rows, :], ROT[pe_rows, 0, :], ALU.add).then_inc(S("kp_rot"), 1)
                for t in range(5):
                    dve.wait_ge(S("rms"), 1 if t < 3 else 2)
                    dve.wait_ge(S("evicted"), t + 1)
                    v.scalar_tensor_tensor(out=QN[:, t, :], in0=QL[:, t, :], scalar=par_col("q_norm", t), in1=RST[:, 0 if t < 3 else 1, :],
                                           op0=ALU.mult, op1=ALU.mult).then_inc(S("normed"), 1)
                dve.wait_ge(S("kp_rot"), 1)
                for h in range(8):
                    i = h % 2
                    dve.wait_ge(S("q_swapped"), h + 1)
                    if h >= 2:
                        dve.wait_ge(S("q_done"), h - 1)
                    v.tensor_tensor(ROT[pe_rows, i, :], PS[pe_rows, 6 + i, :], sin, ALU.mult).then_inc(S("q_rot"), 1)
                    v.tensor_tensor(QH[pe_rows, h, :], QH[pe_rows, h, :], cos, ALU.mult).then_inc(S("q_cos"), 1)
                    dve.wait_ge(S("q_cos"), h + 1)
                    v.tensor_tensor(QH[pe_rows, h, :], QH[pe_rows, h, :], ROT[pe_rows, i, :], ALU.add).then_inc(S("q_done"), 1)

            @block.gpsimd
            def _(pool):
                pool.wait_ge(S("kp_rot"), 1)
                for h in range(8):
                    nc.gpsimd.tensor_copy(KH[pe_rows, h, :], KPR[pe_rows, :]).then_inc(S("kp_copied"), 1)

        attention(nc, stage, PS, ident, C("causal", P), heads=8, dv=64, rows=96, blocks=4,
                  query=lambda h: QH[0:96, h, :], key=lambda h: KH[0:96, h, :],
                  value=lambda h, kb: VV[:, kb, h * 64:(h + 1) * 64], nkeys=[128, 256, 384, 512],
                  scale=96.0 ** -0.5, out=lambda h: BR[64 * (h % 2):64 * (h % 2) + 64, 4 + h // 2, :],
                  probs=[XT(0), XT(1), XT(2)], probsT=[XT(4, 4), XT(8, 4)], small=XT(14), part=lambda h: 64 * (h % 2))
        if debug == "mla":
            dump(nc, A, BR[:, 4:8, :], stage, loaded)
            return

        n0, nx, ng = FIRST["conv"], FIRST["xattn"], FIRST["gates"]
        H0 = X[:, 0:4 * (T + TAPS - 1)].rearrange("p (c t) -> p c t", c=4)
        SGM, ACC, Y0, SQ, RST = XT(5, 4), XT(9, 4), XT(13, 4), XT(17, 4), XT(21)
        QX, KX, VX = XT(22, 4), X[:, 26 * T:28 * T].rearrange("p (h t) -> p h t", h=4), XT(28, 2)
        GNOW, GLATER = XT(30, 4), XT(34, 8)
        S, other = stage()
        with nc.Block() as block:
            @block.sync
            def _(sp):
                clear(sp, other)
                stream.send(sp, ng + 16 + RING - 1)

            @block.tensor
            def _(pe):
                for t in range(8):
                    gemm(pe, t, n0 + t, xT[:, :, :], S("u"))
                for t in range(8):
                    if t < 4:
                        pe.wait_ge(S("gate"), t + 1)
                    else:
                        pe.wait_ge(S("evicted"), t - 3)
                    gemm(pe, 4 + t % 4, nx + t, xT[:, :, :] if t < 4 else memT[:, :, :], S("product"))
                pe.wait_ge(S("glu"), 4)
                for kc in range(4):
                    n = nx + 8 + kc
                    stream.wait(pe, n)
                    for q in range(2):
                        for k in range(2):
                            mm = nc.tensor.matmul(PS[:, 2 + q, :], memT[:, 2 * kc + k, q * P:(q + 1) * P], stream.chunk(n)[:, k * 512:(k + 1) * 512],
                                                  start=(kc == 0 and k == 0), stop=(kc == 3 and k == 1))
                            if q == 0 and k == 0:
                                mm.then_inc(used, 1)
                        if kc == 3:
                            mm.then_inc(S("product"), 1)
                for t in range(16):
                    if t < 4:
                        pe.wait_ge(S("evicted"), 5 + t)
                    else:
                        pe.wait_ge(S("silu"), t - 3)
                    gemm(pe, 4 + t % 4, ng + t, xT[:, :, :], S("gate_product"))
                for c in range(4):
                    pe.wait_ge(S("conv"), c + 1)
                    mm = nc.tensor.matmul(PS[:, 0, :], C("ones", P), ACC[:, c, :], start=(c == 0), stop=(c == 3))
                mm.then_inc(S("sum"), 1)
                for c in range(4):
                    pe.wait_ge(S("sq"), c + 1)
                    mm = nc.tensor.matmul(PS[:, 1, :], C("ones", P), SQ[:, c, :], start=(c == 0), stop=(c == 3))
                mm.then_inc(S("sumsq"), 1)

            @block.scalar
            def _(act):
                a = nc.scalar
                for c in range(4):
                    act.wait_ge(S("u"), 4 + c + 1)
                    a.activation(SGM[:, c, :], PS[:, 4 + c, :], ACT.Sigmoid).then_inc(S("gate"), 1)
                for t in range(10):
                    act.wait_ge(S("product"), t + 1)
                    dst, src = ((QX[:, t, :], PS[:, 4 + t % 4, :]) if t < 4 else (KX[:, t - 4, :], PS[:, 4 + t % 4, 0:MEM]) if t < 8
                                else (VX[:, t - 8, :], PS[:, 2 + t - 8, :]))
                    a.activation(dst, src, ACT.Copy).then_inc(S("evicted"), 1)
                for t in range(16):
                    act.wait_ge(S("gate_product"), t + 1)
                    if 4 <= t < 8:
                        act.wait_ge(S("gated"), t - 3)
                    a.activation(GNOW[:, t % 4, :] if t < 8 else GLATER[:, t - 8, :], PS[:, 4 + t % 4, :], ACT.Silu).then_inc(S("silu"), 1)
                for c in range(4):
                    act.wait_ge(S("centred"), c + 1)
                    a.activation(SQ[:, c, :], Y0[:, c, :], ACT.Square).then_inc(S("sq"), 1)
                act.wait_ge(S("sumsq"), 1)
                a.activation(RST, PS[:, 1, :], ACT.Ln, scale=1.0 / W, bias=C("eps", 1, 2)).then_inc(S("log"), 1)
                act.wait_ge(S("log"), 1)
                a.activation(RST, RST, ACT.Exp, scale=-0.5).then_inc(S("rstd"), 1)
                for c in range(4):
                    act.wait_ge(S("normed"), c + 1)
                    a.activation(BR[:, 8 + c, :], Y0[:, c, :], ACT.Silu, scale=par_col("cln_g", c), bias=par_col("cln_b", c)).then_inc(S("branch"), 1)

            @block.vector
            def _(dve):
                v = nc.vector
                v.memset(H0[:, :, 0:TAPS - 1], 0.0).then_inc(S("pad"), 1)
                for c in range(4):
                    dve.wait_ge(S("gate"), c + 1)
                    v.tensor_tensor(H0[:, c, TAPS - 1:], PS[:, c, :], SGM[:, c, :], ALU.mult).then_inc(S("glu"), 1)
                dve.wait_ge(S("pad"), 1)
                dve.wait_ge(S("glu"), 4)
                for tap in range(TAPS):
                    for c in range(4):
                        w = par_col("conv_w", c * TAPS + tap)
                        if tap == 0:
                            ins = v.tensor_scalar(ACC[:, c, :], H0[:, c, 0:T], w, par_col("conv_b", c), ALU.mult, ALU.add)
                        else:
                            dve.wait_ge(S("tap"), 4 * (tap - 1) + c + 1)
                            ins = v.scalar_tensor_tensor(out=ACC[:, c, :], in0=H0[:, c, tap:tap + T], scalar=w, in1=ACC[:, c, :],
                                                         op0=ALU.mult, op1=ALU.add)
                        ins.then_inc(S("conv") if tap == TAPS - 1 else S("tap"), 1)
                dve.wait_ge(S("sum"), 1)
                dve.wait_ge(S("conv"), 4)
                for c in range(4):
                    v.scalar_tensor_tensor(out=Y0[:, c, :], in0=PS[:, 0, :], scalar=-1.0 / W, in1=ACC[:, c, :], op0=ALU.mult, op1=ALU.add).then_inc(S("centred"), 1)
                dve.wait_ge(S("rstd"), 1)
                dve.wait_ge(S("centred"), 4)
                for c in range(4):
                    dve.wait_ge(S("sq"), c + 1)
                    v.tensor_tensor(Y0[:, c, :], Y0[:, c, :], RST, ALU.mult).then_inc(S("normed"), 1)

            @block.gpsimd
            def _(pool):
                for t in range(8):
                    pool.wait_ge(S("silu"), t + 1)
                    nc.gpsimd.tensor_tensor(BR[:, t, :], BR[:, t, :], GNOW[:, t % 4, :], ALU.mult).then_inc(S("gated"), 1)

        attention(nc, stage, PS, ident, None, heads=4, dv=128, rows=128, blocks=4,
                  query=lambda h: QX[:, h, :], key=lambda h: KX[:, h, :],
                  value=lambda h, kb: VX[:, kb, h * P:(h + 1) * P], nkeys=[256] * 4,
                  scale=128.0 ** -0.5, out=lambda h: BR[:, 12 + h, :],
                  probs=[XT(0), XT(1), XT(2)], probsT=[XT(4, 4), XT(8, 4)], small=XT(14), part=lambda h: 0)
        if debug == "xattn":
            dump(nc, A, BR[:, 12:16, :], stage, loaded)
            return

        n0 = FIRST["merge"]
        MG = XT(12, 8)
        AD = X[:, 4 * T:4 * T + 96].rearrange("p (m c) -> p m c", c=2)
        CB = X[:, 30 * T:34 * T].rearrange("p (c k) -> p c k", c=2)
        PROD = X[:, 28 * T:30 * T]

        def rows_of(t):
            return X[:, (20 + 2 * (t % 4)) * T:(22 + 2 * (t % 4)) * T]

        S, other = stage()
        with nc.Block() as block:
            @block.sync
            def _(sp):
                clear(sp, other)
                for c in range(2):
                    sp.dma_start(CB[:, c, :], A["cond"][c].partition_broadcast(P)).then_inc(S("cond"), 16)
                for t in range(48):
                    stream.send(sp, n0 + t + RING)
                    if t >= 4:
                        sp.wait_ge(S("ada"), 2 * (t - 3))
                    sp.dma_start(rows_of(t), A["ada"][bass.ds(layer, 1), t, :, :].rearrange("l p c -> p (l c)")).then_inc(S(f"rows{t % 4}"), 16)

            @block.tensor
            def _(pe):
                for m in range(8):
                    for n in range(4):
                        i = 4 * m + n
                        o = n0 + 6 * m + 3 * (n // 2)
                        if i >= 4:
                            pe.wait_ge(S("weighted"), i - 3)
                        if n % 2 == 0:
                            stream.wait(pe, o)
                        bank = 4 + i % 4
                        if n % 2 == 0:
                            for nn in (n, n + 1):
                                if 4 * m + nn >= 4:
                                    pe.wait_ge(S("weighted"), 4 * m + nn - 3)
                                if m == 0 and nn >= 2:
                                    pe.wait_ge(S("gated"), 4 * (nn - 1))
                                for k in range(4):
                                    mm = nc.tensor.matmul(PS[:, 4 + (4 * m + nn) % 4, :], stream.chunk(o)[:, (nn % 2) * 512 + k * P:(nn % 2) * 512 + (k + 1) * P],
                                                          BR[:, 4 * nn + k, :], start=(k == 0), stop=(k == 3))
                                    if nn == n and k == 0:
                                        mm.then_inc(used, 1)
                                mm.then_inc(S("product"), 1)
                        if i >= 4:
                            pe.wait_ge(S("gate"), i - 3)
                        gemm(pe, i % 4, o + 1 + n % 2, xT[:, :, :], S("gate_product"))

            @block.scalar
            def _(act):
                act.wait_ge(S("cond"), 32)
                nc.scalar.activation(CB, CB, ACT.Silu).then_inc(S("silu_c"), 1)
                for i in range(32):
                    act.wait_ge(S("gate_product"), i + 1)
                    if i >= 4:
                        act.wait_ge(S("weighted"), i - 3)
                    nc.scalar.activation(XT(i % 4), PS[:, i % 4, :], ACT.Sigmoid, bias=par_col("b_gate", 8 * (i % 4) + i // 4)).then_inc(S("gate"), 1)

            @block.vector
            def _(dve):
                v = nc.vector
                for i in range(32):
                    m, n = i // 4, i % 4
                    dve.wait_ge(S("gate"), i + 1)
                    dve.wait_ge(S("product"), i + 1)
                    dst = MG[:, m, :] if n == 0 else XT(8 + i % 4)
                    if i >= 4 and n:
                        dve.wait_ge(S("merged"), 3 * m - 3 + n)
                    v.tensor_tensor(dst, PS[:, 4 + i % 4, :], XT(i % 4), ALU.mult).then_inc(S("weighted"), 1)
                    if n:
                        dve.wait_ge(S("weighted"), i + 1)
                        if n > 1:
                            dve.wait_ge(S("merged"), 3 * m + n - 1)
                        v.tensor_tensor(MG[:, m, :], MG[:, m, :], XT(8 + i % 4), ALU.add).then_inc(S("merged"), 1)
                    if i == 0:
                        dve.wait_ge(S("silu_c"), 1)
                    for t in range(48 * i // 32, 48 * (i + 1) // 32):
                        dve.wait_ge(S(f"rows{t % 4}"), 16 * (t // 4 + 1))
                        for c in range(2):
                            if 2 * t + c:
                                dve.wait_ge(S("ada"), 2 * t + c)
                            v.tensor_tensor_reduce(PROD, rows_of(t), CB[:, c, :], 1.0, 0.0, ALU.mult, ALU.add, AD[:, t, c:c + 1]).then_inc(S("ada"), 1)
                dve.wait_ge(S("ada"), 96)
                v.tensor_copy(mods[:, bass.ds(layer, 1), :].rearrange("p l m -> p (l m)"), X[:, 4 * T:4 * T + 96]).then_inc(S("mods"), 1)

            @block.gpsimd
            def _(pool):
                for t in range(8):
                    nc.gpsimd.tensor_tensor(BR[:, 8 + t, :], BR[:, 8 + t, :], GLATER[:, t, :], ALU.mult).then_inc(S("gated"), 1)

        n0 = FIRST["out"]
        RR, SQ, RST = XT(0, 8), XT(8, 8), XT(16)
        S, other = stage()
        with nc.Block() as block:
            @block.sync
            def _(sp):
                clear(sp, other)
                stream.send(sp, n0 + 8)

            @block.tensor
            def _(pe):
                for t in range(8):
                    if t >= 4:
                        pe.wait_ge(S("residual"), t - 3)
                    gemm(pe, t % 4, n0 + t, MG, S("product"))
                for t in range(8):
                    pe.wait_ge(S("residual"), t + 1)
                    mm = nc.tensor.matmul(PS[:, 4, :], C("ones", P), RR[:, t, :], start=(t == 0), stop=(t == 7))
                mm.then_inc(S("sum"), 1)
                for t in range(8):
                    pe.wait_ge(S("sq"), t + 1)
                    mm = nc.tensor.matmul(PS[:, 5, :], C("ones", P), SQ[:, t, :], start=(t == 0), stop=(t == 7))
                mm.then_inc(S("sumsq"), 1)

            @block.scalar
            def _(act):
                a = nc.scalar
                for t in range(8):
                    act.wait_ge(S("centred"), t + 1)
                    a.activation(SQ[:, t, :], RR[:, t, :], ACT.Square).then_inc(S("sq"), 1)
                act.wait_ge(S("sumsq"), 1)
                a.activation(RST, PS[:, 5, :], ACT.Ln, scale=1.0 / D, bias=C("eps", 1, 2)).then_inc(S("log"), 1)
                act.wait_ge(S("log"), 1)
                a.activation(RST, RST, ACT.Exp, scale=-0.5).then_inc(S("rstd"), 1)
                for t in range(8):
                    act.wait_ge(S("normed"), t + 1)
                    a.activation(xT[:, t, :], RR[:, t, :], ACT.Identity, scale=par_col("ln_g", t), bias=par_col("ln_b", t)).then_inc(S("x_new"), 1)

            @block.vector
            def _(dve):
                v = nc.vector
                for t in range(8):
                    dve.wait_ge(S("product"), t + 1)
                    v.scalar_tensor_tensor(out=RR[:, t, :], in0=xT[:, t, :], scalar=DEEP_ALPHA, in1=PS[:, t % 4, :], op0=ALU.mult, op1=ALU.add).then_inc(S("residual"), 1)
                dve.wait_ge(S("sum"), 1)
                for t in range(8):
                    v.scalar_tensor_tensor(out=RR[:, t, :], in0=PS[:, 4, :], scalar=-1.0 / D, in1=RR[:, t, :], op0=ALU.mult, op1=ALU.add).then_inc(S("centred"), 1)
                dve.wait_ge(S("rstd"), 1)
                for t in range(8):
                    dve.wait_ge(S("sq"), t + 1)
                    v.tensor_tensor(RR[:, t, :], RR[:, t, :], RST, ALU.mult).then_inc(S("normed"), 1)

        S, other = stage()
        with nc.Block() as block:
            @block.sync
            def _(sp):
                clear(sp, other)
                clear(sp, arrived)
                sp.sem_clear(used)


CKV = CTX + T
FF = 2816
FT = FF // P
XB = T + 16
PCOL2 = {}
_at = 0
for _name, _n in (("g_mix", 8), ("g_ffn", 8), ("b_ada", 48), ("q_gain", 1), ("k_gain", 1), ("pool_scale", 2),
                  ("w_pool", 256), ("w_four", 256)):
    PCOL2[_name] = _at
    _at += _n
NPAR2 = _at
CCOL2 = {}
_at = 0
for _name, _n in (("ident", 128), ("head_ones", 128), ("ones", 128), ("swap", 128), ("cos", T), ("sin", T), ("cs64", 256),
                  ("count_x", 2 * T), ("count_c", 2 * CTX), ("eps", 1)):
    CCOL2[_name] = _at
    _at += _n
NCST2 = _at
STAGE_CHUNKS2 = (("in", 11), ("out", 8), ("up", 2 * FT), ("down", 24))
FIRST2 = {}
_at = 0
for _name, _n in STAGE_CHUNKS2:
    FIRST2[_name] = _at
    _at += _n
NCHUNK2 = _at


def second(nc, ctx, A, PS, xT, ring, mods, stage, arrived, used, loaded, stored, debug):
    def sb(name, shape, dt=F32):
        return ctx.enter_context(nc.sbuf_tensor(name, shape, dt))

    cst = sb("cst2", [P, NCST2])
    par = sb("par2", [P, NPAR2])
    cT = sb("cT", [P, DK, CTX])
    mod = sb("mod", [P, 48, 2])
    gain = sb("gain", [P, 2, 8, 2])
    X = sb("X2", [P, 66 * T])

    def C(name, n=1, k=0):
        a = CCOL2[name] + k
        return cst[:, a:a + n]

    def par_col(name, k=0, n=1):
        a = PCOL2[name] + k
        return par[:, a:a + n]

    def XT(i, n=1, w=T):
        a = X[:, i * T:i * T + n * w]
        return a if n == 1 else a.rearrange("p (n t) -> p n t", n=n)

    ident = C("ident", P)
    eps = C("eps")
    SH1, SC1, GA1, SH2, SC2, GA2 = (8 * i for i in range(6))

    S, other = stage()
    with nc.Block() as block:
        @block.sync
        def _(sp):
            clear(sp, other)
            sp.dma_start(cst[:, :], A["cst2"]).then_inc(S("in"), 16)
            sp.dma_start(cT[:, :, :].rearrange("p k t -> p (k t)"), A["ctxT"]).then_inc(S("in"), 16)
            sp.wait_ge(S("in"), 32)

    for layer in range(LAYERS):
        update = layer < LAYERS - 1
        stream = Stream(ring, arrived, used, lambda n: A["w2"][layer, n, :, :])
        HX, HC = XT(0, 8), XT(8, 8, CTX)
        streams = [dict(name="x", n=T, src=xT, h=HX, k=0, bank=0), dict(name="c", n=CTX, src=cT, h=HC, k=1, bank=4)]

        def first_use(mm, n):
            if n:
                mm.then_inc(used, 1)

        def gemm(pe, n, outs):
            stream.wait(pe, n)
            for i, (ps, rhs, done) in enumerate(outs):
                for k in range(DK):
                    mm = nc.tensor.matmul(ps, tile_of(stream.chunk(n), k), rhs[:, k, :], start=(k == 0), stop=(k == DK - 1))
                    if i == 0 and k == 0:
                        first_use(mm, n)
                mm.then_inc(done, 1)

        S, other = stage()
        with nc.Block() as block:
            @block.sync
            def _(sp):
                clear(sp, other)
                sp.dma_start(par[:, :], A["par2"][layer]).then_inc(S("par"), 16)
                stream.send(sp, RING)
                sp.wait_ge(S("par"), 16)

            @block.vector
            def _(dve):
                v = nc.vector
                dve.wait_ge(S("par"), 16)
                v.tensor_tensor(mod[:, :, :], mods[:, layer, :].rearrange("p (m c) -> p m c", m=48),
                                par_col("b_ada", 0, 48)[:, :, None].to_broadcast([P, 48, 2]), ALU.add).then_inc(S("mod"), 1)
                dve.wait_ge(S("mod"), 1)
                for i, (sc, g) in enumerate(((SC1, "g_mix"), (SC2, "g_ffn"))):
                    v.tensor_scalar(gain[:, i, :, :], mod[:, sc:sc + 8, :], 1.0, None, ALU.add).then_inc(S("one_plus"), 1)
                dve.wait_ge(S("one_plus"), 2)
                for i, (sc, g) in enumerate(((SC1, "g_mix"), (SC2, "g_ffn"))):
                    v.tensor_tensor(gain[:, i, :, :], gain[:, i, :, :], par_col(g, 0, 8)[:, :, None].to_broadcast([P, 8, 2]), ALU.mult).then_inc(S("gain"), 1)

        def norm_mod(which, shift, sts):
            S, other = stage()
            SQ, RST = {"x": XT(45, 8), "c": XT(53, 8, CTX)}, {"x": XT(57), "c": XT(58)[:, 0:CTX]}
            with nc.Block() as block:
                @block.sync
                def _(sp):
                    clear(sp, other)

                @block.tensor
                def _(pe):
                    for s in sts:
                        nm, n = s["name"], s["n"]
                        for t in range(DK):
                            pe.wait_ge(S("sq" + nm), t + 1)
                            mm = nc.tensor.matmul(PS[:, s["bank"], 0:n], C("ones", P), SQ[nm][:, t, :], start=(t == 0), stop=(t == DK - 1))
                        mm.then_inc(S("sumsq" + nm), 1)

                @block.scalar
                def _(act):
                    a = nc.scalar
                    for s in sts:
                        nm = s["name"]
                        for t in range(DK):
                            a.activation(SQ[nm][:, t, :], s["src"][:, t, :], ACT.Square).then_inc(S("sq" + nm), 1)
                    for s in sts:
                        nm, n = s["name"], s["n"]
                        act.wait_ge(S("sumsq" + nm), 1)
                        a.activation(RST[nm], PS[:, s["bank"], 0:n], ACT.Ln, scale=1.0 / D, bias=eps).then_inc(S("log" + nm), 1)
                        act.wait_ge(S("log" + nm), 1)
                        a.activation(RST[nm], RST[nm], ACT.Exp, scale=-0.5).then_inc(S("rstd" + nm), 1)
                    for s in sts:
                        nm = s["name"]
                        for t in range(DK):
                            act.wait_ge(S("normed" + nm), t + 1)
                            a.activation(s["h"][:, t, :], SQ[nm][:, t, :], ACT.Identity, bias=mod[:, shift + t, s["k"]:s["k"] + 1]).then_inc(S("h" + nm), 1)

                @block.vector
                def _(dve):
                    for s in sts:
                        nm = s["name"]
                        dve.wait_ge(S("rstd" + nm), 1)
                        for t in range(DK):
                            nc.vector.scalar_tensor_tensor(out=SQ[nm][:, t, :], in0=s["src"][:, t, :], scalar=gain[:, which, t, s["k"]:s["k"] + 1],
                                                           in1=RST[nm], op0=ALU.mult, op1=ALU.mult).then_inc(S("normed" + nm), 1)

        norm_mod(0, SH1, streams)

        n0 = FIRST2["in"]
        QR, KR, FO, VV = XT(12, 4), XT(16, 2), XT(21, 2), XT(23, 6, P)
        PL = X[:, 18 * T:18 * T + 2 * XB].rearrange("p (c t) -> p c t", c=2)
        QRc, KRc, FOc = XT(25, 4, CTX), XT(27, 2, CTX), XT(30, 2, CTX)
        PLc = X[:, 28 * T:28 * T + 2 * (CTX + 16)].rearrange("p (c t) -> p c t", c=2)
        tiles = [("q", i) for i in range(4)] + [("k", i) for i in range(2)] + [("v", 0)] + [("p", i) for i in range(2)] + [("f", i) for i in range(2)]
        plan = {"x": tiles, "c": tiles if update else [t for t in tiles if t[0] in "kv"]}
        where = {"x": {"q": QR, "k": KR, "f": FO, "p": PL[:, :, 8:8 + T], "v": VV[:, 2:6, :]},
                 "c": {"q": QRc, "k": KRc, "f": FOc, "p": PLc[:, :, 8:8 + CTX], "v": VV[:, 0:2, :]}}
        S, other = stage()
        with nc.Block() as block:
            @block.sync
            def _(sp):
                clear(sp, other)
                stream.send(sp, n0 + 11 + RING - 1)

            @block.tensor
            def _(pe):
                for j, t in enumerate(tiles):
                    stream.wait(pe, n0 + j)
                    started = False
                    for s in streams:
                        if t not in plan[s["name"]]:
                            continue
                        i = plan[s["name"]].index(t)
                        if i >= 4:
                            pe.wait_ge(S("evicted" + s["name"]), i - 3)
                        bank = s["bank"] + i % 4
                        if t[0] != "v":
                            for k in range(DK):
                                mm = nc.tensor.matmul(PS[:, bank, 0:s["n"]], tile_of(stream.chunk(n0 + j), k), s["h"][:, k, :], start=(k == 0), stop=(k == DK - 1))
                                if not started:
                                    first_use(mm, n0 + j)
                                    started = True
                        else:
                            for q in range(s["n"] // P):
                                for k in range(DK):
                                    mm = nc.tensor.matmul(PS[:, bank, q * P:(q + 1) * P], s["h"][:, k, q * P:(q + 1) * P], tile_of(stream.chunk(n0 + j), k), start=(k == 0), stop=(k == DK - 1))
                                    if not started:
                                        first_use(mm, n0 + j)
                                        started = True
                        mm.then_inc(S("product" + s["name"]), 1)

            @block.scalar
            def _(act):
                for t in tiles:
                    for s in streams:
                        if t not in plan[s["name"]]:
                            continue
                        i = plan[s["name"]].index(t)
                        act.wait_ge(S("product" + s["name"]), i + 1)
                        dst = where[s["name"]][t[0]]
                        src = PS[:, s["bank"] + i % 4, 0:s["n"]]
                        if t[0] == "v":
                            src = src.rearrange("p (q c) -> p q c", c=P)
                        else:
                            dst = dst[:, t[1], :]
                        nc.scalar.activation(dst, src, ACT.Copy).then_inc(S("evicted" + s["name"]), 1)

        KA = XT(31, 2, CKV)
        QN, QNc = XT(34, 4), XT(38, 4, CTX)
        MX, MXc = XT(40, 8), XT(48, 8, CTX)
        items = [(QR[:, i, :], T, "q_gain", QN[:, i, :], True) for i in range(4)]
        items += [(KR[:, i, :], T, "k_gain", KA[:, i, CTX:CKV], True) for i in range(2)]
        items += [(KRc[:, i, :], CTX, "k_gain", KA[:, i, 0:CTX], False) for i in range(2)]
        if update:
            items += [(QRc[:, i, :], CTX, "q_gain", QNc[:, i, :], False) for i in range(4)]
        S, other = stage()
        with nc.Block() as block:
            @block.sync
            def _(sp):
                clear(sp, other)

            @block.tensor
            def _(pe):
                for i, (raw, n, g, dst, turn) in enumerate(items):
                    pe.wait_ge(S("sq"), i + 1)
                    if i >= 4:
                        pe.wait_ge(S("log"), i - 3)
                    nc.tensor.matmul(PS[:, i % 4, 0:n], C("head_ones", P), XT(0 + i % 4)[:, 0:n], start=True, stop=True).then_inc(S("sumsq"), 1)
                for i in range(6):
                    pe.wait_ge(S("normed"), i + 1)
                    if i >= 4:
                        pe.wait_ge(S("sin"), i - 3)
                    nc.tensor.matmul(PS[:, 4 + i % 4, :], C("swap", P), XT(52 + i), start=True, stop=True).then_inc(S("swapped"), 1)

            def logs(act, i):
                n = items[i][1]
                act.wait_ge(S("sumsq"), i + 1)
                if i >= 4:
                    act.wait_ge(S("normed"), i - 3)
                nc.scalar.activation(XT(4 + i % 4)[:, 0:n], PS[:, i % 4, 0:n], ACT.Ln, scale=1.0 / HD, bias=eps).then_inc(S("log"), 1)
                act.wait_ge(S("log"), i + 1)
                nc.scalar.activation(XT(4 + i % 4)[:, 0:n], XT(4 + i % 4)[:, 0:n], ACT.Exp, scale=-0.5).then_inc(S("rstd"), 1)

            @block.scalar
            def _(act):
                a = nc.scalar
                for i, (raw, n, g, dst, turn) in enumerate(items):
                    if i >= 4:
                        act.wait_ge(S("sumsq"), i - 3)
                    a.activation(XT(i % 4)[:, 0:n], raw, ACT.Square).then_inc(S("sq"), 1)
                    if i >= 3:
                        logs(act, i - 3)
                for i in range(len(items) - 3, len(items)):
                    logs(act, i)

            @block.vector
            def _(dve):
                v = nc.vector

                def rotate(i):
                    dst = items[i][3]
                    dve.wait_ge(S("normed"), i + 1)
                    if i >= 2:
                        dve.wait_ge(S("rotated"), i - 1)
                    v.tensor_tensor(XT(58 + i % 2), XT(52 + i), C("cos", T), ALU.mult).then_inc(S("cos"), 1)
                    dve.wait_ge(S("swapped"), i + 1)
                    v.tensor_tensor(XT(60 + i % 2), PS[:, 4 + i % 4, :], C("sin", T), ALU.mult).then_inc(S("sin"), 1)
                    dve.wait_ge(S("cos"), i + 1)
                    dve.wait_ge(S("sin"), i + 1)
                    v.tensor_tensor(dst, XT(58 + i % 2), XT(60 + i % 2), ALU.add).then_inc(S("rotated"), 1)

                for i, (raw, n, g, dst, turn) in enumerate(items):
                    dve.wait_ge(S("rstd"), i + 1)
                    v.scalar_tensor_tensor(out=XT(52 + i) if turn else dst, in0=raw, scalar=par_col(g), in1=XT(4 + i % 4)[:, 0:n],
                                           op0=ALU.mult, op1=ALU.mult).then_inc(S("normed"), 1)
                for i in range(6):
                    rotate(i)

        full = streams if update else streams[:1]
        U = {"x": dict(p=PL, f=FO, mx=MX, dft=X[:, 0:8 * T].rearrange("p (q c t) -> p q c t", q=4, c=2), g=X[:, 52 * T:56 * T], f2=XT(56, 2), d=XT(62, 2), cnt=C("count_x", 2 * T).rearrange("p (c t) -> p c t", c=2), w=T + 16, at=10 * T),
             "c": dict(p=PLc, f=FOc, mx=MXc, dft=X[:, 8 * T:10 * T].rearrange("p (q c t) -> p q c t", q=2, c=2), g=X[:, 58 * T:60 * T], f2=XT(60, 2, CTX), d=XT(61, 2, CTX), cnt=C("count_c", 2 * CTX).rearrange("p (c t) -> p c t", c=2), w=CTX + 16, at=10 * T)}
        S, other = stage()
        with nc.Block() as block:
            @block.sync
            def _(sp):
                clear(sp, other)
                sp.dma_start(X[:, 0:8 * T], A["dft_x"]).then_inc(S("dft"), 16)
                sp.dma_start(X[:, 8 * T:10 * T], A["dft_c"]).then_inc(S("dft"), 16)
                sp.wait_ge(S("dft"), 32)

            @block.gpsimd
            def _(pool):
                g = nc.gpsimd
                done = [0]

                def link(ins):
                    done[0] += 1
                    ins.then_inc(S("pool_step"), 1)
                    pool.wait_ge(S("pool_step"), done[0])

                for s in full:
                    u, n = U[s["name"]], s["n"]
                    w = n + 16
                    s2, s4, s8 = (X[:, (12 + 2 * i) * T:(12 + 2 * i) * T + w] for i in range(3))
                    link(g.memset(u["p"][:, :, 0:8], 0.0))
                    link(g.memset(u["p"][:, :, 8 + n:16 + n], 0.0))
                    for c in range(2):
                        src = u["p"][:, c, :]
                        rows = slice(0, P)
                        link(g.tensor_tensor(s2[:, 1:w], src[:, 0:w - 1], src[:, 1:w], ALU.add))
                        link(g.tensor_tensor(s4[:, 2:w - 2], s2[:, 1:w - 3], s2[:, 3:w - 1], ALU.add))
                        lo, hi = s2[0:64, 8:8 + n], s4[64:128, 8:8 + n]
                        if c:
                            link(g.tensor_tensor(s8[:, 4:w - 4], s4[:, 2:w - 6], s4[:, 6:w - 2], ALU.add))
                            link(g.tensor_tensor(s2[64:128, 8:8 + n], s8[64:128, 4:4 + n], s8[64:128, 12:12 + n], ALU.add))
                            lo, hi = s8[0:64, 8:8 + n], s2[64:128, 8:8 + n]
                        link(g.tensor_tensor(u["d"][0:64, c, :], lo, u["cnt"][0:64, c, :], ALU.mult))
                        link(g.tensor_tensor(u["d"][64:128, c, :], hi, u["cnt"][64:128, c, :], ALU.mult))
                        g.tensor_tensor(u["d"][:, c, :], u["d"][:, c, :], src[:, 8:8 + n], ALU.subtract).then_inc(S("d" + s["name"]), 1)

            @block.tensor
            def _(pe):
                for s in full:
                    nm, n, b = s["name"], s["n"], s["bank"]
                    u, nq = U[nm], s["n"] // P
                    for q in range(nq):
                        if q >= 2:
                            pe.wait_ge(S("g" + nm), q - 1)
                        for c in range(2):
                            mm = nc.tensor.matmul(PS[:, b + q % 2, c * 256:(c + 1) * 256], u["f"][:, c, q * P:(q + 1) * P], C("cs64", 256), start=True, stop=True)
                        mm.then_inc(S("gp" + nm), 1)
                    pe.wait_ge(S("dft"), 32)
                    pe.wait_ge(S("g" + nm), nq)
                    gg = u["g"].rearrange("p (q c x j) -> p q c x j", q=nq, c=2, x=2)
                    for c in range(2):
                        for q in range(nq):
                            for x in range(2):
                                mm = nc.tensor.matmul(PS[:, b + c, 0:n], gg[:, q, c, x, :], u["dft"][:, q, x, :], start=(q == 0 and x == 0), stop=(q == nq - 1 and x == 1))
                        mm.then_inc(S("f" + nm), 1)
                    for c in range(2):
                        pe.wait_ge(S("f_out" + nm), c + 1)
                        nc.tensor.matmul(PS[:, b + 2 + c, 0:n], par_col("w_four", c * P, P), u["f2"][:, c, :], start=True, stop=True).then_inc(S("y" + nm), 1)
                for s in full:
                    nm, n, b = s["name"], s["n"], s["bank"]
                    for c in range(2):
                        pe.wait_ge(S("d" + nm), c + 1)
                        pe.wait_ge(S("y_out" + nm), c + 1)
                        nc.tensor.matmul(PS[:, b + 2 + c, 0:n], par_col("w_pool", c * P, P), U[nm]["d"][:, c, :], start=True, stop=True).then_inc(S("pooled" + nm), 1)

            @block.scalar
            def _(act):
                a = nc.scalar
                for s in full:
                    nm, n, b = s["name"], s["n"], s["bank"]
                    u, nq = U[nm], s["n"] // P
                    for q in range(nq):
                        act.wait_ge(S("gp" + nm), q + 1)
                        a.activation(u["g"][:, q * T:(q + 1) * T], PS[:, b + q % 2, :], ACT.Copy).then_inc(S("g" + nm), 1)
                    for c in range(2):
                        act.wait_ge(S("f" + nm), c + 1)
                        a.activation(u["f2"][:, c, :], PS[:, b + c, 0:n], ACT.Copy).then_inc(S("f_out" + nm), 1)
                    for c in range(2):
                        act.wait_ge(S("y" + nm), c + 1)
                        a.activation(u["mx"][:, 6 + c, :], PS[:, b + 2 + c, 0:n], ACT.Copy).then_inc(S("y_out" + nm), 1)
                for s in full:
                    nm, n, b = s["name"], s["n"], s["bank"]
                    for c in range(2):
                        act.wait_ge(S("pooled" + nm), c + 1)
                        a.activation(U[nm]["mx"][:, 4 + c, :], PS[:, b + 2 + c, 0:n], ACT.Copy, scale=par_col("pool_scale", c)).then_inc(S("pool_out"), 1)

        def half(h):
            return slice(64 * (h % 2), 64 * (h % 2) + 64)

        attention(nc, stage, PS, ident, None, heads=8, dv=64, rows=64, blocks=T // P,
                  query=lambda h: QN[half(h), h // 2, :], key=lambda h: KA[half(h), h // 4, :],
                  value=lambda h, kb: VV[:, kb, (h // 4) * 64:(h // 4) * 64 + 64], nkeys=[CKV] * (T // P),
                  scale=HD ** -0.5, out=lambda h: MX[half(h), h // 2, :],
                  probs=[X[:, a * T:a * T + CKV] for a in (52, 54, 56)], probsT=[XT(0, 6), XT(6, 6)], small=XT(58), part=lambda h: 64 * (h % 2))
        if update:
            attention(nc, stage, PS, ident, None, heads=8, dv=64, rows=64, blocks=CTX // P,
                      query=lambda h: QNc[half(h), h // 2, :], key=lambda h: KA[half(h), h // 4, 0:CTX],
                      value=lambda h, kb: VV[:, kb, (h // 4) * 64:(h // 4) * 64 + 64], nkeys=[CTX] * (CTX // P),
                      scale=HD ** -0.5, out=lambda h: MXc[half(h), h // 2, :],
                      probs=[XT(a)[:, 0:CTX] for a in (52, 54, 56)], probsT=[XT(0, 2), XT(6, 2)], small=XT(58), part=lambda h: 64 * (h % 2))
        if debug == f"mx{layer}":
            dump(nc, A, MX, stage, loaded)
            return

        def project(first, kt, rhs, gate):
            S, other = stage()
            per = (kt + 7) // 8
            with nc.Block() as block:
                @block.sync
                def _(sp):
                    clear(sp, other)
                    stream.send(sp, min(first + 8 * per + RING - 1, NCHUNK2))

                @block.tensor
                def _(pe):
                    for m in range(8):
                        if m >= 4:
                            for s in full:
                                pe.wait_ge(S("added" + s["name"]), m - 3)
                        for j in range(per):
                            n = first + m * per + j
                            stream.wait(pe, n)
                            for i, s in enumerate(full):
                                for k in range(8 * j, min(8 * j + 8, kt)):
                                    mm = nc.tensor.matmul(PS[:, s["bank"] + m % 4, 0:s["n"]], tile_of(stream.chunk(n), k - 8 * j), rhs[s["name"]][:, k, :], start=(k == 0), stop=(k == kt - 1))
                                    if i == 0 and k == 8 * j:
                                        first_use(mm, n)
                                if j == per - 1:
                                    mm.then_inc(S("product" + s["name"]), 1)

                @block.vector
                def _(dve):
                    for m in range(8):
                        for s in full:
                            dve.wait_ge(S("product" + s["name"]), m + 1)
                            nc.vector.scalar_tensor_tensor(out=s["src"][:, m, :], in0=PS[:, s["bank"] + m % 4, 0:s["n"]], scalar=mod[:, gate + m, s["k"]:s["k"] + 1],
                                                           in1=s["src"][:, m, :], op0=ALU.mult, op1=ALU.add).then_inc(S("added" + s["name"]), 1)

        project(FIRST2["out"], 8, {"x": MX, "c": MXc}, GA1)
        norm_mod(1, SH2, full)

        n0 = FIRST2["up"]
        FFN = {"x": XT(12, FT), "c": XT(34, FT, CTX)}
        SG = {"x": XT(45, 2), "c": XT(47, 2, CTX)}
        S, other = stage()
        with nc.Block() as block:
            @block.sync
            def _(sp):
                clear(sp, other)
                stream.send(sp, n0 + 2 * FT + RING - 1)

            @block.tensor
            def _(pe):
                for t in range(FT):
                    if t >= 2:
                        for s in full:
                            pe.wait_ge(S("act" + s["name"]), t - 1)
                    for j in range(2):
                        gemm(pe, n0 + 2 * t + j, [(PS[:, s["bank"] + 2 * (t % 2) + j, 0:s["n"]], s["h"], S(("gate", "up")[j] + s["name"])) for s in full])

            @block.scalar
            def _(act):
                for t in range(FT):
                    for s in full:
                        act.wait_ge(S("gate" + s["name"]), t + 1)
                        if t >= 2:
                            act.wait_ge(S("act" + s["name"]), t - 1)
                        nc.scalar.activation(SG[s["name"]][:, t % 2, :], PS[:, s["bank"] + 2 * (t % 2), 0:s["n"]], ACT.Silu).then_inc(S("silu" + s["name"]), 1)

            @block.vector
            def _(dve):
                for t in range(FT):
                    for s in full:
                        dve.wait_ge(S("silu" + s["name"]), t + 1)
                        dve.wait_ge(S("up" + s["name"]), t + 1)
                        nc.vector.tensor_tensor(FFN[s["name"]][:, t, :], PS[:, s["bank"] + 2 * (t % 2) + 1, 0:s["n"]], SG[s["name"]][:, t % 2, :], ALU.mult).then_inc(S("act" + s["name"]), 1)

        project(FIRST2["down"], FT, FFN, GA2)

        S, other = stage()
        with nc.Block() as block:
            @block.sync
            def _(sp):
                clear(sp, other)
                clear(sp, arrived)
                sp.sem_clear(used)


def dump(nc, A, what, stage, loaded):
    S, other = stage()
    with nc.Block() as block:
        @block.sync
        def _(sp):
            clear(sp, other)
            n = what.shape[1] * what.shape[2]
            sp.dma_start(A["out"][:, 0:n].rearrange("p (a b) -> p a b", a=what.shape[1]), what).then_inc(S("dumped"), 16)
            sp.wait_ge(S("dumped"), 16)


def blocks(w, m=P):
    k = w.shape[0] // P
    return w.reshape(k, P, w.shape[1]).transpose(1, 0, 2).reshape(P, -1)


def fill(a):
    out = np.zeros((P, CW), np.float32)
    out[:, :a.shape[1]] = a
    return out


OFF = {}
_at = 0
for _name, _n in (("rw", 1664), ("rw_g", 512), ("q_lat", 384), ("kv_lat", 256), ("k_pe", 32), ("mla_g", 512),
                  ("conv_u", 1024), ("conv_g", 512), ("xq", 512), ("xg", 512), ("merge", 4096)):
    OFF[_name] = _at
    _at += _n


def chunks1(I, l):
    w = I["w_in"][l]

    def cols(name, t, n=P):
        a = OFF[name] + t * P
        return blocks(w[:, a:a + n])

    out = [cols("rw", t) for t in range(13)]
    out += [cols("q_lat", t) for t in range(3)] + [cols("kv_lat", t) for t in range(2)]
    kpe = np.zeros((D, P), np.float32)
    kpe[:, :32] = w[:, OFF["k_pe"]:OFF["k_pe"] + 32]
    out.append(blocks(kpe))
    uq = I["mla_w_uq"][l]
    heads = [blocks(uq[:, h * 96:(h + 1) * 96]) for h in range(8)]
    for a in (0, 3, 6):
        out.append(fill(np.concatenate(heads[a:a + 3], 1)))
    ukv = I["mla_w_ukv"][l].reshape(256, 8, 128)
    out.append(np.concatenate([blocks(ukv[:, h, :64]) for h in range(8)], 1))
    out.append(blocks(ukv[:, :, 64:].reshape(256, 512)))
    out += [cols("conv_u", t) for t in range(8)]
    out += [cols("xq", t) for t in range(4)]
    mk = I["xattn_w_mem_kv"][l]
    out += [blocks(mk[:, t * P:(t + 1) * P]) for t in range(4)]
    out += [blocks(mk[k * 256:(k + 1) * 256, 512:]) for k in range(4)]
    for name in ("rw_g", "mla_g", "conv_g", "xg"):
        out += [cols(name, t) for t in range(4)]
    ob = I["w_o_branch"][l]
    for m in range(8):
        o = [blocks(ob[n][:, m * P:(m + 1) * P]) for n in range(4)]
        g = [cols("merge", 8 * n + m) for n in range(4)]
        out += [np.concatenate(o[0:2], 1), g[0], g[1], np.concatenate(o[2:4], 1), g[2], g[3]]
    out += [blocks(I["w_out"][l][:, m * P:(m + 1) * P]) for m in range(8)]
    return np.stack(out)


def colsof(v):
    return v.reshape(-1, P).T


def params1(I, l):
    out = np.zeros((P, NPAR), np.float32)

    def put(name, a):
        out[:, PCOL[name]:PCOL[name] + a.shape[1]] = a

    put("b_gate", colsof(I["b_gate"][l].reshape(-1)))
    for name, key in (("mu", "rwkv_mu"), ("w0", "rwkv_w0"), ("a0", "rwkv_a0"), ("k_k", "rwkv_k_k"), ("k_a", "rwkv_k_a"),
                      ("lnx_g", "rwkv_lnx_g"), ("lnx_b", "rwkv_lnx_b"), ("q_norm", "mla_q_norm"), ("kv_norm", "mla_kv_norm"),
                      ("conv_b", "conv_b"), ("cln_g", "conv_ln_g"), ("cln_b", "conv_ln_b"), ("ln_g", "ln_g"), ("ln_b", "ln_b")):
        put(name, colsof(I[key][l]))
    put("r_k", colsof(I["rwkv_r_k"][l].reshape(-1)))
    put("conv_w", I["conv_w"][l].reshape(TAPS, WT, P).transpose(2, 1, 0).reshape(P, WT * TAPS))
    put("w2a2", np.concatenate([I["rwkv_w2"][l], I["rwkv_a2"][l]], 0))
    return out


def consts1():
    out = np.zeros((P, NCST), np.float32)

    def put(name, a, k=0):
        out[:, CCOL[name] + k:CCOL[name] + k + a.shape[1]] = a

    i = np.arange(P)
    row, col = i[:, None], i[None, :]
    put("ident", np.eye(P, dtype=np.float32))
    put("head_ones", (row // 64 == col // 64).astype(np.float32))
    put("ones", np.ones((P, P), np.float32))
    same = row // 64 == col // 64
    put("tri", (same & (row < col)).astype(np.float32))
    put("tri", (same & (row <= col)).astype(np.float32), P)
    for lv in range(6):
        n = 1 << lv
        low = (row // (2 * n) == col // (2 * n)) & ((row // n) % 2 == 1) & ((col // n) % 2 == 0)
        if lv == 0:
            put("m0", low.astype(np.float32))
        put("lev", low.T.astype(np.float32), lv * P)
    put("causal", np.where(col > row, -1e30, 0.0).astype(np.float32))
    for a in range(32):
        out[64 + (a + 16) % 32, CCOL["swap"] + a] = 1.0
    inv = (np.float32(10000.0) ** (-np.arange(0, 32, 2, dtype=np.float32) / np.float32(32))).astype(np.float32)
    out[64:96, CCOL["freq"]] = np.concatenate([inv, inv])
    out[64:80, CCOL["sign"]] = -1.0
    out[80:96, CCOL["sign"]] = 1.0
    for k, e in enumerate((64e-5, 1e-6, 1e-5, 0.0)):
        out[:, CCOL["eps"] + k] = e
    put("reset", np.broadcast_to((np.arange(T) % CH != 0).astype(np.float32), (P, T)))
    return out


def turned(a):
    return np.ascontiguousarray(a.T.reshape(DK, P, -1).transpose(1, 0, 2).reshape(P, -1))


def layouts(I):
    return {
        "xT": turned(I["x"][0]),
        "memT": turned(I["mem"][0]),
        "pos": np.ascontiguousarray(I["positions"].reshape(T)),
        "cst1": consts1(),
        "par1": np.stack([params1(I, l) for l in range(LAYERS)]),
        "w1": np.stack([chunks1(I, l) for l in range(LAYERS)]),
    }


def pair_diag(w):
    out = np.zeros((P, P), np.float32)
    out[:64, :64], out[64:, 64:] = w[0], w[1]
    return out


def chunks2(I, l):
    w = I["w_in_2"][l]
    out = [blocks(w[:, t * P:(t + 1) * P]) for t in range(4)]
    for g in range(2):
        k = w[:, 512 + 64 * g:512 + 64 * g + 64]
        out.append(blocks(np.concatenate([k, k], 1)))
    out += [blocks(w[:, a:a + P]) for a in (640, 768, 896, 1024, 1152)]
    out += [blocks(I["w_out_2"][l][:, m * P:(m + 1) * P]) for m in range(8)]
    gu = I["w_gate_up_2"][l]
    for t in range(FT):
        out += [blocks(gu[:, t * P:(t + 1) * P]), blocks(gu[:, FF + t * P:FF + (t + 1) * P])]
    dn = I["w_down_2"][l]
    for m in range(8):
        for a in (0, 8, 16):
            out.append(fill(blocks(dn[a * P:min(a + 8, FT) * P, m * P:(m + 1) * P])))
    return np.stack(out)


def params2(I, l):
    out = np.zeros((P, NPAR2), np.float32)

    def put(name, a, k=0):
        out[:, PCOL2[name] + k:PCOL2[name] + k + a.shape[1]] = a

    put("g_mix", colsof(I["g_mix_2"][l]))
    put("g_ffn", colsof(I["g_ffn_2"][l]))
    put("b_ada", colsof(I["b_ada_2"][l]))
    for name in ("q_gain", "k_gain"):
        g = I[name + "_2"][l]
        put(name, np.concatenate([g, g])[:, None])
    put("pool_scale", colsof(I["pool_scale_2"][l]))
    for c in range(2):
        put("w_pool", pair_diag(I["w_pool_2"][l][2 * c:2 * c + 2]), c * P)
        put("w_four", pair_diag(I["w_four_2"][l][2 * c:2 * c + 2]), c * P)
    return out


def dft(n):
    i = np.arange(n)
    a = 2.0 * np.pi * ((i[:, None] * i[None, :]) % n) / n
    both = np.stack([np.cos(a), -np.sin(a)], 1) / np.sqrt(n * 64.0)
    return both.reshape(n // P, P, 2, n).transpose(1, 0, 2, 3).reshape(P, -1).astype(np.float32)


def counts(n):
    t = np.arange(n)
    out = np.zeros((P, 2, n), np.float32)
    for g, w in enumerate((2, 4, 8, 16)):
        lo, hi = np.clip(t - w // 2, 0, n), np.clip(t + w - w // 2, 0, n)
        out[64 * (g % 2):64 * (g % 2) + 64, g // 2, :] = (1.0 / (hi - lo)).astype(np.float32)
    return out.reshape(P, -1)


def consts2():
    out = np.zeros((P, NCST2), np.float32)

    def put(name, a):
        out[:, CCOL2[name]:CCOL2[name] + a.shape[1]] = a

    i = np.arange(P)
    row, col = i[:, None], i[None, :]
    put("ident", np.eye(P, dtype=np.float32))
    put("head_ones", (row // 64 == col // 64).astype(np.float32))
    put("ones", np.ones((P, P), np.float32))
    put("swap", (row == (col ^ 16)).astype(np.float32))
    t = np.arange(T)
    freqs = (np.float32(10000.0) ** (-np.arange(16, dtype=np.float32) / np.float32(16))).astype(np.float32)
    place = np.stack([t // 64, t % 64]).astype(np.float32)
    r = i % 64
    ang = (place[r // 32] * freqs[r % 16][:, None]).astype(np.float32).astype(np.float64)
    put("cos", np.cos(ang).astype(np.float32))
    put("sin", (np.sin(ang) * np.where((r // 16) % 2, 1.0, -1.0)[:, None]).astype(np.float32))
    j = np.arange(64)
    a = 2.0 * np.pi * ((j[:, None] * j[None, :]) % 64) / 64
    put("cs64", np.concatenate([pair_diag(np.stack([f, f])) for f in (np.cos(a), np.sin(a))], 1).astype(np.float32))
    put("count_x", counts(T))
    put("count_c", counts(CTX))
    out[:, CCOL2["eps"]] = 1e-6
    return out


def layouts2(I):
    return {
        "ctxT": turned(I["ctx_2"][0]),
"cond": np.ascontiguousarray(np.stack([I["c_2"].reshape(D), I["c_ctx_2"].reshape(D)])),
        "ada": np.stack([I["w_ada_2"][l].T.reshape(48, P, D) for l in range(LAYERS)]),
        "cst2": consts2(),
        "par2": np.stack([params2(I, l) for l in range(LAYERS)]),
        "dft_x": dft(T),
        "dft_c": dft(CTX),
        "w2": np.stack([chunks2(I, l) for l in range(LAYERS)]),
    }


_INS = ["x", "mem", "positions", "w_in", "b_gate", "rwkv_mu", "rwkv_w0", "rwkv_w2", "rwkv_a0", "rwkv_a2", "rwkv_k_k",
        "rwkv_k_a", "rwkv_r_k", "rwkv_lnx_g", "rwkv_lnx_b", "mla_q_norm", "mla_w_uq", "mla_kv_norm", "mla_w_ukv",
        "conv_w", "conv_b", "conv_ln_g", "conv_ln_b", "xattn_w_mem_kv", "w_o_branch", "w_out", "ln_g", "ln_b", "c_2",
        "ctx_2", "c_ctx_2", "w_ada_2", "b_ada_2", "g_mix_2", "g_ffn_2", "w_in_2", "q_gain_2", "k_gain_2", "w_pool_2",
        "pool_scale_2", "w_four_2", "w_out_2", "w_gate_up_2", "w_down_2"]


def kernel(**inputs):
    import concourse.bacc as bacc
    from concourse.bass_utils import run_bass_kernel_spmd as run

    I = {name: np.asarray(inputs[name]) for name in _INS}
    nc = bacc.Bacc("TRN2", target_bir_lowering=False, num_devices=1)
    arrays, A = {}, {}
    for name, a in {**layouts(I), **layouts2(I)}.items():
        a = np.ascontiguousarray(a)
        arrays[f"in_{name}"] = a
        A[name] = nc.dram_tensor(f"in_{name}", a.shape, mybir.dt.from_np(a.dtype), kind="ExternalInput").ap()
    A["out"] = nc.dram_tensor("out_0", (P, DK * T), F32, kind="ExternalOutput").ap()
    build(nc, A)
    r = run(nc, [arrays], core_ids=[0])
    got = r.results[0]["out_0"]
    return np.ascontiguousarray(got.reshape(P, DK, T).transpose(2, 1, 0).reshape(1, T, D))
```

```python
from contextlib import ExitStack

import numpy as np

import concourse.bass as bass
from concourse import mybir
from concourse.alu_op_type import AluOpType as ALU

F32 = mybir.dt.float32
I32 = mybir.dt.int32
F32R = mybir.dt.float32r
ACT = mybir.ActivationFunctionType
AX_X = mybir.AxisListType.X

P = 128
T = 512
D = 1024
DK = D // P
W = 512
WT = W // P
NB = 4
LAYERS = 2
MEM = 256
CTX = 256
HD = 64
CH = 64
NCH = T // CH
TAPS = 31
RW_TILES = 13
EXPH = float(np.exp(-0.5))
DEEP_ALPHA = (2.0 * LAYERS) ** 0.25
RING = 3
PARTS = 2
CW = 1024

PCOL = {}
_at = 0
for _name, _n in (("b_gate", 32), ("mu", 13), ("w0", 4), ("a0", 4), ("k_k", 4), ("k_a", 4), ("r_k", 4),
                  ("lnx_g", 4), ("lnx_b", 4), ("q_norm", 3), ("kv_norm", 2), ("conv_b", 4),
                  ("cln_g", 4), ("cln_b", 4), ("ln_g", 8), ("ln_b", 8), ("conv_w", WT * TAPS),
                  ("w2a2", 512)):
    PCOL[_name] = _at
    _at += _n
NPAR = _at

CCOL = {}
_at = 0
for _name, _n in (("ident", 128), ("head_ones", 128), ("ones", 128), ("tri", 256), ("m0", 128),
                  ("lev", 6 * 128), ("causal", 128), ("swap", 32), ("freq", 1), ("sign", 1),
                  ("eps", 4), ("reset", 512)):
    CCOL[_name] = _at
    _at += _n
NCST = _at

STAGE_CHUNKS = (("rwkv", RW_TILES), ("mla", 6 + 3 + 2), ("conv", 8), ("xattn", 4 + 8), ("gates", 16),
                ("merge", 6 * 8), ("out", 8))
FIRST = {}
_at = 0
for _name, _n in STAGE_CHUNKS:
    FIRST[_name] = _at
    _at += _n
NCHUNK1 = _at
SPLIT1 = [FIRST[_name] + _i for _name, _n in (("rwkv", RW_TILES), ("mla", 6), ("conv", 8), ("xattn", 4), ("gates", 16)) for _i in range(_n)]
SPLIT1 += [FIRST["merge"] + _i for _i in range(48) if _i % 3]


class Names:

    def __init__(self, handles):
        self.handles, self.of = handles, {}

    def __call__(self, name):
        if name not in self.of:
            self.of[name] = self.handles[len(self.of)]
        return self.of[name]


class Stream:

    def __init__(self, W, source, is_split):
        self.ring, self.highs, self.lows, self.arrived, self.used, self.hi_made, self.lo_made = W
        self.source, self.splits = source, is_split
        self.sent = self.hi_at = self.lo_at = 0

    def send(self, sp, upto):
        for n in range(self.sent, upto):
            last = n - RING
            if last in self.splits:
                sp.wait_ge(self.lo_made, self.splits.index(last) + 1)
            elif last >= 0:
                sp.wait_ge(self.used, last + 1)
            sp.dma_start(self.ring[:, n % RING, :], self.source(n)).then_inc(self.arrived[n % RING], 16)
        self.sent = max(self.sent, upto)

    def hi(self, nc, act, upto):
        for n in range(self.hi_at, upto):
            if n in self.splits:
                s = self.splits.index(n)
                self.wait(act, n)
                if s >= PARTS:
                    act.wait_ge(self.used, self.splits[s - PARTS] + 1)
                nc.scalar.activation(self.high(n), self.chunk(n), ACT.Copy).then_inc(self.hi_made, 1)
        self.hi_at = max(self.hi_at, upto)

    def lo(self, nc, pool, upto):
        for n in range(self.lo_at, upto):
            if n in self.splits:
                pool.wait_ge(self.hi_made, self.splits.index(n) + 1)
                nc.gpsimd.tensor_tensor(self.low(n), self.chunk(n), self.high(n).bitcast(F32), ALU.subtract).then_inc(self.lo_made, 1)
        self.lo_at = max(self.lo_at, upto)

    def wait(self, eng, n):
        eng.wait_ge(self.arrived[n % RING], 16 * (n // RING + 1))

    def wait_split(self, pe, n):
        pe.wait_ge(self.lo_made, self.splits.index(n) + 1)

    def chunk(self, n):
        return self.ring[:, n % RING, :]

    def high(self, n):
        return self.highs[:, self.splits.index(n) % PARTS, :]

    def low(self, n):
        return self.lows[:, self.splits.index(n) % PARTS, :]


def three(nc, ps, high, low, xhigh, xlow, start, stop, mark=None):
    mm = nc.tensor.matmul(ps, high, xhigh, start=start, stop=False)
    if mark is not None:
        mm.then_inc(mark, 1)
    nc.tensor.matmul(ps, high, xlow, start=False, stop=False)
    return nc.tensor.matmul(ps, low, xhigh, start=False, stop=stop)


def tile_of(chunk, k, m=P):
    return chunk[:, k * m:(k + 1) * m]


def build(nc, A):
    with ExitStack() as ctx:
        def sb(name, shape, dt=F32):
            return ctx.enter_context(nc.sbuf_tensor(name, shape, dt))

        pools = [[nc.alloc_semaphore(f"stage{p}_{i}") for i in range(50)] for p in range(2)]
        arrived = [nc.alloc_semaphore(f"chunk_arrived{i}") for i in range(RING)]
        used = nc.alloc_semaphore("chunks_used")
        hi_made, lo_made = nc.alloc_semaphore("high_made"), nc.alloc_semaphore("low_made")
        loaded = nc.alloc_semaphore("loaded")
        stored = nc.alloc_semaphore("stored")
        PS = ctx.enter_context(nc.psum_tensor("ps", [P, 8, 512], F32))
        turn = [0]

        def stage():
            turn[0] += 1
            return Names(pools[turn[0] % 2]), pools[(turn[0] + 1) % 2]

        WR = (sb("ring", [P, RING, CW]), sb("highs", [P, PARTS, CW], F32R), sb("lows", [P, PARTS, CW], F32R),
              arrived, used, hi_made, lo_made)
        mods = sb("mods", [P, LAYERS, 96])
        XH, XL = sb("x_high", [P, DK, T], F32R)[:, :, :], sb("x_low", [P, DK, T], F32R)[:, :, :]
        with ExitStack() as one:
            first(nc, one, A, PS, XH, XL, WR, mods, stage, loaded)
        with ExitStack() as two:
            second(nc, two, A, PS, XH, XL, WR, mods, stage, stored)


def clear(sp, sems):
    for s in sems:
        sp.sem_clear(s)


def attention(nc, stage, PS, ident, causal, heads, dv, rows, blocks, query, key, value, nkeys, scale, out,
              probs, probsT, small, part):
    S, other = stage()
    units = [(h, q) for h in range(heads) for q in range(blocks)]
    wide = max(nkeys) > 512
    nbuf = len(probs)

    def turns(q):
        return (nkeys[q] + 511) // 512

    before = [0]
    for h, q in units:
        before.append(before[-1] + turns(q))
    stats = small.rearrange("p (s u) -> p s u", s=4)

    def scores(i, q):
        a = 2 * (i % 2) if wide else i % 4
        return PS[:, a:a + 2, :].rearrange("p b n -> p (b n)")[:, 0:nkeys[q]] if wide else PS[:, a, 0:nkeys[q]]

    sbuf = 2 if wide else 4

    def finish(act, h):
        act.wait_ge(S("product"), h + 1)
        nc.scalar.activation(out(h), PS[part(h):part(h) + dv, 6 + h % 2, 0:blocks * P], ACT.Copy).then_inc(S("out"), 1)

    with nc.Block() as block:
        @block.sync
        def _(sp):
            clear(sp, other)

        @block.tensor
        def _(pe):
            def make_scores(i):
                h, q = units[i]
                if i >= sbuf:
                    pe.wait_ge(S("probs"), i - sbuf + 1)
                s = scores(i, q)
                for a in range(0, nkeys[q], 512):
                    b = min(a + 512, nkeys[q])
                    mm = nc.tensor.matmul(s[:, a:b], query(h)[:, q * P:(q + 1) * P], key(h)[:, a:b], start=True, stop=True)
                mm.then_inc(S("scores"), 1)

            def turn(i):
                h, q = units[i]
                pe.wait_ge(S("scaled"), i + 1)
                for j in range(turns(q)):
                    n = before[i] + j
                    if n >= 2:
                        pe.wait_ge(S("turned_out"), n - 1)
                    for kb in range(4 * j, min(4 * j + 4, nkeys[q] // P)):
                        mm = nc.tensor.transpose(PS[:, 4 + n % 2, (kb % 4) * P:(kb % 4 + 1) * P], probs[i % nbuf][:, kb * P:(kb + 1) * P], ident)
                    mm.then_inc(S("turned"), 1)

            def product(h):
                pe.wait_ge(S("turned_out"), before[blocks * (h + 1)])
                if h >= 2:
                    pe.wait_ge(S("out"), h - 1)
                top = nkeys[-1] // P
                for kb in range(top):
                    q0 = min(q for q in range(blocks) if nkeys[q] > kb * P)
                    mm = nc.tensor.matmul(PS[part(h):part(h) + dv, 6 + h % 2, q0 * P:blocks * P], value(h, kb), probsT[h % 2][:, kb, q0 * P:blocks * P],
                                          start=(kb == 0), stop=(kb == top - 1))
                mm.then_inc(S("product"), 1)

            lead = 2 if wide else 3
            for i in range(min(lead, len(units))):
                make_scores(i)
            for i in range(len(units)):
                if i + lead < len(units):
                    make_scores(i + lead)
                turn(i)
                if i and i % blocks == 0:
                    product(i // blocks - 1)
            product(heads - 1)

        @block.scalar
        def _(act):
            for i, (h, q) in enumerate(units):
                act.wait_ge(S("negmax"), i + 1)
                if i >= nbuf:
                    act.wait_ge(S("turned"), before[i - nbuf + 1])
                nc.scalar.activation(probs[i % nbuf][:, 0:nkeys[q]], scores(i, q), ACT.Exp, scale=scale, bias=stats[:, 1, i:i + 1],
                                     accum_out=stats[:, 2, i:i + 1]).then_inc(S("probs"), 1)
                if i >= 2 and (i - 2) % blocks == blocks - 1:
                    finish(act, (i - 2) // blocks)
            finish(act, heads - 1)

        @block.vector
        def _(dve):
            v = nc.vector

            def maximum(i):
                h, q = units[i]
                dve.wait_ge(S("scores"), i + 1)
                s = scores(i, q)
                if causal is not None:
                    v.tensor_tensor(s[:, q * P:(q + 1) * P], s[:, q * P:(q + 1) * P], causal, ALU.add).then_inc(S("causal"), 1)
                    dve.wait_ge(S("causal"), i + 1)
                v.tensor_reduce(stats[:, 0, i:i + 1], s, AX_X, ALU.max).then_inc(S("max"), 1)
                dve.wait_ge(S("max"), i + 1)
                v.tensor_scalar(stats[:, 1, i:i + 1], stats[:, 0, i:i + 1], -scale, None, ALU.mult).then_inc(S("negmax"), 1)

            def normalise(i):
                h, q = units[i]
                dve.wait_ge(S("probs"), i + 1)
                v.reciprocal(stats[:, 3, i:i + 1], stats[:, 2, i:i + 1]).then_inc(S("inverse"), 1)
                dve.wait_ge(S("inverse"), i + 1)
                p = probs[i % nbuf][:, 0:nkeys[q]]
                v.tensor_scalar(p, p, stats[:, 3, i:i + 1], None, ALU.mult).then_inc(S("scaled"), 1)

            def turned_out(i):
                h, q = units[i]
                if q == 0 and h >= 2:
                    dve.wait_ge(S("product"), h - 1)
                for j in range(turns(q)):
                    n = before[i] + j
                    nb = min(4, nkeys[q] // P - 4 * j)
                    dve.wait_ge(S("turned"), n + 1)
                    v.tensor_copy(probsT[h % 2][:, 4 * j:4 * j + nb, q * P:(q + 1) * P],
                                  PS[:, 4 + n % 2, 0:nb * P].rearrange("p (k t) -> p k t", k=nb)).then_inc(S("turned_out"), 1)

            for i in range(len(units) + 2):
                if i < len(units):
                    maximum(i)
                if 1 <= i <= len(units):
                    normalise(i - 1)
                if i >= 2:
                    turned_out(i - 2)


def first(nc, ctx, A, PS, XH, XL, WR, mods, stage, loaded):
    def sb(name, shape, dt=F32):
        return ctx.enter_context(nc.sbuf_tensor(name, shape, dt))

    memT = sb("memT", [P, DK, MEM])
    xh = XH.bitcast(F32)
    used = WR[4]
    cst = sb("cst", [P, NCST])
    par = sb("par", [P, NPAR])
    oneless = sb("oneless", [P, 4])
    rope = sb("rope", [P, 2, T])
    BR = sb("BR", [P, NB * WT, T])
    X = sb("X", [P, 44 * T])

    def C(name, n=1, k=0):
        a = CCOL[name] + k
        return cst[:, a:a + n]

    def par_col(name, k=0):
        a = PCOL[name] + k
        return par[:, a:a + 1]

    def XT(i, n=1):
        return X[:, i * T:(i + n) * T] if n == 1 else X[:, i * T:(i + n) * T].rearrange("p (n t) -> p n t", n=n)

    ident = C("ident", P)

    S, other = stage()
    with nc.Block() as block:
        @block.sync
        def _(sp):
            sp.dma_start(cst[:, :], A["cst1"]).then_inc(loaded, 16)
            sp.dma_start(XT(4, 8).rearrange("p k t -> p (k t)"), A["xT"]).then_inc(loaded, 16)
            sp.dma_start(memT[:, :, :].rearrange("p k t -> p (k t)"), A["memT"]).then_inc(loaded, 16)
            sp.dma_start(X[64:96, 0:T].bitcast(I32), A["pos"].partition_broadcast(32)).then_inc(loaded, 16)
            sp.wait_ge(loaded, 64)

        @block.vector
        def _(dve):
            count = [0]

            def link(ins):
                count[0] += 1
                ins.then_inc(S("angle_step"), 1)
                dve.wait_ge(S("angle_step"), count[0])

            two_pi = 2.0 * np.pi
            c1 = float(np.float32(6.28125))
            c2 = float(np.float32(np.float32(two_pi - c1).view(np.uint32) & np.uint32(0xFFFFF000)) if False else np.float32(round((two_pi - c1) * 2 ** 19) / 2 ** 19))
            c3 = float(np.float32(two_pi - c1 - c2))
            magic = float(1.5 * 2 ** 23)
            pos, ang, turns, cosr = (X[64:96, i * T:(i + 1) * T] for i in range(4))
            rows = slice(64, 96)
            freq = cst[rows, CCOL["freq"]:CCOL["freq"] + 1]
            sgn = cst[rows, CCOL["sign"]:CCOL["sign"] + 1]
            dve.wait_ge(loaded, 64)
            v = nc.vector
            link(v.tensor_copy(turns, pos.bitcast(I32)))
            link(v.tensor_scalar(ang, turns, freq, None, ALU.mult))
            link(v.tensor_scalar(pos, ang, 1.0 / two_pi, None, ALU.mult))
            link(v.tensor_scalar(turns, pos, magic, None, ALU.add))
            link(v.tensor_scalar(turns, turns, magic, None, ALU.subtract))
            for c in (c1, c2, c3):
                link(v.scalar_tensor_tensor(out=ang, in0=turns, scalar=-c, in1=ang, op0=ALU.mult, op1=ALU.add))
            link(v.tensor_scalar(cosr, ang, float(np.pi / 2), None, ALU.add))
            link(v.tensor_scalar(pos, cosr, float(np.pi), None, ALU.is_gt))
            link(v.scalar_tensor_tensor(out=cosr, in0=pos, scalar=-two_pi, in1=cosr, op0=ALU.mult, op1=ALU.add))
            top = float(np.float32(3.1415925))
            link(v.tensor_scalar(cosr, cosr, top, -top, ALU.min, ALU.max))
            link(v.tensor_scalar(ang, ang, top, -top, ALU.min, ALU.max))
            v.memset(oneless[:, :], 0.0).then_inc(S("angles"), 1)
            dve.wait_ge(S("sines"), 2)
            v.tensor_scalar(rope[rows, 1, :], rope[rows, 1, :], sgn, None, ALU.mult).then_inc(S("signed"), 1)

        @block.scalar
        def _(act):
            act.wait_ge(loaded, 64)
            for k in range(DK):
                nc.scalar.activation(XH[:, k, :], XT(4 + k), ACT.Copy).then_inc(S("x_hi"), 1)
            act.wait_ge(S("angles"), 1)
            nc.scalar.activation(rope[64:96, 0, :], X[64:96, 3 * T:4 * T], ACT.Sin).then_inc(S("sines"), 1)
            nc.scalar.activation(rope[64:96, 1, :], X[64:96, T:2 * T], ACT.Sin).then_inc(S("sines"), 1)

        @block.gpsimd
        def _(pool):
            for k in range(DK):
                pool.wait_ge(S("x_hi"), k + 1)
                nc.gpsimd.tensor_tensor(XL[:, k, :], XT(4 + k), xh[:, k, :], ALU.subtract).then_inc(S("x_lo"), 1)

    with nc.Fori(0, LAYERS) as layer:
        stream = Stream(WR, lambda n: A["w1"][bass.ds(layer, 1), n, :, :].rearrange("l p c -> p (l c)"), SPLIT1)

        def gemm(pe, bank, n, rhs, done, m=P, base=0, wait_bank=None):
            stream.wait(pe, n)
            for k in range(DK):
                mm = nc.tensor.matmul(PS[base:base + m, bank, 0:rhs.shape[2]], tile_of(stream.chunk(n), k)[:, 0:m],
                                      rhs[:, k, :], start=(k == 0), stop=(k == DK - 1))
                if k == 0 and n:
                    mm.then_inc(used, 1)
            mm.then_inc(done, 1)

        def gemm3(pe, bank, n, xh, xl, done):
            stream.wait_split(pe, n)
            for k in range(DK):
                mm = three(nc, PS[:, bank, :], tile_of(stream.high(n), k), tile_of(stream.low(n), k), xh[:, k, :], xl[:, k, :],
                           k == 0, k == DK - 1, used if k == 0 and n else None)
            mm.then_inc(done, 1)

        n0 = FIRST["rwkv"]
        P0 = 0
        praw = X[:, 30 * T:30 * T + 13 * 513].rearrange("p (c t) -> p c t", c=13)
        M = XT(0, 13)
        S, other = stage()
        with nc.Block() as block:
            @block.sync
            def _(sp):
                clear(sp, other)
                sp.dma_start(par[:, :], A["par1"][bass.ds(layer, 1), :, :].rearrange("l p c -> p (l c)")).then_inc(S("par"), 16)
                stream.send(sp, n0 + RW_TILES + RING - 1)
                sp.wait_ge(S("par"), 16)

            @block.tensor
            def _(pe):
                for t in range(RW_TILES):
                    if t >= 4:
                        pe.wait_ge(S("evicted"), t - 3)
                    gemm3(pe, t % 4, n0 + t, XH, XL, S("product"))

            @block.scalar
            def _(act):
                stream.hi(nc, act, n0 + PARTS)
                for t in range(RW_TILES):
                    act.wait_ge(S("product"), t + 1)
                    nc.scalar.activation(praw[:, t, 1:T + 1], PS[:, t % 4, :], ACT.Copy).then_inc(S("evicted"), 1)
                    stream.hi(nc, act, n0 + min(t + 3, RW_TILES + 1))

            @block.gpsimd
            def _(pool):
                stream.lo(nc, pool, n0 + RW_TILES + 1)

            @block.vector
            def _(dve):
                v = nc.vector
                v.memset(praw[:, :, 0:1], 0.0).then_inc(S("zeroed"), 1)
                dve.wait_ge(S("zeroed"), 1)
                dve.wait_ge(S("par"), 16)
                v.tensor_scalar(oneless[:, :], par[:, PCOL["k_a"]:PCOL["k_a"] + 4], -1.0, 1.0, ALU.mult, ALU.add).then_inc(S("oneless"), 1)
                for t in range(RW_TILES):
                    dve.wait_ge(S("evicted"), t + 1)
                    v.tensor_tensor(XT(13 + t % 4), praw[:, t, 0:T], praw[:, t, 1:T + 1], ALU.subtract).then_inc(S("diff"), 1)
                    dve.wait_ge(S("diff"), t + 1)
                    v.scalar_tensor_tensor(out=M[:, t, :], in0=XT(13 + t % 4), scalar=par_col("mu", t),
                                           in1=praw[:, t, 1:T + 1], op0=ALU.mult, op1=ALU.add).then_inc(S("mixed"), 1)


        SG, LC = XT(13, 4), XT(17, 4)
        AA, TH = XT(21, 4), XT(25)
        PP = X[:, 26 * T:26 * T + 4 * NCH * 65].rearrange("p (c j t) -> p c j t", c=4, j=NCH)
        PI = XT(31, 4)
        KK, TMP = XT(35, 4), XT(39, 4)
        AR = BR[:, 0:8, :].rearrange("p a t -> p (a t)").rearrange("p (c q x t) -> p c q x t", c=4, q=4, x=2)
        BT, KT = BR[:, 8:12, :], BR[:, 12:16, :]
        S, other = stage()
        with nc.Block() as block:
            @block.sync
            def _(sp):
                clear(sp, other)

            @block.tensor
            def _(pe):
                w2a2 = par[:, PCOL["w2a2"]:PCOL["w2a2"] + 512]
                pe.wait_ge(S("tanh"), 1)
                for c in range(4):
                    nc.tensor.matmul(PS[:, c, :], w2a2[0:64, c * P:(c + 1) * P], TH[0:64, :], start=True, stop=True).then_inc(S("lora"), 1)
                for c in range(4):
                    nc.tensor.matmul(PS[:, 4 + c, :], w2a2[64:128, c * P:(c + 1) * P], M[64:128, 12, :], start=True, stop=True).then_inc(S("lora"), 1)
                for c in range(4):
                    pe.wait_ge(S("ksq"), c + 1)
                    pe.wait_ge(S("gates"), 4)
                    nc.tensor.matmul(PS[:, c, :], C("head_ones", P), TMP[:, c, :], start=True, stop=True).then_inc(S("knorm2"), 1)
                for c in range(4):
                    pe.wait_ge(S("rkr"), c + 1)
                    pe.wait_ge(S("gates"), 8)
                    nc.tensor.matmul(PS[:, 4 + c, :], C("head_ones", P), TMP[:, c, :], start=True, stop=True).then_inc(S("bonus_sum"), 1)

            @block.scalar
            def _(act):
                a = nc.scalar
                a.activation(TH[0:64, :], M[0:64, 12, :], ACT.Tanh).then_inc(S("tanh"), 1)
                for c in range(4):
                    act.wait_ge(S("lora"), c + 1)
                    a.activation(SG[:, c, :], PS[:, c, :], ACT.Sigmoid, bias=par_col("w0", c)).then_inc(S("gates"), 1)
                for c in range(4):
                    act.wait_ge(S("lora"), 4 + c + 1)
                    a.activation(AA[:, c, :], PS[:, 4 + c, :], ACT.Sigmoid, bias=par_col("a0", c)).then_inc(S("gates"), 1)
                for c in range(4):
                    act.wait_ge(S("kraw"), c + 1)
                    a.activation(TMP[:, c, :], KK[:, c, :], ACT.Square).then_inc(S("ksq"), 1)
                for c in range(4):
                    act.wait_ge(S("kfloor"), c + 1)
                    a.activation(TMP[:, c, :], TMP[:, c, :], ACT.Ln).then_inc(S("klog"), 1)
                for c in range(4):
                    act.wait_ge(S("klog"), c + 1)
                    act.wait_ge(S("kmod"), c + 1)
                    a.activation(SG[:, c, :], TMP[:, c, :], ACT.Exp, scale=-0.5).then_inc(S("kinv"), 1)
                for c in range(4):
                    act.wait_ge(S("cum"), c + 1)
                    a.activation(PP[:, c, :, 1:65], LC[:, c, :].rearrange("p (j t) -> p j t", j=NCH), ACT.Exp, scale=-EXPH).then_inc(S("decays"), 1)
                    a.activation(PI[:, c, :], LC[:, c, :], ACT.Exp, scale=EXPH).then_inc(S("decays"), 1)

            @block.vector
            def _(dve):
                v = nc.vector
                v.memset(PP[:, :, :, 0:1], 1.0).then_inc(S("first_decay"), 1)
                for c in range(4):
                    v.tensor_scalar(KK[:, c, :], M[:, 4 + c, :], par_col("k_k", c), None, ALU.mult).then_inc(S("kraw"), 1)
                for c in range(4):
                    dve.wait_ge(S("gates"), c + 1)
                    v.tensor_tensor_scan(LC[:, c, :], C("reset", T), SG[:, c, :], 0.0, ALU.mult, ALU.add).then_inc(S("cum"), 1)
                for c in range(4):
                    dve.wait_ge(S("gates"), 4 + c + 1)
                    dve.wait_ge(S("cum"), c + 1)
                    v.tensor_scalar(SG[:, c, :], AA[:, c, :], par_col("k_a", c), oneless[:, c:c + 1], ALU.mult, ALU.add).then_inc(S("kscale"), 1)
                for c in range(4):
                    dve.wait_ge(S("kscale"), c + 1)
                    v.tensor_tensor(M[:, 4 + c, :], M[:, 4 + c, :], SG[:, c, :], ALU.mult).then_inc(S("kmod"), 1)
                for c in range(4):
                    dve.wait_ge(S("knorm2"), c + 1)
                    v.tensor_scalar(TMP[:, c, :], PS[:, c, :], 1e-24, None, ALU.max).then_inc(S("kfloor"), 1)
                for c in range(4):
                    dve.wait_ge(S("kinv"), c + 1)
                    v.tensor_tensor(KK[:, c, :], KK[:, c, :], SG[:, c, :], ALU.mult).then_inc(S("kk"), 1)
                for c in range(4):
                    dve.wait_ge(S("kinv"), 4)
                    dve.wait_ge(S("kmod"), c + 1)
                    v.scalar_tensor_tensor(out=TMP[:, c, :], in0=M[:, c, :], scalar=par_col("r_k", c), in1=M[:, 4 + c, :],
                                           op0=ALU.mult, op1=ALU.mult).then_inc(S("rkr"), 1)
                for c in range(4):
                    dve.wait_ge(S("kk"), c + 1)
                    v.tensor_tensor(AA[:, c, :], AA[:, c, :], KK[:, c, :], ALU.mult).then_inc(S("b0"), 1)
                for c in range(4):
                    dve.wait_ge(S("decays"), 2 * c + 2)
                    dve.wait_ge(S("first_decay"), 1)
                    dve.wait_ge(S("b0"), c + 1)
                    for q in range(4):
                        before = PP[:, c, 2 * q:2 * q + 2, 0:64]
                        upto = PP[:, c, 2 * q:2 * q + 2, 1:65]
                        sl = slice(q * P, (q + 1) * P)
                        v.scalar_tensor_tensor(out=AR[:, c, q, 0, :].rearrange("p (j t) -> p j t", j=2),
                                               in0=KK[:, c, sl].rearrange("p (j t) -> p j t", j=2), scalar=-1.0,
                                               in1=before, op0=ALU.mult, op1=ALU.mult).then_inc(S("done"), 1)
                        v.tensor_tensor(AR[:, c, q, 1, :].rearrange("p (j t) -> p j t", j=2),
                                        M[:, c, sl].rearrange("p (j t) -> p j t", j=2), upto, ALU.mult).then_inc(S("done"), 1)
                    v.tensor_tensor(BT[:, c, :], AA[:, c, :], PI[:, c, :], ALU.mult).then_inc(S("done"), 1)
                    v.tensor_tensor(KT[:, c, :], M[:, 4 + c, :], PI[:, c, :], ALU.mult).then_inc(S("done"), 1)
                for c in range(4):
                    dve.wait_ge(S("bonus_sum"), c + 1)
                    dve.wait_ge(S("done"), 10 * (c + 1))
                    v.tensor_tensor(M[:, c, :], PS[:, 4 + c, :], M[:, 8 + c, :], ALU.mult).then_inc(S("bonus"), 1)


        BON = M[:, 0:4, :]
        VF = M[:, 8:12, :]
        TB, TK, TV = XT(12, 4), XT(16, 4), XT(4, 4)
        GB, GK = X[:, 20 * T:24 * T].rearrange("p (h x t) -> p h x t", h=8, x=2), X[:, 32 * T:36 * T].rearrange("p (h x t) -> p h x t", h=8, x=2)
        DT = X[:, 36 * T:38 * T].rearrange("p (h t) -> p h t", h=8)
        DD = X[:, 38 * T:40 * T].rearrange("p (h t) -> p h t", h=8)
        XX = X[:, 40 * T:42 * T].rearrange("p (h t) -> p h t", h=8)
        MK = X[:, 42 * T:44 * T].rearrange("p (h t) -> p h t", h=8)
        PC = X[:, 31 * T + 0:31 * T + 32].rearrange("p (c j) -> p c j", c=4)
        ST, SN, PCM = (XT(i).rearrange("p (c v) -> p c v", c=4) for i in (24, 30, 9))
        ZS, US = XT(25), XT(8)
        S, other = stage()
        with nc.Block() as block:
            @block.sync
            def _(sp):
                clear(sp, other)

            @block.tensor
            def _(pe):
                for i in range(12):
                    src = (BT, KT, VF)[i // 4]
                    if i >= 4:
                        pe.wait_ge(S("tok"), i - 3)
                    for c in range(4):
                        mm = nc.tensor.transpose(PS[:, i % 4, c * P:(c + 1) * P], src[:, c, (i % 4) * P:(i % 4 + 1) * P], ident)
                    mm.then_inc(S("turned"), 1)

            @block.scalar
            def _(act):
                for i in range(12):
                    act.wait_ge(S("turned"), i + 1)
                    dst = (TB, TK, TV)[i // 4]
                    nc.scalar.activation(dst[:, i % 4, :], PS[:, i % 4, :], ACT.Copy).then_inc(S("tok"), 1)

            @block.vector
            def _(dve):
                nc.vector.tensor_copy(PC, PP[:, :, :, 64]).then_inc(S("pc"), 1)
                nc.vector.memset(XT(24), 0.0).then_inc(S("pc"), 1)
                nc.vector.memset(ZS, 0.0).then_inc(S("pc"), 1)

        YY = XT(26, 4)
        for q in range(4):
            S, other = stage()
            GR = slice(q * P, (q + 1) * P)
            with nc.Block() as block:
                @block.sync
                def _(sp):
                    clear(sp, other)

                @block.tensor
                def _(pe):
                    for g in range(2):
                        for which, src in ((0, BT), (1, KT)):
                            for half in range(2):
                                i = 4 * g + 2 * which + half
                                if i >= 4:
                                    pe.wait_ge(S("masked"), i - 3)
                                for hh in range(2):
                                    h = 4 * g + 2 * hh + half
                                    c, b = h // 2, 64 * (h % 2)
                                    mm = nc.tensor.matmul(PS[:, i % 4, hh * 256:(hh + 1) * 256], src[b:b + 64, c, GR],
                                                          AR[b:b + 64, c, q, :, :], start=True, stop=True)
                                mm.then_inc(S("gram"), 1)
                    for g in range(2):
                        for hh in range(4):
                            h = 2 * hh + g
                            c, b = h // 2, 64 * (h % 2)
                            mm = nc.tensor.matmul(PS[:, 4 + g, hh * P:(hh + 1) * P], AR[b:b + 64, c, q, 0, :], BT[b:b + 64, c, GR], start=True, stop=True)
                        mm.then_inc(S("gramM"), 1)
                    for lv in range(1, 6):
                        for g in range(2):
                            i = 2 * (lv - 1) + g
                            pe.wait_ge(S("level_mask"), i + 1)
                            pe.wait_ge(S("inv"), i + 1)
                            pe.wait_ge(S("invT"), i + 1)
                            pe.wait_ge(S("masked"), 8)
                            for hh in range(4):
                                h = 2 * hh + g
                                mm = nc.tensor.matmul(PS[:, g, hh * P:(hh + 1) * P], MK[:, h, :], DD[:, h, :], start=True, stop=True)
                            mm.then_inc(S("md"), 1)
                        for g in range(2):
                            i = 2 * (lv - 1) + g
                            pe.wait_ge(S("x_out"), i + 1)
                            for hh in range(4):
                                h = 2 * hh + g
                                mm = nc.tensor.matmul(PS[:, 2 + g, hh * P:(hh + 1) * P], XX[:, h, :], DT[:, h, :], start=True, stop=True)
                            mm.then_inc(S("dxT"), 1)
                            if lv < 5:
                                for hh in range(4):
                                    h = 2 * hh + g
                                    mm = nc.tensor.matmul(PS[:, 4 + g, hh * P:(hh + 1) * P], DT[:, h, :], XX[:, h, :], start=True, stop=True)
                                mm.then_inc(S("dx"), 1)
                    for j in range(2):
                        b = 64 * j
                        tt = slice(b, b + 64)
                        R = slice(b, b + 64)
                        pe.wait_ge(S("invT"), 12)
                        if j:
                            pe.wait_ge(S("state"), 1)
                        for c in range(4):
                            pv = slice(c * P, (c + 1) * P)
                            nc.tensor.matmul(PS[R, 6, pv], AR[:, c, q, 0, tt], ST[:, c, :], start=True, stop=False)
                            for h in (2 * c, 2 * c + 1):
                                hv = slice(h * 64, (h + 1) * 64)
                                mm = nc.tensor.matmul(PS[R, 6, hv], GK[:, h, 0, tt], TV[:, q, hv], start=False, stop=(h % 2 == 1))
                        mm.then_inc(S("z"), 1)
                        pe.wait_ge(S("z_out"), j + 1)
                        for h in range(8):
                            hv = slice(h * 64, (h + 1) * 64)
                            mm = nc.tensor.matmul(PS[R, 7, hv], DT[:, h, tt], ZS[:, hv], start=True, stop=True)
                        mm.then_inc(S("u"), 1)
                        pe.wait_ge(S("u_out"), j + 1)
                        if j:
                            pe.wait_ge(S("y_out"), 1)
                        for c in range(4):
                            pv = slice(c * P, (c + 1) * P)
                            nc.tensor.matmul(PS[:, 0, pv], TB[R, q, pv], US[R, pv], start=True, stop=False)
                            mm = nc.tensor.matmul(PS[:, 0, pv], TK[R, q, pv], TV[R, q, pv], start=False, stop=True)
                        mm.then_inc(S("s_new"), 1)
                        for c in range(4):
                            nc.tensor.matmul(PS[:, 1, c * 64:(c + 1) * 64], ST[:, c, :], AR[:, c, q, 1, tt], start=True, stop=False)
                            for h in (2 * c, 2 * c + 1):
                                hb = 64 * (h % 2)
                                hv = slice(h * 64, (h + 1) * 64)
                                o = PS[hb:hb + 64, 1, c * 64:(c + 1) * 64]
                                nc.tensor.matmul(o, US[:, hv], GB[:, h, 1, tt], start=False, stop=False)
                                mm = nc.tensor.matmul(o, TV[:, q, hv], GK[:, h, 1, tt], start=False, stop=True)
                        mm.then_inc(S("y"), 1)

                @block.scalar
                def _(act):
                    for lv in range(1, 6):
                        for g in range(2):
                            i = 2 * (lv - 1) + g
                            act.wait_ge(S("md"), i + 1)
                            if lv > 1:
                                act.wait_ge(S("dxT"), i - 1)
                                act.wait_ge(S("dx"), i - 1)
                            nc.scalar.activation(XX[:, g::2, :], PS[:, g, :].rearrange("p (h t) -> p h t", h=4), ACT.Copy).then_inc(S("x_out"), 1)
                    for j in range(2):
                        R = slice(64 * j, 64 * j + 64)
                        act.wait_ge(S("y"), j + 1)
                        nc.scalar.activation(YY[:, :, q * P + 64 * j:q * P + 64 * j + 64],
                                             PS[:, 1, 0:256].rearrange("p (c t) -> p c t", c=4), ACT.Copy).then_inc(S("y_out"), 1)

                @block.vector
                def _(dve):
                    v = nc.vector
                    tri = C("tri", 256)[:, None, :].to_broadcast([P, 2, 256])

                    def level(k):
                        return C("lev", P, k * P)[:, None, :].to_broadcast([P, 4, P])

                    for g in range(2):
                        for which, dst in ((0, GB), (1, GK)):
                            for half in range(2):
                                i = 4 * g + 2 * which + half
                                h = 4 * g + half
                                dve.wait_ge(S("gram"), i + 1)
                                v.tensor_tensor(dst[:, h:h + 3:2, :, :].rearrange("p h x t -> p h (x t)"),
                                                PS[:, i % 4, :].rearrange("p (h x) -> p h x", h=2), tri, ALU.mult).then_inc(S("masked"), 1)
                    if q == 0:
                        v.memset(US, 0.0).then_inc(S("u_zero"), 1)
                        dve.wait_ge(S("u_zero"), 1)
                    idb = ident[:, None, :].to_broadcast([P, 4, P])
                    for g in range(2):
                        hs = slice(g, 8, 2)
                        dve.wait_ge(S("gramM"), g + 1)
                        dve.wait_ge(S("masked"), 5 + g)
                        v.tensor_tensor(DD[:, hs, :], PS[:, 4 + g, :].rearrange("p (h t) -> p h t", h=4), C("m0", P)[:, None, :].to_broadcast([P, 4, P]), ALU.mult).then_inc(S("d_low"), 1)
                        v.tensor_tensor(DT[:, hs, :], GB[:, hs, 0, :], level(0), ALU.mult).then_inc(S("dT_low"), 1)
                        v.tensor_tensor(MK[:, hs, :], GB[:, hs, 0, :], level(1), ALU.mult).then_inc(S("level_mask"), 1)
                        dve.wait_ge(S("dT_low"), g + 1)
                        v.tensor_tensor(DD[:, hs, :], DD[:, hs, :], idb, ALU.add).then_inc(S("inv"), 1)
                        v.tensor_tensor(DT[:, hs, :], DT[:, hs, :], idb, ALU.add).then_inc(S("invT"), 1)
                    for lv in range(1, 6):
                        if lv < 5:
                            for g in range(2):
                                i = 2 * (lv - 1) + g
                                hs = slice(g, 8, 2)
                                dve.wait_ge(S("md"), i + 1)
                                v.tensor_tensor(MK[:, hs, :], GB[:, hs, 0, :], level(lv + 1), ALU.mult).then_inc(S("level_mask"), 1)
                        for g in range(2):
                            i = 2 * (lv - 1) + g
                            hs = slice(g, 8, 2)
                            dve.wait_ge(S("dxT"), i + 1)
                            if lv < 5:
                                dve.wait_ge(S("dx"), i + 1)
                            v.tensor_tensor(DT[:, hs, :], DT[:, hs, :], PS[:, 2 + g, :].rearrange("p (h t) -> p h t", h=4), ALU.add).then_inc(S("invT"), 1)
                            if lv < 5:
                                v.tensor_tensor(DD[:, hs, :], DD[:, hs, :], PS[:, 4 + g, :].rearrange("p (h t) -> p h t", h=4), ALU.add).then_inc(S("inv"), 1)
                    for j in range(2):
                        R = slice(64 * j, 64 * j + 64)
                        dve.wait_ge(S("z"), j + 1)
                        if j:
                            dve.wait_ge(S("state"), 1)
                        v.tensor_copy(ZS[R, :], PS[R, 6, :]).then_inc(S("z_out"), 1)
                        dve.wait_ge(S("u"), j + 1)
                        v.tensor_copy(US[R, :], PS[R, 7, :]).then_inc(S("u_out"), 1)
                        v.tensor_tensor(PCM, C("head_ones", P)[:, None, :].to_broadcast([P, 4, P]),
                                        PC[:, :, 2 * q + j:2 * q + j + 1].to_broadcast([P, 4, P]), ALU.mult).then_inc(S("decay_mask"), 1)
                        dve.wait_ge(S("s_new"), j + 1)
                        v.tensor_tensor(SN, PS[:, 0, :].rearrange("p (c v) -> p c v", c=4), ST, ALU.add).then_inc(S("s_sum"), 1)
                        dve.wait_ge(S("s_sum"), j + 1)
                        dve.wait_ge(S("y"), j + 1)
                        dve.wait_ge(S("decay_mask"), j + 1)
                        v.tensor_tensor(ST, SN, PCM, ALU.mult).then_inc(S("state"), 1)


        Y0, SQ, RV = XT(30, 4), XT(34, 4), XT(38, 4)
        S, other = stage()
        with nc.Block() as block:
            @block.sync
            def _(sp):
                clear(sp, other)

            @block.tensor
            def _(pe):
                for c in range(4):
                    nc.tensor.matmul(PS[:, c, :], C("head_ones", P), YY[:, c, :], start=True, stop=True).then_inc(S("sum"), 1)
                for c in range(4):
                    pe.wait_ge(S("sq"), c + 1)
                    nc.tensor.matmul(PS[:, 4 + c, :], C("head_ones", P), SQ[:, c, :], start=True, stop=True).then_inc(S("sumsq"), 1)

            @block.scalar
            def _(act):
                for c in range(4):
                    act.wait_ge(S("centred"), c + 1)
                    nc.scalar.activation(SQ[:, c, :], Y0[:, c, :], ACT.Square).then_inc(S("sq"), 1)
                for c in range(4):
                    act.wait_ge(S("sumsq"), c + 1)
                    nc.scalar.activation(SQ[:, c, :], PS[:, 4 + c, :], ACT.Ln, scale=1.0 / HD, bias=C("eps", 1, 0)).then_inc(S("log"), 1)
                for c in range(4):
                    act.wait_ge(S("log"), c + 1)
                    nc.scalar.activation(RV[:, c, :], SQ[:, c, :], ACT.Exp, scale=-0.5).then_inc(S("rstd"), 1)
                for c in range(4):
                    act.wait_ge(S("normed"), c + 1)
                    nc.scalar.activation(YY[:, c, :], Y0[:, c, :], ACT.Identity, scale=par_col("lnx_g", c), bias=par_col("lnx_b", c)).then_inc(S("affine"), 1)

            @block.vector
            def _(dve):
                v = nc.vector
                for c in range(4):
                    dve.wait_ge(S("sum"), c + 1)
                    v.scalar_tensor_tensor(out=Y0[:, c, :], in0=PS[:, c, :], scalar=-1.0 / HD, in1=YY[:, c, :], op0=ALU.mult, op1=ALU.add).then_inc(S("centred"), 1)
                for c in range(4):
                    dve.wait_ge(S("rstd"), c + 1)
                    v.tensor_tensor(Y0[:, c, :], Y0[:, c, :], RV[:, c, :], ALU.mult).then_inc(S("normed"), 1)
                for c in range(4):
                    dve.wait_ge(S("affine"), c + 1)
                    v.tensor_tensor(BR[:, c, :], YY[:, c, :], BON[:, c, :], ALU.add).then_inc(S("branch"), 1)


        n0 = FIRST["mla"]
        QL, QN = XT(0, 5), XT(5, 5)
        SQ, KP, RST = XT(10, 5), XT(15), XT(16, 2)
        KPR, ROT = XT(18), XT(19, 2)
        QH, KH, VV = XT(24, 8), XT(32, 8), XT(40, 4)
        pe_rows = slice(64, 96)
        S, other = stage()
        with nc.Block() as block:
            @block.sync
            def _(sp):
                clear(sp, other)
                stream.send(sp, n0 + 11 + RING - 1)

            @block.tensor
            def _(pe):
                for t in range(5):
                    gemm3(pe, t, n0 + t, XH, XL, S("latent"))
                gemm3(pe, 5, n0 + 5, XH, XL, S("latent"))
                pe.wait_ge(S("kpe"), 1)
                nc.tensor.matmul(PS[64:96, 6, :], cst[64:96, CCOL["swap"]:CCOL["swap"] + 32], KP[pe_rows, :], start=True, stop=True).then_inc(S("swapped"), 1)
                for t in range(5):
                    pe.wait_ge(S("sq"), t + 1)
                    pe.wait_ge(S("evicted"), t + 1)
                    bank = 0 if t < 3 else 1
                    mm = nc.tensor.matmul(PS[:, bank, :], C("ones", P), SQ[:, t, :], start=t in (0, 3), stop=t in (2, 4))
                    if t in (2, 4):
                        mm.then_inc(S("sumsq"), 1)
                pe.wait_ge(S("normed"), 5)
                for h in range(8):
                    n = n0 + 6 + h // 3
                    if h % 3 == 0:
                        stream.wait(pe, n)
                    if h >= 2:
                        pe.wait_ge(S("q_out"), h - 1)
                    for k in range(3):
                        mm = nc.tensor.matmul(PS[0:96, 2 + h % 2, :], stream.chunk(n)[:, (h % 3) * 288 + k * 96:(h % 3) * 288 + (k + 1) * 96],
                                              QN[:, k, :], start=(k == 0), stop=(k == 2))
                        if h % 3 == 0 and k == 0:
                            mm.then_inc(used, 1)
                    mm.then_inc(S("q"), 1)
                for h in range(8):
                    pe.wait_ge(S("q_out"), h + 1)
                    if h >= 2:
                        pe.wait_ge(S("q_rot"), h - 1)
                    nc.tensor.matmul(PS[pe_rows, 6 + h % 2, :], cst[64:96, CCOL["swap"]:CCOL["swap"] + 32], QH[pe_rows, h, :],
                                     start=True, stop=True).then_inc(S("q_swapped"), 1)
                n = n0 + 9
                stream.wait(pe, n)
                for h in range(8):
                    pe.wait_ge(S("k_out"), h - 1) if h >= 2 else None
                    for k in range(2):
                        mm = nc.tensor.matmul(PS[0:64, 4 + h % 2, :], stream.chunk(n)[:, h * 128 + k * 64:h * 128 + (k + 1) * 64],
                                              QN[:, 3 + k, :], start=(k == 0), stop=(k == 1))
                        if h == 0 and k == 0:
                            mm.then_inc(used, 1)
                    mm.then_inc(S("k"), 1)
                n = n0 + 10
                stream.wait(pe, n)
                pe.wait_ge(S("rms"), 2)
                for q in range(4):
                    if q >= 2:
                        pe.wait_ge(S("v_out"), q - 1)
                    for k in range(2):
                        mm = nc.tensor.matmul(PS[:, q % 2, :], QN[:, 3 + k, q * P:(q + 1) * P], stream.chunk(n)[:, k * 512:(k + 1) * 512],
                                              start=(k == 0), stop=(k == 1))
                        if q == 0 and k == 0:
                            mm.then_inc(used, 1)
                    mm.then_inc(S("v"), 1)

            @block.scalar
            def _(act):
                a = nc.scalar
                stream.hi(nc, act, n0 + PARTS)
                for t in range(5):
                    act.wait_ge(S("latent"), t + 1)
                    a.activation(QL[:, t, :], PS[:, t, :], ACT.Copy).then_inc(S("evicted"), 1)
                    a.activation(SQ[:, t, :], PS[:, t, :], ACT.Square).then_inc(S("sq"), 1)
                    stream.hi(nc, act, n0 + min(t + 3, 6))
                act.wait_ge(S("latent"), 6)
                a.activation(KP[pe_rows, :], PS[pe_rows, 5, :], ACT.Copy).then_inc(S("kpe"), 1)
                for i, width in enumerate((384, 256)):
                    act.wait_ge(S("sumsq"), i + 1)
                    a.activation(RST[:, i, :], PS[:, i, :], ACT.Ln, scale=1.0 / width, bias=C("eps", 1, 1)).then_inc(S("log"), 1)
                for i in range(2):
                    act.wait_ge(S("log"), i + 1)
                    a.activation(RST[:, i, :], RST[:, i, :], ACT.Exp, scale=-0.5).then_inc(S("rms"), 1)
                for h in range(8):
                    act.wait_ge(S("q"), h + 1)
                    a.activation(QH[0:96, h, :], PS[0:96, 2 + h % 2, :], ACT.Copy).then_inc(S("q_out"), 1)
                for h in range(8):
                    act.wait_ge(S("k"), h + 1)
                    a.activation(KH[0:64, h, :], PS[0:64, 4 + h % 2, :], ACT.Copy).then_inc(S("k_out"), 1)
                for q in range(4):
                    act.wait_ge(S("v"), q + 1)
                    a.activation(VV[:, q, :], PS[:, q % 2, :], ACT.Copy).then_inc(S("v_out"), 1)
                stream.hi(nc, act, n0 + 11 + 1)

            @block.vector
            def _(dve):
                v = nc.vector
                cos, sin = rope[pe_rows, 0, :], rope[pe_rows, 1, :]
                dve.wait_ge(S("kpe"), 1)
                v.tensor_tensor(KPR[pe_rows, :], KP[pe_rows, :], cos, ALU.mult).then_inc(S("kp_cos"), 1)
                dve.wait_ge(S("swapped"), 1)
                v.tensor_tensor(ROT[pe_rows, 0, :], PS[pe_rows, 6, :], sin, ALU.mult).then_inc(S("kp_sin"), 1)
                dve.wait_ge(S("kp_sin"), 1)
                v.tensor_tensor(KPR[pe_rows, :], KPR[pe_rows, :], ROT[pe_rows, 0, :], ALU.add).then_inc(S("kp_rot"), 1)
                for t in range(5):
                    dve.wait_ge(S("rms"), 1 if t < 3 else 2)
                    dve.wait_ge(S("evicted"), t + 1)
                    v.scalar_tensor_tensor(out=QN[:, t, :], in0=QL[:, t, :], scalar=par_col("q_norm", t), in1=RST[:, 0 if t < 3 else 1, :],
                                           op0=ALU.mult, op1=ALU.mult).then_inc(S("normed"), 1)
                dve.wait_ge(S("kp_rot"), 1)
                for h in range(8):
                    i = h % 2
                    dve.wait_ge(S("q_swapped"), h + 1)
                    if h >= 2:
                        dve.wait_ge(S("q_done"), h - 1)
                    v.tensor_tensor(ROT[pe_rows, i, :], PS[pe_rows, 6 + i, :], sin, ALU.mult).then_inc(S("q_rot"), 1)
                    v.tensor_tensor(QH[pe_rows, h, :], QH[pe_rows, h, :], cos, ALU.mult).then_inc(S("q_cos"), 1)
                    dve.wait_ge(S("q_cos"), h + 1)
                    v.tensor_tensor(QH[pe_rows, h, :], QH[pe_rows, h, :], ROT[pe_rows, i, :], ALU.add).then_inc(S("q_done"), 1)

            @block.gpsimd
            def _(pool):
                stream.lo(nc, pool, n0 + 6)
                pool.wait_ge(S("kp_rot"), 1)
                for h in range(8):
                    nc.gpsimd.tensor_copy(KH[pe_rows, h, :], KPR[pe_rows, :]).then_inc(S("kp_copied"), 1)
                pool.wait_ge(S("kp_copied"), 8)
                stream.lo(nc, pool, n0 + 11 + 1)

        attention(nc, stage, PS, ident, C("causal", P), heads=8, dv=64, rows=96, blocks=4,
                  query=lambda h: QH[0:96, h, :], key=lambda h: KH[0:96, h, :],
                  value=lambda h, kb: VV[:, kb, h * 64:(h + 1) * 64], nkeys=[128, 256, 384, 512],
                  scale=96.0 ** -0.5, out=lambda h: BR[64 * (h % 2):64 * (h % 2) + 64, 4 + h // 2, :],
                  probs=[XT(0), XT(1), XT(2)], probsT=[XT(4, 4), XT(8, 4)], small=XT(14), part=lambda h: 64 * (h % 2))

        n0, nx, ng = FIRST["conv"], FIRST["xattn"], FIRST["gates"]
        H0 = X[:, 0:4 * (T + TAPS - 1)].rearrange("p (c t) -> p c t", c=4)
        SGM, ACC, Y0, SQ, RST = XT(5, 4), XT(9, 4), XT(13, 4), XT(17, 4), XT(21)
        QX, KX, VX = XT(22, 4), X[:, 26 * T:28 * T].rearrange("p (h t) -> p h t", h=4), XT(28, 2)
        GNOW, GLATER = XT(30, 4), XT(34, 8)
        S, other = stage()
        with nc.Block() as block:
            @block.sync
            def _(sp):
                clear(sp, other)
                stream.send(sp, ng + 16 + RING - 1)

            @block.tensor
            def _(pe):
                for t in range(8):
                    gemm3(pe, t, n0 + t, XH, XL, S("u"))
                for t in range(8):
                    if t < 4:
                        pe.wait_ge(S("gate"), t + 1)
                    else:
                        pe.wait_ge(S("evicted"), t - 3)
                    if t < 4:
                        gemm3(pe, 4 + t % 4, nx + t, XH, XL, S("product"))
                    else:
                        gemm(pe, 4 + t % 4, nx + t, memT[:, :, :], S("product"))
                pe.wait_ge(S("glu"), 4)
                for kc in range(4):
                    n = nx + 8 + kc
                    stream.wait(pe, n)
                    for q in range(2):
                        for k in range(2):
                            mm = nc.tensor.matmul(PS[:, 2 + q, :], memT[:, 2 * kc + k, q * P:(q + 1) * P], stream.chunk(n)[:, k * 512:(k + 1) * 512],
                                                  start=(kc == 0 and k == 0), stop=(kc == 3 and k == 1))
                            if q == 0 and k == 0:
                                mm.then_inc(used, 1)
                        if kc == 3:
                            mm.then_inc(S("product"), 1)
                for t in range(16):
                    if t < 4:
                        pe.wait_ge(S("evicted"), 5 + t)
                    else:
                        pe.wait_ge(S("silu"), t - 3)
                    gemm3(pe, 4 + t % 4, ng + t, XH, XL, S("gate_product"))
                for c in range(4):
                    pe.wait_ge(S("conv"), c + 1)
                    mm = nc.tensor.matmul(PS[:, 0, :], C("ones", P), ACC[:, c, :], start=(c == 0), stop=(c == 3))
                mm.then_inc(S("sum"), 1)
                for c in range(4):
                    pe.wait_ge(S("sq"), c + 1)
                    mm = nc.tensor.matmul(PS[:, 1, :], C("ones", P), SQ[:, c, :], start=(c == 0), stop=(c == 3))
                mm.then_inc(S("sumsq"), 1)

            @block.scalar
            def _(act):
                a = nc.scalar
                stream.hi(nc, act, n0 + 7)
                for c in range(4):
                    act.wait_ge(S("u"), 4 + c + 1)
                    a.activation(SGM[:, c, :], PS[:, 4 + c, :], ACT.Sigmoid).then_inc(S("gate"), 1)
                    stream.hi(nc, act, n0 + 8 + c)
                for t in range(10):
                    if t < 2:
                        stream.hi(nc, act, n0 + 11 + t)
                    if t == 9:
                        stream.hi(nc, act, ng + 1)
                    act.wait_ge(S("product"), t + 1)
                    dst, src = ((QX[:, t, :], PS[:, 4 + t % 4, :]) if t < 4 else (KX[:, t - 4, :], PS[:, 4 + t % 4, 0:MEM]) if t < 8
                                else (VX[:, t - 8, :], PS[:, 2 + t - 8, :]))
                    a.activation(dst, src, ACT.Copy).then_inc(S("evicted"), 1)
                stream.hi(nc, act, ng + 2)
                for t in range(16):
                    act.wait_ge(S("gate_product"), t + 1)
                    if 4 <= t < 8:
                        act.wait_ge(S("gated"), t - 3)
                    a.activation(GNOW[:, t % 4, :] if t < 8 else GLATER[:, t - 8, :], PS[:, 4 + t % 4, :], ACT.Silu).then_inc(S("silu"), 1)
                    stream.hi(nc, act, ng + min(t + 3, 16 + 1))
                for c in range(4):
                    act.wait_ge(S("centred"), c + 1)
                    a.activation(SQ[:, c, :], Y0[:, c, :], ACT.Square).then_inc(S("sq"), 1)
                act.wait_ge(S("sumsq"), 1)
                a.activation(RST, PS[:, 1, :], ACT.Ln, scale=1.0 / W, bias=C("eps", 1, 2)).then_inc(S("log"), 1)
                act.wait_ge(S("log"), 1)
                a.activation(RST, RST, ACT.Exp, scale=-0.5).then_inc(S("rstd"), 1)
                for c in range(4):
                    act.wait_ge(S("normed"), c + 1)
                    a.activation(BR[:, 8 + c, :], Y0[:, c, :], ACT.Silu, scale=par_col("cln_g", c), bias=par_col("cln_b", c)).then_inc(S("branch"), 1)

            @block.vector
            def _(dve):
                v = nc.vector
                v.memset(H0[:, :, 0:TAPS - 1], 0.0).then_inc(S("pad"), 1)
                for c in range(4):
                    dve.wait_ge(S("gate"), c + 1)
                    v.tensor_tensor(H0[:, c, TAPS - 1:], PS[:, c, :], SGM[:, c, :], ALU.mult).then_inc(S("glu"), 1)
                dve.wait_ge(S("pad"), 1)
                dve.wait_ge(S("glu"), 4)
                for tap in range(TAPS):
                    for c in range(4):
                        w = par_col("conv_w", c * TAPS + tap)
                        if tap == 0:
                            ins = v.tensor_scalar(ACC[:, c, :], H0[:, c, 0:T], w, par_col("conv_b", c), ALU.mult, ALU.add)
                        else:
                            dve.wait_ge(S("tap"), 4 * (tap - 1) + c + 1)
                            ins = v.scalar_tensor_tensor(out=ACC[:, c, :], in0=H0[:, c, tap:tap + T], scalar=w, in1=ACC[:, c, :],
                                                         op0=ALU.mult, op1=ALU.add)
                        ins.then_inc(S("conv") if tap == TAPS - 1 else S("tap"), 1)
                dve.wait_ge(S("sum"), 1)
                dve.wait_ge(S("conv"), 4)
                for c in range(4):
                    v.scalar_tensor_tensor(out=Y0[:, c, :], in0=PS[:, 0, :], scalar=-1.0 / W, in1=ACC[:, c, :], op0=ALU.mult, op1=ALU.add).then_inc(S("centred"), 1)
                dve.wait_ge(S("rstd"), 1)
                dve.wait_ge(S("centred"), 4)
                for c in range(4):
                    dve.wait_ge(S("sq"), c + 1)
                    v.tensor_tensor(Y0[:, c, :], Y0[:, c, :], RST, ALU.mult).then_inc(S("normed"), 1)

            @block.gpsimd
            def _(pool):
                stream.lo(nc, pool, ng + 2)
                for t in range(16):
                    if t < 8:
                        pool.wait_ge(S("silu"), t + 1)
                        nc.gpsimd.tensor_tensor(BR[:, t, :], BR[:, t, :], GNOW[:, t % 4, :], ALU.mult).then_inc(S("gated"), 1)
                    stream.lo(nc, pool, ng + min(t + 3, 16 + 1))

        attention(nc, stage, PS, ident, None, heads=4, dv=128, rows=128, blocks=4,
                  query=lambda h: QX[:, h, :], key=lambda h: KX[:, h, :],
                  value=lambda h, kb: VX[:, kb, h * P:(h + 1) * P], nkeys=[256] * 4,
                  scale=128.0 ** -0.5, out=lambda h: BR[:, 12 + h, :],
                  probs=[XT(0), XT(1), XT(2)], probsT=[XT(4, 4), XT(8, 4)], small=XT(14), part=lambda h: 0)

        n0 = FIRST["merge"]
        MG = XT(12, 8)

        def gate_chunk(i):
            return n0 + 6 * (i // 4) + 3 * (i % 4 // 2) + 1 + i % 2
        AD = X[:, 4 * T:4 * T + 96].rearrange("p (m c) -> p m c", c=2)
        CB = X[:, 30 * T:34 * T].rearrange("p (c k) -> p c k", c=2)
        PROD = X[:, 28 * T:30 * T]

        def rows_of(t):
            return X[:, (20 + 2 * (t % 4)) * T:(22 + 2 * (t % 4)) * T]

        S, other = stage()
        with nc.Block() as block:
            @block.sync
            def _(sp):
                clear(sp, other)
                for c in range(2):
                    sp.dma_start(CB[:, c, :], A["cond"][c].partition_broadcast(P)).then_inc(S("cond"), 16)
                for t in range(48):
                    stream.send(sp, n0 + t + RING)
                    if t >= 4:
                        sp.wait_ge(S("ada"), 2 * (t - 3))
                    sp.dma_start(rows_of(t), A["ada"][bass.ds(layer, 1), t, :, :].rearrange("l p c -> p (l c)")).then_inc(S(f"rows{t % 4}"), 16)

            @block.tensor
            def _(pe):
                for m in range(8):
                    for n in range(4):
                        i = 4 * m + n
                        o = n0 + 6 * m + 3 * (n // 2)
                        if i >= 4:
                            pe.wait_ge(S("weighted"), i - 3)
                        if n % 2 == 0:
                            stream.wait(pe, o)
                        bank = 4 + i % 4
                        if n % 2 == 0:
                            for nn in (n, n + 1):
                                if 4 * m + nn >= 4:
                                    pe.wait_ge(S("weighted"), 4 * m + nn - 3)
                                if m == 0 and nn >= 2:
                                    pe.wait_ge(S("gated"), 4 * (nn - 1))
                                for k in range(4):
                                    mm = nc.tensor.matmul(PS[:, 4 + (4 * m + nn) % 4, :], stream.chunk(o)[:, (nn % 2) * 512 + k * P:(nn % 2) * 512 + (k + 1) * P],
                                                          BR[:, 4 * nn + k, :], start=(k == 0), stop=(k == 3))
                                    if nn == n and k == 0:
                                        mm.then_inc(used, 1)
                                mm.then_inc(S("product"), 1)
                        if i >= 4:
                            pe.wait_ge(S("gate"), i - 3)
                        gemm3(pe, i % 4, gate_chunk(i), XH, XL, S("gate_product"))

            @block.scalar
            def _(act):
                stream.hi(nc, act, gate_chunk(1) + 1)
                act.wait_ge(S("cond"), 32)
                nc.scalar.activation(CB, CB, ACT.Silu).then_inc(S("silu_c"), 1)
                for i in range(32):
                    act.wait_ge(S("gate_product"), i + 1)
                    if i >= 4:
                        act.wait_ge(S("weighted"), i - 3)
                    nc.scalar.activation(XT(i % 4), PS[:, i % 4, :], ACT.Sigmoid, bias=par_col("b_gate", 8 * (i % 4) + i // 4)).then_inc(S("gate"), 1)
                    stream.hi(nc, act, min(gate_chunk(i + 2) + 1, n0 + 48))

            @block.vector
            def _(dve):
                v = nc.vector
                for i in range(32):
                    m, n = i // 4, i % 4
                    dve.wait_ge(S("gate"), i + 1)
                    dve.wait_ge(S("product"), i + 1)
                    dst = MG[:, m, :] if n == 0 else XT(8 + i % 4)
                    if i >= 4 and n:
                        dve.wait_ge(S("merged"), 3 * m - 3 + n)
                    v.tensor_tensor(dst, PS[:, 4 + i % 4, :], XT(i % 4), ALU.mult).then_inc(S("weighted"), 1)
                    if n:
                        dve.wait_ge(S("weighted"), i + 1)
                        if n > 1:
                            dve.wait_ge(S("merged"), 3 * m + n - 1)
                        v.tensor_tensor(MG[:, m, :], MG[:, m, :], XT(8 + i % 4), ALU.add).then_inc(S("merged"), 1)
                    if i == 0:
                        dve.wait_ge(S("silu_c"), 1)
                    for t in range(48 * i // 32, 48 * (i + 1) // 32):
                        dve.wait_ge(S(f"rows{t % 4}"), 16 * (t // 4 + 1))
                        for c in range(2):
                            if 2 * t + c:
                                dve.wait_ge(S("ada"), 2 * t + c)
                            v.tensor_tensor_reduce(PROD, rows_of(t), CB[:, c, :], 1.0, 0.0, ALU.mult, ALU.add, AD[:, t, c:c + 1]).then_inc(S("ada"), 1)
                dve.wait_ge(S("ada"), 96)
                v.tensor_copy(mods[:, bass.ds(layer, 1), :].rearrange("p l m -> p (l m)"), X[:, 4 * T:4 * T + 96]).then_inc(S("mods"), 1)

            @block.gpsimd
            def _(pool):
                stream.lo(nc, pool, gate_chunk(1) + 1)
                for t in range(8):
                    nc.gpsimd.tensor_tensor(BR[:, 8 + t, :], BR[:, 8 + t, :], GLATER[:, t, :], ALU.mult).then_inc(S("gated"), 1)
                    if t == 3:
                        stream.lo(nc, pool, gate_chunk(2) + 1)
                stream.lo(nc, pool, n0 + 48)

        n0 = FIRST["out"]
        RR, SQ, RST = XT(0, 8), XT(8, 8), XT(16)
        S, other = stage()
        with nc.Block() as block:
            @block.sync
            def _(sp):
                clear(sp, other)
                stream.send(sp, n0 + 8)

            @block.tensor
            def _(pe):
                for t in range(8):
                    if t >= 4:
                        pe.wait_ge(S("residual"), t - 3)
                    gemm(pe, t % 4, n0 + t, MG, S("product"))
                for t in range(8):
                    pe.wait_ge(S("residual"), t + 1)
                    mm = nc.tensor.matmul(PS[:, 4, :], C("ones", P), RR[:, t, :], start=(t == 0), stop=(t == 7))
                mm.then_inc(S("sum"), 1)
                for t in range(8):
                    pe.wait_ge(S("sq"), t + 1)
                    mm = nc.tensor.matmul(PS[:, 5, :], C("ones", P), SQ[:, t, :], start=(t == 0), stop=(t == 7))
                mm.then_inc(S("sumsq"), 1)

            @block.scalar
            def _(act):
                a = nc.scalar
                for t in range(8):
                    act.wait_ge(S("centred"), t + 1)
                    a.activation(SQ[:, t, :], RR[:, t, :], ACT.Square).then_inc(S("sq"), 1)
                act.wait_ge(S("sumsq"), 1)
                a.activation(RST, PS[:, 5, :], ACT.Ln, scale=1.0 / D, bias=C("eps", 1, 2)).then_inc(S("log"), 1)
                act.wait_ge(S("log"), 1)
                a.activation(RST, RST, ACT.Exp, scale=-0.5).then_inc(S("rstd"), 1)
                for t in range(8):
                    act.wait_ge(S("normed"), t + 1)
                    a.activation(SQ[:, t, :], RR[:, t, :], ACT.Identity, scale=par_col("ln_g", t), bias=par_col("ln_b", t)).then_inc(S("x_new"), 1)

            @block.gpsimd
            def _(pool):
                for t in range(8):
                    pool.wait_ge(S("x_high"), t + 1)
                    nc.gpsimd.tensor_tensor(XL[:, t, :], SQ[:, t, :], xh[:, t, :], ALU.subtract).then_inc(S("x_low"), 1)

            @block.vector
            def _(dve):
                v = nc.vector
                for t in range(8):
                    dve.wait_ge(S("product"), t + 1)
                    v.scalar_tensor_tensor(out=RR[:, t, :], in0=xh[:, t, :], scalar=DEEP_ALPHA, in1=PS[:, t % 4, :], op0=ALU.mult, op1=ALU.add).then_inc(S("residual_high"), 1)
                    dve.wait_ge(S("residual_high"), t + 1)
                    v.scalar_tensor_tensor(out=RR[:, t, :], in0=XL[:, t, :].bitcast(F32), scalar=DEEP_ALPHA, in1=RR[:, t, :], op0=ALU.mult, op1=ALU.add).then_inc(S("residual"), 1)
                dve.wait_ge(S("sum"), 1)
                for t in range(8):
                    v.scalar_tensor_tensor(out=RR[:, t, :], in0=PS[:, 4, :], scalar=-1.0 / D, in1=RR[:, t, :], op0=ALU.mult, op1=ALU.add).then_inc(S("centred"), 1)
                dve.wait_ge(S("rstd"), 1)
                for t in range(8):
                    dve.wait_ge(S("sq"), t + 1)
                    v.tensor_tensor(RR[:, t, :], RR[:, t, :], RST, ALU.mult).then_inc(S("normed"), 1)
                for t in range(8):
                    dve.wait_ge(S("x_new"), t + 1)
                    v.tensor_copy(XH[:, t, :], SQ[:, t, :]).then_inc(S("x_high"), 1)

        S, other = stage()
        with nc.Block() as block:
            @block.sync
            def _(sp):
                clear(sp, other)
                clear(sp, WR[3])
                clear(sp, WR[4:])


CKV = CTX + T
FF = 2816
FT = FF // P
XB = T + 16
PCOL2 = {}
_at = 0
for _name, _n in (("g_mix", 8), ("g_ffn", 8), ("b_ada", 48), ("q_gain", 1), ("k_gain", 1), ("pool_scale", 2),
                  ("w_pool", 256), ("w_four", 256)):
    PCOL2[_name] = _at
    _at += _n
NPAR2 = _at
CCOL2 = {}
_at = 0
for _name, _n in (("ident", 128), ("head_ones", 128), ("ones", 128), ("swap", 128), ("cos", T), ("sin", T), ("cs64", 256),
                  ("count_x", 2 * T), ("count_c", 2 * CTX), ("eps", 1)):
    CCOL2[_name] = _at
    _at += _n
NCST2 = _at
FH = FT // 2
STAGE_CHUNKS2 = (("in", 11), ("out", 8), ("up0", 2 * FH), ("down0", FH), ("up1", 2 * FH), ("down1", FH))
FIRST2 = {}
_at = 0
for _name, _n in STAGE_CHUNKS2:
    FIRST2[_name] = _at
    _at += _n
NCHUNK2 = _at


def second(nc, ctx, A, PS, XH, XL, WR, mods, stage, stored):
    def sb(name, shape, dt=F32):
        return ctx.enter_context(nc.sbuf_tensor(name, shape, dt))

    cst = sb("cst2", [P, NCST2])
    par = sb("par2", [P, NPAR2])
    cT = sb("cT", [P, DK, CTX])
    mod = sb("mod", [P, 48, 2])
    gain = sb("gain", [P, 2, 8, 2])
    xT = sb("xT", [P, DK, T])

    def C(name, n=1, k=0):
        a = CCOL2[name] + k
        return cst[:, a:a + n]

    def par_col(name, k=0, n=1):
        a = PCOL2[name] + k
        return par[:, a:a + n]

    def tiles_of(X, i, n=1, w=T):
        a = X[:, i * T:i * T + n * w]
        return a if n == 1 else a.rearrange("p (n t) -> p n t", n=n)

    ident = C("ident", P)
    eps = C("eps")
    SH1, SC1, GA1, SH2, SC2, GA2 = (8 * i for i in range(6))

    S, other = stage()
    with nc.Block() as block:
        @block.sync
        def _(sp):
            clear(sp, other)
            sp.dma_start(cst[:, :], A["cst2"]).then_inc(S("in"), 16)
            sp.dma_start(cT[:, :, :].rearrange("p k t -> p (k t)"), A["ctxT"]).then_inc(S("in"), 16)
            sp.wait_ge(S("in"), 32)

        @block.vector
        def _(dve):
            for t in range(0, DK, 2):
                nc.vector.tensor_tensor(xT[:, t:t + 2, :], XH[:, t:t + 2, :].bitcast(F32), XL[:, t:t + 2, :].bitcast(F32), ALU.add).then_inc(S("x_whole"), 1)

    for layer in range(LAYERS):
        update = layer < LAYERS - 1
        stream = Stream(WR, lambda n: A["w2"][layer, n, :, :], list(range(NCHUNK2)))
        used = WR[4]
        room = ExitStack()
        mixed = room.enter_context(nc.sbuf_tensor(f"mixed{layer}", [P, 12 * T], F32))
        lower = ExitStack()
        Y = lower.enter_context(nc.sbuf_tensor(f"tiles{layer}", [P, 32 * T], F32))
        above = ExitStack()
        HC, HCL = (above.enter_context(nc.sbuf_tensor(f"context_{part}{layer}", [P, DK, CTX], F32R))[:, :, :] for part in ("high", "low"))

        def XT(i, n=1, w=T):
            return tiles_of(Y, i, n, w)

        streams = [dict(name="x", n=T, src=xT, h=XH, l=XL, k=0, bank=0), dict(name="c", n=CTX, src=cT, h=HC, l=HCL, k=1, bank=4)]

        def mark(n, first):
            return used if n and first else None

        def gemm(pe, n, outs):
            stream.wait_split(pe, n)
            for i, (ps, high, low, done) in enumerate(outs):
                for k in range(DK):
                    mm = three(nc, ps, tile_of(stream.high(n), k), tile_of(stream.low(n), k), high[:, k, :], low[:, k, :],
                               k == 0, k == DK - 1, mark(n, i == 0 and k == 0))
                mm.then_inc(done, 1)

        S, other = stage()
        with nc.Block() as block:
            @block.sync
            def _(sp):
                clear(sp, other)
                sp.dma_start(par[:, :], A["par2"][layer]).then_inc(S("par"), 16)
                stream.send(sp, RING)
                sp.wait_ge(S("par"), 16)

            @block.scalar
            def _(act):
                stream.hi(nc, act, PARTS)

            @block.gpsimd
            def _(pool):
                stream.lo(nc, pool, PARTS)

            @block.vector
            def _(dve):
                v = nc.vector
                dve.wait_ge(S("par"), 16)
                v.tensor_tensor(mod[:, :, :], mods[:, layer, :].rearrange("p (m c) -> p m c", m=48),
                                par_col("b_ada", 0, 48)[:, :, None].to_broadcast([P, 48, 2]), ALU.add).then_inc(S("mod"), 1)
                dve.wait_ge(S("mod"), 1)
                for i, (sc, g) in enumerate(((SC1, "g_mix"), (SC2, "g_ffn"))):
                    v.tensor_scalar(gain[:, i, :, :], mod[:, sc:sc + 8, :], 1.0, None, ALU.add).then_inc(S("one_plus"), 1)
                dve.wait_ge(S("one_plus"), 2)
                for i, (sc, g) in enumerate(((SC1, "g_mix"), (SC2, "g_ffn"))):
                    v.tensor_tensor(gain[:, i, :, :], gain[:, i, :, :], par_col(g, 0, 8)[:, :, None].to_broadcast([P, 8, 2]), ALU.mult).then_inc(S("gain"), 1)

        def norm_mod(which, shift, sts, scratch):
            S, other = stage()
            SQ = {"x": tiles_of(scratch, 0, 8), "c": tiles_of(scratch, 8, 8, CTX)}
            RST = {"x": tiles_of(scratch, 12), "c": tiles_of(scratch, 13)[:, 0:CTX]}
            with nc.Block() as block:
                @block.sync
                def _(sp):
                    clear(sp, other)

                @block.tensor
                def _(pe):
                    for s in sts:
                        nm, n = s["name"], s["n"]
                        for t in range(DK):
                            pe.wait_ge(S("sq" + nm), t + 1)
                            mm = nc.tensor.matmul(PS[:, s["bank"], 0:n], C("ones", P), SQ[nm][:, t, :], start=(t == 0), stop=(t == DK - 1))
                        mm.then_inc(S("sumsq" + nm), 1)

                @block.scalar
                def _(act):
                    a = nc.scalar
                    for s in sts:
                        nm = s["name"]
                        for t in range(DK):
                            a.activation(SQ[nm][:, t, :], s["src"][:, t, :], ACT.Square).then_inc(S("sq" + nm), 1)
                    for s in sts:
                        nm, n = s["name"], s["n"]
                        act.wait_ge(S("sumsq" + nm), 1)
                        a.activation(RST[nm], PS[:, s["bank"], 0:n], ACT.Ln, scale=1.0 / D, bias=eps).then_inc(S("log" + nm), 1)
                        act.wait_ge(S("log" + nm), 1)
                        a.activation(RST[nm], RST[nm], ACT.Exp, scale=-0.5).then_inc(S("rstd" + nm), 1)
                    for s in sts:
                        nm = s["name"]
                        for t in range(DK):
                            act.wait_ge(S("normed" + nm), t + 1)
                            a.activation(s["h"][:, t, :], SQ[nm][:, t, :], ACT.Identity, bias=mod[:, shift + t, s["k"]:s["k"] + 1]).then_inc(S("h" + nm), 1)

                @block.vector
                def _(dve):
                    for s in sts:
                        nm = s["name"]
                        dve.wait_ge(S("rstd" + nm), 1)
                        for t in range(DK):
                            nc.vector.scalar_tensor_tensor(out=SQ[nm][:, t, :], in0=s["src"][:, t, :], scalar=gain[:, which, t, s["k"]:s["k"] + 1],
                                                           in1=RST[nm], op0=ALU.mult, op1=ALU.mult).then_inc(S("normed" + nm), 1)
                    for s in sts:
                        nm = s["name"]
                        for t in range(DK):
                            dve.wait_ge(S("h" + nm), t + 1)
                            nc.vector.scalar_tensor_tensor(out=s["l"][:, t, :], in0=SQ[nm][:, t, :], scalar=mod[:, shift + t, s["k"]:s["k"] + 1],
                                                           in1=s["h"][:, t, :].bitcast(F32), op0=ALU.add, op1=ALU.subtract).then_inc(S("l" + nm), 1)

        norm_mod(0, SH1, streams, Y[:, 18 * T:32 * T])

        n0 = FIRST2["in"]
        def padded(at, n):
            return Y[:, at:at + 2 * (n + 16)].rearrange("p (c t) -> p c t", c=2)

        QR, KR, FO, VV = XT(0, 4), XT(4, 2), XT(13, 2), XT(16, 6, P)
        QRc, KRc, FOc = XT(6, 4, CTX), XT(8, 2, CTX), XT(15, 2, CTX)
        PL, PLc = padded(9 * T, T), padded(9 * T + 2 * XB, CTX)
        tiles = [("q", i) for i in range(4)] + [("k", i) for i in range(2)] + [("v", 0)] + [("p", i) for i in range(2)] + [("f", i) for i in range(2)]
        plan = {"x": tiles, "c": tiles if update else [t for t in tiles if t[0] in "kv"]}
        where = {"x": {"q": QR, "k": KR, "f": FO, "p": PL[:, :, 8:8 + T], "v": VV[:, 2:6, :]},
                 "c": {"q": QRc, "k": KRc, "f": FOc, "p": PLc[:, :, 8:8 + CTX], "v": VV[:, 0:2, :]}}
        S, other = stage()
        with nc.Block() as block:
            @block.sync
            def _(sp):
                clear(sp, other)
                stream.send(sp, n0 + 11 + RING - 1)

            @block.tensor
            def _(pe):
                for j, t in enumerate(tiles):
                    n = n0 + j
                    stream.wait_split(pe, n)
                    first = True
                    for s in streams:
                        if t not in plan[s["name"]]:
                            continue
                        i = plan[s["name"]].index(t)
                        if i >= 4:
                            pe.wait_ge(S("evicted" + s["name"]), i - 3)
                        bank = s["bank"] + i % 4
                        if t[0] != "v":
                            for k in range(DK):
                                mm = three(nc, PS[:, bank, 0:s["n"]], tile_of(stream.high(n), k), tile_of(stream.low(n), k),
                                           s["h"][:, k, :], s["l"][:, k, :], k == 0, k == DK - 1, mark(n, first))
                                first = False
                        else:
                            for q in range(s["n"] // P):
                                for k in range(DK):
                                    mm = three(nc, PS[:, bank, q * P:(q + 1) * P], s["h"][:, k, q * P:(q + 1) * P], s["l"][:, k, q * P:(q + 1) * P],
                                               tile_of(stream.high(n), k), tile_of(stream.low(n), k), k == 0, k == DK - 1, mark(n, first))
                                    first = False
                        mm.then_inc(S("product" + s["name"]), 1)

            @block.scalar
            def _(act):
                for j, t in enumerate(tiles):
                    for s in streams:
                        if t not in plan[s["name"]]:
                            continue
                        i = plan[s["name"]].index(t)
                        act.wait_ge(S("product" + s["name"]), i + 1)
                        dst = where[s["name"]][t[0]]
                        src = PS[:, s["bank"] + i % 4, 0:s["n"]]
                        if t[0] == "v":
                            src = src.rearrange("p (q c) -> p q c", c=P)
                        else:
                            dst = dst[:, t[1], :]
                        nc.scalar.activation(dst, src, ACT.Copy).then_inc(S("evicted" + s["name"]), 1)
                    stream.hi(nc, act, n0 + min(j + 3, 11 + 1))

            @block.gpsimd
            def _(pool):
                stream.lo(nc, pool, n0 + 11 + 1)

        above.close()
        above = ExitStack()
        Z = above.enter_context(nc.sbuf_tensor(f"more_tiles{layer}", [P, 9 * T], F32))
        KA = XT(18, 2, CKV)
        QN, QNc = XT(21, 4), XT(25, 4, CTX)
        MX, MXc = tiles_of(mixed, 0, 8), tiles_of(mixed, 8, 8, CTX)
        items = [(QR[:, i, :], T, "q_gain", QN[:, i, :], True) for i in range(4)]
        items += [(KR[:, i, :], T, "k_gain", KA[:, i, CTX:CKV], True) for i in range(2)]
        items += [(KRc[:, i, :], CTX, "k_gain", KA[:, i, 0:CTX], False) for i in range(2)]
        if update:
            items += [(QRc[:, i, :], CTX, "q_gain", QNc[:, i, :], False) for i in range(4)]
        S, other = stage()
        with nc.Block() as block:
            @block.sync
            def _(sp):
                clear(sp, other)

            def scratch(i):
                n = items[i][1]
                return mixed[:, i * T:(i + 1) * T] if i < 6 else mixed[:, 6 * T + (i - 6) * CTX:6 * T + (i - 6) * CTX + n]

            @block.tensor
            def _(pe):
                for i, (raw, n, g, dst, turn) in enumerate(items):
                    pe.wait_ge(S("sq"), i + 1)
                    if i >= 4:
                        pe.wait_ge(S("log"), i - 3)
                    nc.tensor.matmul(PS[:, i % 4, 0:n], C("head_ones", P), scratch(i), start=True, stop=True).then_inc(S("sumsq"), 1)
                for i in range(6):
                    pe.wait_ge(S("normed"), i + 1)
                    if i >= 4:
                        pe.wait_ge(S("sin"), i - 3)
                    nc.tensor.matmul(PS[:, 4 + i % 4, :], C("swap", P), items[i][0], start=True, stop=True).then_inc(S("swapped"), 1)

            @block.scalar
            def _(act):
                a = nc.scalar
                for i, (raw, n, g, dst, turn) in enumerate(items):
                    a.activation(scratch(i), raw, ACT.Square).then_inc(S("sq"), 1)
                for i, (raw, n, g, dst, turn) in enumerate(items):
                    act.wait_ge(S("sumsq"), i + 1)
                    a.activation(scratch(i), PS[:, i % 4, 0:n], ACT.Ln, scale=1.0 / HD, bias=eps).then_inc(S("log"), 1)
                for i in range(len(items)):
                    act.wait_ge(S("log"), i + 1)
                    a.activation(scratch(i), scratch(i), ACT.Exp, scale=-0.5).then_inc(S("rstd"), 1)

            @block.vector
            def _(dve):
                v = nc.vector

                def rotate(i):
                    dst = items[i][3]
                    dve.wait_ge(S("normed"), i + 1)
                    if i >= 2:
                        dve.wait_ge(S("rotated"), i - 1)
                    v.tensor_tensor(XT(27 + i % 2), items[i][0], C("cos", T), ALU.mult).then_inc(S("cos"), 1)
                    dve.wait_ge(S("swapped"), i + 1)
                    v.tensor_tensor(XT(29 + i % 2), PS[:, 4 + i % 4, :], C("sin", T), ALU.mult).then_inc(S("sin"), 1)
                    dve.wait_ge(S("cos"), i + 1)
                    dve.wait_ge(S("sin"), i + 1)
                    v.tensor_tensor(dst, XT(27 + i % 2), XT(29 + i % 2), ALU.add).then_inc(S("rotated"), 1)

                for i, (raw, n, g, dst, turn) in enumerate(items):
                    dve.wait_ge(S("rstd"), i + 1)
                    v.scalar_tensor_tensor(out=raw if turn else dst, in0=raw, scalar=par_col(g), in1=scratch(i),
                                           op0=ALU.mult, op1=ALU.mult).then_inc(S("normed"), 1)
                    if 1 <= i <= 6:
                        rotate(i - 1)

        full = streams if update else streams[:1]
        DFT = Z[:, 0:8 * T].rearrange("p (q c t) -> p q c t", q=4, c=2)
        U = {"x": dict(p=PL, f=FO, mx=MX, dft=DFT, norm=1.0, g=Y[:, 27 * T:31 * T], f2=XT(7, 2), cnt=C("count_x", 2 * T).rearrange("p (c t) -> p c t", c=2)),
             "c": dict(p=PLc, f=FOc, mx=MXc, dft=DFT[:, :, :, 0:T:2], norm=float(np.sqrt(2.0)), g=Y[:, 5 * T:7 * T], f2=XT(31, 2, CTX), cnt=C("count_c", 2 * CTX).rearrange("p (c t) -> p c t", c=2))}
        S, other = stage()
        with nc.Block() as block:
            @block.sync
            def _(sp):
                clear(sp, other)
                sp.dma_start(Z[:, 0:8 * T], A["dft"]).then_inc(S("dft"), 16)
                sp.wait_ge(S("dft"), 16)

            @block.gpsimd
            def _(pool):
                g = nc.gpsimd
                done = [0]

                def link(ins):
                    done[0] += 1
                    ins.then_inc(S("pool_step"), 1)
                    pool.wait_ge(S("pool_step"), done[0])

                for s in full:
                    u, n = U[s["name"]], s["n"]
                    w = n + 16
                    s2, s4, s8, mean = (Y[:, i * XB:i * XB + w] for i in range(4))
                    link(g.memset(u["p"][:, :, 0:8], 0.0))
                    link(g.memset(u["p"][:, :, 8 + n:16 + n], 0.0))
                    for c in range(2):
                        src = u["p"][:, c, :]
                        rows = slice(0, P)
                        link(g.tensor_tensor(s2[:, 1:w], src[:, 0:w - 1], src[:, 1:w], ALU.add))
                        link(g.tensor_tensor(s4[:, 2:w - 2], s2[:, 1:w - 3], s2[:, 3:w - 1], ALU.add))
                        lo, hi = s2[0:64, 8:8 + n], s4[64:128, 8:8 + n]
                        if c:
                            link(g.tensor_tensor(s8[:, 4:w - 4], s4[:, 2:w - 6], s4[:, 6:w - 2], ALU.add))
                            link(g.tensor_tensor(s2[64:128, 8:8 + n], s8[64:128, 4:4 + n], s8[64:128, 12:12 + n], ALU.add))
                            lo, hi = s8[0:64, 8:8 + n], s2[64:128, 8:8 + n]
                        link(g.tensor_tensor(mean[0:64, 0:n], lo, u["cnt"][0:64, c, :], ALU.mult))
                        link(g.tensor_tensor(mean[64:128, 0:n], hi, u["cnt"][64:128, c, :], ALU.mult))
                        link(g.tensor_tensor(src[:, 8:8 + n], mean[:, 0:n], src[:, 8:8 + n], ALU.subtract))
                    g.memset(mean[:, 0:1], 0.0).then_inc(S("d" + s["name"]), 1)

            @block.tensor
            def _(pe):
                for s in full:
                    nm, n, b = s["name"], s["n"], s["bank"]
                    u, nq = U[nm], s["n"] // P
                    for q in range(nq):
                        if q >= 2:
                            pe.wait_ge(S("g" + nm), q - 1)
                        for c in range(2):
                            mm = nc.tensor.matmul(PS[:, b + q % 2, c * 256:(c + 1) * 256], u["f"][:, c, q * P:(q + 1) * P], C("cs64", 256), start=True, stop=True)
                        mm.then_inc(S("gp" + nm), 1)
                    pe.wait_ge(S("dft"), 16)
                    pe.wait_ge(S("g" + nm), nq)
                    gg = u["g"].rearrange("p (q c x j) -> p q c x j", q=nq, c=2, x=2)
                    for c in range(2):
                        for q in range(nq):
                            for x in range(2):
                                mm = nc.tensor.matmul(PS[:, b + c, 0:n], gg[:, q, c, x, :], u["dft"][:, q, x, :], start=(q == 0 and x == 0), stop=(q == nq - 1 and x == 1))
                        mm.then_inc(S("f" + nm), 1)
                    for c in range(2):
                        pe.wait_ge(S("f_out" + nm), c + 1)
                        nc.tensor.matmul(PS[:, b + 2 + c, 0:n], par_col("w_four", c * P, P), u["f2"][:, c, :], start=True, stop=True).then_inc(S("y" + nm), 1)
                for s in full:
                    nm, n, b = s["name"], s["n"], s["bank"]
                    for c in range(2):
                        pe.wait_ge(S("d" + nm), 1)
                        pe.wait_ge(S("y_out" + nm), c + 1)
                        nc.tensor.matmul(PS[:, b + 2 + c, 0:n], par_col("w_pool", c * P, P), U[nm]["p"][:, c, 8:8 + n], start=True, stop=True).then_inc(S("pooled" + nm), 1)

            @block.scalar
            def _(act):
                a = nc.scalar
                for s in full:
                    nm, n, b = s["name"], s["n"], s["bank"]
                    u, nq = U[nm], s["n"] // P
                    for q in range(nq):
                        act.wait_ge(S("gp" + nm), q + 1)
                        a.activation(u["g"][:, q * T:(q + 1) * T], PS[:, b + q % 2, :], ACT.Copy).then_inc(S("g" + nm), 1)
                    for c in range(2):
                        act.wait_ge(S("f" + nm), c + 1)
                        a.activation(u["f2"][:, c, :], PS[:, b + c, 0:n], ACT.Copy, scale=u["norm"]).then_inc(S("f_out" + nm), 1)
                    for c in range(2):
                        act.wait_ge(S("y" + nm), c + 1)
                        a.activation(u["mx"][:, 6 + c, :], PS[:, b + 2 + c, 0:n], ACT.Copy).then_inc(S("y_out" + nm), 1)
                for s in full:
                    nm, n, b = s["name"], s["n"], s["bank"]
                    for c in range(2):
                        act.wait_ge(S("pooled" + nm), c + 1)
                        a.activation(U[nm]["mx"][:, 4 + c, :], PS[:, b + 2 + c, 0:n], ACT.Copy, scale=par_col("pool_scale", c)).then_inc(S("pool_out"), 1)

        def half(h):
            return slice(64 * (h % 2), 64 * (h % 2) + 64)

        attention(nc, stage, PS, ident, None, heads=8, dv=64, rows=64, blocks=T // P,
                  query=lambda h: QN[half(h), h // 2, :], key=lambda h: KA[half(h), h // 4, :],
                  value=lambda h, kb: VV[:, kb, (h // 4) * 64:(h // 4) * 64 + 64], nkeys=[CKV] * (T // P),
                  scale=HD ** -0.5, out=lambda h: MX[half(h), h // 2, :],
                  probs=[Y[:, a:a + CKV] for a in (12 * T, 12 * T + CKV, 27 * T)], probsT=[XT(0, 6), XT(6, 6)], small=XT(29), part=lambda h: 64 * (h % 2))
        if update:
            attention(nc, stage, PS, ident, None, heads=8, dv=64, rows=64, blocks=CTX // P,
                      query=lambda h: QNc[half(h), h // 2, :], key=lambda h: KA[half(h), h // 4, 0:CTX],
                      value=lambda h, kb: VV[:, kb, (h // 4) * 64:(h // 4) * 64 + 64], nkeys=[CTX] * (CTX // P),
                      scale=HD ** -0.5, out=lambda h: MXc[half(h), h // 2, :],
                      probs=[XT(a)[:, 0:CTX] for a in (12, 13, 14)], probsT=[XT(0, 2), XT(6, 2)], small=XT(29), part=lambda h: 64 * (h % 2))

        def project(first, kt, rhs, gate, split=()):
            S, other = stage()
            chunks = kt
            with nc.Block() as block:
                @block.sync
                def _(sp):
                    clear(sp, other)
                    stream.send(sp, min(first + chunks + RING - 1, NCHUNK2))

                @block.tensor
                def _(pe):
                    if split:
                        pe.wait_ge(S("low"), len(split))
                    for m in range(8):
                        if m >= 4:
                            for s in full:
                                pe.wait_ge(S("added" + s["name"]), m - 3)
                        for k in range(kt):
                            n, b = first + (m * kt + k) // 8, (m * kt + k) % 8
                            if b == 0:
                                stream.wait_split(pe, n)
                            for i, s in enumerate(full):
                                high, low = rhs[s["name"]]
                                mm = three(nc, PS[:, s["bank"] + m % 4, 0:s["n"]], tile_of(stream.high(n), b), tile_of(stream.low(n), b),
                                           high[:, k, :], low[:, k, :], k == 0, k == kt - 1, mark(n, i == 0 and b == 0))
                                if k == kt - 1:
                                    mm.then_inc(S("product" + s["name"]), 1)

                @block.scalar
                def _(act):
                    for x, high, low in split:
                        nc.scalar.activation(high, x, ACT.Copy).then_inc(S("high"), 1)
                    stream.hi(nc, act, min(first + chunks + 1, NCHUNK2))

                @block.gpsimd
                def _(pool):
                    stream.lo(nc, pool, min(first + chunks + 1, NCHUNK2))

                @block.vector
                def _(dve):
                    for i, (x, high, low) in enumerate(split):
                        dve.wait_ge(S("high"), i + 1)
                        nc.vector.tensor_tensor(low, x, high.bitcast(F32), ALU.subtract).then_inc(S("low"), 1)
                    for m in range(8):
                        for s in full:
                            dve.wait_ge(S("product" + s["name"]), m + 1)
                            nc.vector.scalar_tensor_tensor(out=s["src"][:, m, :], in0=PS[:, s["bank"] + m % 4, 0:s["n"]], scalar=mod[:, gate + m, s["k"]:s["k"] + 1],
                                                           in1=s["src"][:, m, :], op0=ALU.mult, op1=ALU.add).then_inc(S("added" + s["name"]), 1)

        above.close()
        lower.close()
        with nc.sbuf_tensor(f"mixed_parts{layer}", [P, 24 * T], F32R) as parts:
            MH, ML, MHc, MLc = tiles_of(parts, 0, 8), tiles_of(parts, 8, 8), tiles_of(parts, 16, 8, CTX), tiles_of(parts, 20, 8, CTX)
            split = [(MX[:, k, :], MH[:, k, :], ML[:, k, :]) for k in range(DK)]
            if update:
                split += [(MXc[:, k, :], MHc[:, k, :], MLc[:, k, :]) for k in range(DK)]
            project(FIRST2["out"], 8, {"x": (MH, ML), "c": (MHc, MLc)}, GA1, split)
        room.close()

        HC, HCL = (room.enter_context(nc.sbuf_tensor(f"context_again_{part}{layer}", [P, DK, CTX], F32R))[:, :, :] for part in ("high", "low"))
        streams[1].update(h=HC, l=HCL)
        with nc.sbuf_tensor(f"norm_scratch{layer}", [P, 14 * T], F32) as scratch:
            norm_mod(1, SH2, full, scratch)

        hidden = room.enter_context(nc.sbuf_tensor(f"hidden_parts{layer}", [P, 33 * T], F32R))
        scratch = room.enter_context(nc.sbuf_tensor(f"hidden_scratch{layer}", [P, 6 * T], F32))
        FFN = {"x": (tiles_of(hidden, 0, FH), tiles_of(hidden, 11, FH)),
               "c": (tiles_of(hidden, 22, 2 * FH, CTX)[:, 0:FH, :], tiles_of(hidden, 22, 2 * FH, CTX)[:, FH:2 * FH, :])}
        SG = {"x": tiles_of(scratch, 0, 2), "c": tiles_of(scratch, 4, 2, CTX)}
        PR = {"x": tiles_of(scratch, 2, 2), "c": tiles_of(scratch, 5, 2, CTX)}
        for part in range(2):
            n0 = FIRST2[f"up{part}"]
            S, other = stage()
            with nc.Block() as block:
                @block.sync
                def _(sp):
                    clear(sp, other)
                    stream.send(sp, n0 + 2 * FH + RING - 1)

                @block.tensor
                def _(pe):
                    for t in range(FH):
                        if t >= 2:
                            for s in full:
                                pe.wait_ge(S("act" + s["name"]), t - 1)
                        for j in range(2):
                            gemm(pe, n0 + 2 * t + j, [(PS[:, s["bank"] + 2 * (t % 2) + j, 0:s["n"]], s["h"], s["l"], S(("gate", "up")[j] + s["name"])) for s in full])

                @block.scalar
                def _(act):
                    def high(t):
                        for s in full:
                            act.wait_ge(S("act" + s["name"]), t + 1)
                            nc.scalar.activation(FFN[s["name"]][0][:, t, :], PR[s["name"]][:, t % 2, :], ACT.Copy).then_inc(S("high" + s["name"]), 1)

                    stream.hi(nc, act, n0 + PARTS)
                    for t in range(FH):
                        for s in full:
                            act.wait_ge(S("gate" + s["name"]), t + 1)
                            if t >= 2:
                                act.wait_ge(S("act" + s["name"]), t - 1)
                            nc.scalar.activation(SG[s["name"]][:, t % 2, :], PS[:, s["bank"] + 2 * (t % 2), 0:s["n"]], ACT.Silu).then_inc(S("silu" + s["name"]), 1)
                        stream.hi(nc, act, n0 + 2 * t + 3)
                        if t:
                            high(t - 1)
                        stream.hi(nc, act, n0 + min(2 * t + 4, 2 * FH + 1))
                    high(FH - 1)

                @block.gpsimd
                def _(pool):
                    def low(t):
                        for s in full:
                            pool.wait_ge(S("high" + s["name"]), t + 1)
                            nc.gpsimd.tensor_tensor(FFN[s["name"]][1][:, t, :], PR[s["name"]][:, t % 2, :], FFN[s["name"]][0][:, t, :].bitcast(F32), ALU.subtract).then_inc(S("low" + s["name"]), 1)

                    for t in range(FH):
                        stream.lo(nc, pool, n0 + 2 * t + 3)
                        if t:
                            low(t - 1)
                        stream.lo(nc, pool, n0 + min(2 * t + 4, 2 * FH + 1))
                    low(FH - 1)

                @block.vector
                def _(dve):
                    for t in range(FH):
                        for s in full:
                            dve.wait_ge(S("silu" + s["name"]), t + 1)
                            dve.wait_ge(S("up" + s["name"]), t + 1)
                            if t >= 2:
                                dve.wait_ge(S("low" + s["name"]), t - 1)
                            nc.vector.tensor_tensor(PR[s["name"]][:, t % 2, :], PS[:, s["bank"] + 2 * (t % 2) + 1, 0:s["n"]], SG[s["name"]][:, t % 2, :], ALU.mult).then_inc(S("act" + s["name"]), 1)

            project(FIRST2[f"down{part}"], FH, FFN, GA2)
        room.close()

        S, other = stage()
        with nc.Block() as block:
            @block.sync
            def _(sp):
                clear(sp, other)
                clear(sp, WR[3])
                clear(sp, WR[4:])

    S, other = stage()
    with nc.Block() as block:
        @block.sync
        def _(sp):
            sp.dma_start(A["out"], xT[:, :, :].rearrange("p k t -> p (k t)")).then_inc(stored, 16)
            sp.wait_ge(stored, 16)


def blocks(w, m=P):
    k = w.shape[0] // P
    return w.reshape(k, P, w.shape[1]).transpose(1, 0, 2).reshape(P, -1)


def fill(a):
    out = np.zeros((P, CW), np.float32)
    out[:, :a.shape[1]] = a
    return out


OFF = {}
_at = 0
for _name, _n in (("rw", 1664), ("rw_g", 512), ("q_lat", 384), ("kv_lat", 256), ("k_pe", 32), ("mla_g", 512),
                  ("conv_u", 1024), ("conv_g", 512), ("xq", 512), ("xg", 512), ("merge", 4096)):
    OFF[_name] = _at
    _at += _n


def chunks1(I, l):
    w = I["w_in"][l]

    def cols(name, t, n=P):
        a = OFF[name] + t * P
        return blocks(w[:, a:a + n])

    out = [cols("rw", t) for t in range(13)]
    out += [cols("q_lat", t) for t in range(3)] + [cols("kv_lat", t) for t in range(2)]
    kpe = np.zeros((D, P), np.float32)
    kpe[:, 64:96] = w[:, OFF["k_pe"]:OFF["k_pe"] + 32]
    out.append(blocks(kpe))
    uq = I["mla_w_uq"][l]
    heads = [blocks(uq[:, h * 96:(h + 1) * 96]) for h in range(8)]
    for a in (0, 3, 6):
        out.append(fill(np.concatenate(heads[a:a + 3], 1)))
    ukv = I["mla_w_ukv"][l].reshape(256, 8, 128)
    out.append(np.concatenate([blocks(ukv[:, h, :64]) for h in range(8)], 1))
    out.append(blocks(ukv[:, :, 64:].reshape(256, 512)))
    out += [cols("conv_u", t) for t in range(8)]
    out += [cols("xq", t) for t in range(4)]
    mk = I["xattn_w_mem_kv"][l]
    out += [blocks(mk[:, t * P:(t + 1) * P]) for t in range(4)]
    out += [blocks(mk[k * 256:(k + 1) * 256, 512:]) for k in range(4)]
    for name in ("rw_g", "mla_g", "conv_g", "xg"):
        out += [cols(name, t) for t in range(4)]
    ob = I["w_o_branch"][l]
    for m in range(8):
        o = [blocks(ob[n][:, m * P:(m + 1) * P]) for n in range(4)]
        g = [cols("merge", 8 * n + m) for n in range(4)]
        out += [np.concatenate(o[0:2], 1), g[0], g[1], np.concatenate(o[2:4], 1), g[2], g[3]]
    out += [blocks(I["w_out"][l][:, m * P:(m + 1) * P]) for m in range(8)]
    return np.stack(out)


def colsof(v):
    return v.reshape(-1, P).T


def params1(I, l):
    out = np.zeros((P, NPAR), np.float32)

    def put(name, a):
        out[:, PCOL[name]:PCOL[name] + a.shape[1]] = a

    put("b_gate", colsof(I["b_gate"][l].reshape(-1)))
    for name, key in (("mu", "rwkv_mu"), ("w0", "rwkv_w0"), ("a0", "rwkv_a0"), ("k_k", "rwkv_k_k"), ("k_a", "rwkv_k_a"),
                      ("lnx_g", "rwkv_lnx_g"), ("lnx_b", "rwkv_lnx_b"), ("q_norm", "mla_q_norm"), ("kv_norm", "mla_kv_norm"),
                      ("conv_b", "conv_b"), ("cln_g", "conv_ln_g"), ("cln_b", "conv_ln_b"), ("ln_g", "ln_g"), ("ln_b", "ln_b")):
        put(name, colsof(I[key][l]))
    put("r_k", colsof(I["rwkv_r_k"][l].reshape(-1)))
    put("conv_w", I["conv_w"][l].reshape(TAPS, WT, P).transpose(2, 1, 0).reshape(P, WT * TAPS))
    put("w2a2", np.concatenate([I["rwkv_w2"][l], I["rwkv_a2"][l]], 0))
    return out


def consts1():
    out = np.zeros((P, NCST), np.float32)

    def put(name, a, k=0):
        out[:, CCOL[name] + k:CCOL[name] + k + a.shape[1]] = a

    i = np.arange(P)
    row, col = i[:, None], i[None, :]
    put("ident", np.eye(P, dtype=np.float32))
    put("head_ones", (row // 64 == col // 64).astype(np.float32))
    put("ones", np.ones((P, P), np.float32))
    same = row // 64 == col // 64
    put("tri", (same & (row < col)).astype(np.float32))
    put("tri", (same & (row <= col)).astype(np.float32), P)
    for lv in range(6):
        n = 1 << lv
        low = (row // (2 * n) == col // (2 * n)) & ((row // n) % 2 == 1) & ((col // n) % 2 == 0)
        if lv == 0:
            put("m0", low.astype(np.float32))
        put("lev", low.T.astype(np.float32), lv * P)
    put("causal", np.where(col > row, -1e30, 0.0).astype(np.float32))
    for a in range(32):
        out[64 + (a + 16) % 32, CCOL["swap"] + a] = 1.0
    inv = (np.float32(10000.0) ** (-np.arange(0, 32, 2, dtype=np.float32) / np.float32(32))).astype(np.float32)
    out[64:96, CCOL["freq"]] = np.concatenate([inv, inv])
    out[64:80, CCOL["sign"]] = -1.0
    out[80:96, CCOL["sign"]] = 1.0
    for k, e in enumerate((64e-5, 1e-6, 1e-5, 0.0)):
        out[:, CCOL["eps"] + k] = e
    put("reset", np.broadcast_to((np.arange(T) % CH != 0).astype(np.float32), (P, T)))
    return out


def turned(a):
    return np.ascontiguousarray(a.T.reshape(DK, P, -1).transpose(1, 0, 2).reshape(P, -1))


def layouts(I):
    return {
        "xT": turned(I["x"][0]),
        "memT": turned(I["mem"][0]),
        "pos": np.ascontiguousarray(I["positions"].reshape(T)),
        "cst1": consts1(),
        "par1": np.stack([params1(I, l) for l in range(LAYERS)]),
        "w1": np.stack([chunks1(I, l) for l in range(LAYERS)]),
    }


def pair_diag(w):
    out = np.zeros((P, P), np.float32)
    out[:64, :64], out[64:, 64:] = w[0], w[1]
    return out


def chunks2(I, l):
    w = I["w_in_2"][l]
    out = [blocks(w[:, t * P:(t + 1) * P]) for t in range(4)]
    for g in range(2):
        k = w[:, 512 + 64 * g:512 + 64 * g + 64]
        out.append(blocks(np.concatenate([k, k], 1)))
    out += [blocks(w[:, a:a + P]) for a in (640, 768, 896, 1024, 1152)]
    out += [blocks(I["w_out_2"][l][:, m * P:(m + 1) * P]) for m in range(8)]
    gu = I["w_gate_up_2"][l]
    dn = I["w_down_2"][l]
    for part in range(2):
        for t in range(part * FH, (part + 1) * FH):
            out += [blocks(gu[:, t * P:(t + 1) * P]), blocks(gu[:, FF + t * P:FF + (t + 1) * P])]
        rows = dn[part * FH * P:(part + 1) * FH * P]
        down = np.concatenate([blocks(rows[:, m * P:(m + 1) * P]) for m in range(8)], 1)
        out += [down[:, a:a + CW] for a in range(0, down.shape[1], CW)]
    return np.stack(out)


def params2(I, l):
    out = np.zeros((P, NPAR2), np.float32)

    def put(name, a, k=0):
        out[:, PCOL2[name] + k:PCOL2[name] + k + a.shape[1]] = a

    put("g_mix", colsof(I["g_mix_2"][l]))
    put("g_ffn", colsof(I["g_ffn_2"][l]))
    put("b_ada", colsof(I["b_ada_2"][l]))
    for name in ("q_gain", "k_gain"):
        g = I[name + "_2"][l]
        put(name, np.concatenate([g, g])[:, None])
    put("pool_scale", colsof(I["pool_scale_2"][l]))
    for c in range(2):
        put("w_pool", pair_diag(I["w_pool_2"][l][2 * c:2 * c + 2]), c * P)
        put("w_four", pair_diag(I["w_four_2"][l][2 * c:2 * c + 2]), c * P)
    return out


def dft(n):
    i = np.arange(n)
    a = 2.0 * np.pi * ((i[:, None] * i[None, :]) % n) / n
    both = np.stack([np.cos(a), -np.sin(a)], 1) / np.sqrt(n * 64.0)
    return both.reshape(n // P, P, 2, n).transpose(1, 0, 2, 3).reshape(P, -1).astype(np.float32)


def counts(n):
    t = np.arange(n)
    out = np.zeros((P, 2, n), np.float32)
    for g, w in enumerate((2, 4, 8, 16)):
        lo, hi = np.clip(t - w // 2, 0, n), np.clip(t + w - w // 2, 0, n)
        out[64 * (g % 2):64 * (g % 2) + 64, g // 2, :] = (1.0 / (hi - lo)).astype(np.float32)
    return out.reshape(P, -1)


def consts2():
    out = np.zeros((P, NCST2), np.float32)

    def put(name, a):
        out[:, CCOL2[name]:CCOL2[name] + a.shape[1]] = a

    i = np.arange(P)
    row, col = i[:, None], i[None, :]
    put("ident", np.eye(P, dtype=np.float32))
    put("head_ones", (row // 64 == col // 64).astype(np.float32))
    put("ones", np.ones((P, P), np.float32))
    put("swap", (row == (col ^ 16)).astype(np.float32))
    t = np.arange(T)
    freqs = (np.float32(10000.0) ** (-np.arange(16, dtype=np.float32) / np.float32(16))).astype(np.float32)
    place = np.stack([t // 64, t % 64]).astype(np.float32)
    r = i % 64
    ang = (place[r // 32] * freqs[r % 16][:, None]).astype(np.float32).astype(np.float64)
    put("cos", np.cos(ang).astype(np.float32))
    put("sin", (np.sin(ang) * np.where((r // 16) % 2, 1.0, -1.0)[:, None]).astype(np.float32))
    j = np.arange(64)
    a = 2.0 * np.pi * ((j[:, None] * j[None, :]) % 64) / 64
    put("cs64", np.concatenate([pair_diag(np.stack([f, f])) for f in (np.cos(a), np.sin(a))], 1).astype(np.float32))
    put("count_x", counts(T))
    put("count_c", counts(CTX))
    out[:, CCOL2["eps"]] = 1e-6
    return out


def layouts2(I):
    return {
        "ctxT": turned(I["ctx_2"][0]),
"cond": np.ascontiguousarray(np.stack([I["c_2"].reshape(D), I["c_ctx_2"].reshape(D)])),
        "ada": np.stack([I["w_ada_2"][l].T.reshape(48, P, D) for l in range(LAYERS)]),
        "cst2": consts2(),
        "par2": np.stack([params2(I, l) for l in range(LAYERS)]),
        "dft": dft(T),
        "w2": np.stack([chunks2(I, l) for l in range(LAYERS)]),
    }


_INS = ["x", "mem", "positions", "w_in", "b_gate", "rwkv_mu", "rwkv_w0", "rwkv_w2", "rwkv_a0", "rwkv_a2", "rwkv_k_k",
        "rwkv_k_a", "rwkv_r_k", "rwkv_lnx_g", "rwkv_lnx_b", "mla_q_norm", "mla_w_uq", "mla_kv_norm", "mla_w_ukv",
        "conv_w", "conv_b", "conv_ln_g", "conv_ln_b", "xattn_w_mem_kv", "w_o_branch", "w_out", "ln_g", "ln_b", "c_2",
        "ctx_2", "c_ctx_2", "w_ada_2", "b_ada_2", "g_mix_2", "g_ffn_2", "w_in_2", "q_gain_2", "k_gain_2", "w_pool_2",
        "pool_scale_2", "w_four_2", "w_out_2", "w_gate_up_2", "w_down_2"]


def kernel(**inputs):
    import concourse.bacc as bacc
    from concourse.bass_utils import run_bass_kernel_spmd as run

    I = {name: np.asarray(inputs[name]) for name in _INS}
    nc = bacc.Bacc("TRN2", target_bir_lowering=False, num_devices=1)
    arrays, A = {}, {}
    for name, a in {**layouts(I), **layouts2(I)}.items():
        a = np.ascontiguousarray(a)
        arrays[f"in_{name}"] = a
        A[name] = nc.dram_tensor(f"in_{name}", a.shape, mybir.dt.from_np(a.dtype), kind="ExternalInput").ap()
    A["out"] = nc.dram_tensor("out_0", (P, DK * T), F32, kind="ExternalOutput").ap()
    build(nc, A)
    r = run(nc, [arrays], core_ids=[0])
    got = r.results[0]["out_0"]
    return np.ascontiguousarray(got.reshape(P, DK, T).transpose(2, 1, 0).reshape(1, T, D))
```

```python
from contextlib import ExitStack

import numpy as np

import concourse.bass as bass
from concourse import mybir
from concourse.alu_op_type import AluOpType as ALU

F32 = mybir.dt.float32
I32 = mybir.dt.int32
F32R = mybir.dt.float32r
ACT = mybir.ActivationFunctionType
AX_X = mybir.AxisListType.X

P = 128
T = 512
D = 1024
DK = D // P
W = 512
WT = W // P
NB = 4
LAYERS = 2
MEM = 256
CTX = 256
HD = 64
CH = 64
NCH = T // CH
TAPS = 31
RW_TILES = 13
EXPH = float(np.exp(-0.5))
DEEP_ALPHA = (2.0 * LAYERS) ** 0.25
RING = 3
PARTS = 2
CW = 1024

PCOL = {}
_at = 0
for _name, _n in (("b_gate", 32), ("mu", 13), ("w0", 4), ("a0", 4), ("k_k", 4), ("k_a", 4), ("r_k", 4),
                  ("lnx_g", 4), ("lnx_b", 4), ("q_norm", 3), ("kv_norm", 2), ("conv_b", 4),
                  ("cln_g", 4), ("cln_b", 4), ("ln_g", 8), ("ln_b", 8), ("conv_w", WT * TAPS),
                  ("w2a2", 512)):
    PCOL[_name] = _at
    _at += _n
NPAR = _at

CCOL = {}
_at = 0
for _name, _n in (("ident", 128), ("head_ones", 128), ("ones", 128), ("tri", 384), ("m0", 128),
                  ("lev", 6 * 128), ("causal", 128), ("swap", 32), ("freq", 1), ("sign", 1),
                  ("eps", 4), ("reset", 512)):
    CCOL[_name] = _at
    _at += _n
NCST = _at

STAGE_CHUNKS = (("rwkv", RW_TILES), ("mla", 6 + 3 + 2), ("conv", 8), ("xattn", 4 + 8), ("gates", 16),
                ("merge", 6 * 8), ("out", 8))
FIRST = {}
_at = 0
for _name, _n in STAGE_CHUNKS:
    FIRST[_name] = _at
    _at += _n
NCHUNK1 = _at
SPLIT1 = [FIRST[_name] + _i for _name, _n in (("rwkv", RW_TILES), ("mla", 6), ("conv", 8), ("xattn", 4), ("gates", 16)) for _i in range(_n)]
SPLIT1 += [FIRST["merge"] + _i for _i in range(48) if _i % 3]


class Names:

    def __init__(self, handles):
        self.handles, self.of = handles, {}

    def __call__(self, name):
        if name not in self.of:
            self.of[name] = self.handles[len(self.of)]
        return self.of[name]


class Stream:

    def __init__(self, W, source, is_split):
        self.ring, self.highs, self.lows, self.arrived, self.used, self.hi_made, self.lo_made = W
        self.source, self.splits = source, is_split
        self.sent = self.hi_at = self.lo_at = 0

    def send(self, sp, upto):
        for n in range(self.sent, upto):
            last = n - RING
            if last in self.splits:
                sp.wait_ge(self.lo_made, self.splits.index(last) + 1)
            elif last >= 0:
                sp.wait_ge(self.used, last + 1)
            sp.dma_start(self.ring[:, n % RING, :], self.source(n)).then_inc(self.arrived[n % RING], 16)
        self.sent = max(self.sent, upto)

    def hi(self, nc, act, upto):
        for n in range(self.hi_at, upto):
            if n in self.splits:
                s = self.splits.index(n)
                self.wait(act, n)
                if s >= PARTS:
                    act.wait_ge(self.used, self.splits[s - PARTS] + 1)
                nc.scalar.activation(self.high(n), self.chunk(n), ACT.Copy).then_inc(self.hi_made, 1)
        self.hi_at = max(self.hi_at, upto)

    def lo(self, nc, pool, upto):
        for n in range(self.lo_at, upto):
            if n in self.splits:
                pool.wait_ge(self.hi_made, self.splits.index(n) + 1)
                nc.gpsimd.tensor_tensor(self.low(n), self.chunk(n), self.high(n).bitcast(F32), ALU.subtract).then_inc(self.lo_made, 1)
        self.lo_at = max(self.lo_at, upto)

    def wait(self, eng, n):
        eng.wait_ge(self.arrived[n % RING], 16 * (n // RING + 1))

    def wait_split(self, pe, n):
        pe.wait_ge(self.lo_made, self.splits.index(n) + 1)

    def chunk(self, n):
        return self.ring[:, n % RING, :]

    def high(self, n):
        return self.highs[:, self.splits.index(n) % PARTS, :]

    def low(self, n):
        return self.lows[:, self.splits.index(n) % PARTS, :]


def three(nc, ps, high, low, xhigh, xlow, start, stop, mark=None):
    mm = nc.tensor.matmul(ps, high, xhigh, start=start, stop=False)
    if mark is not None:
        mm.then_inc(mark, 1)
    nc.tensor.matmul(ps, high, xlow, start=False, stop=False)
    return nc.tensor.matmul(ps, low, xhigh, start=False, stop=stop)


def tile_of(chunk, k, m=P):
    return chunk[:, k * m:(k + 1) * m]


def build(nc, A):
    with ExitStack() as ctx:
        def sb(name, shape, dt=F32):
            return ctx.enter_context(nc.sbuf_tensor(name, shape, dt))

        pools = [[nc.alloc_semaphore(f"stage{p}_{i}") for i in range(50)] for p in range(2)]
        arrived = [nc.alloc_semaphore(f"chunk_arrived{i}") for i in range(RING)]
        used = nc.alloc_semaphore("chunks_used")
        hi_made, lo_made = nc.alloc_semaphore("high_made"), nc.alloc_semaphore("low_made")
        loaded = nc.alloc_semaphore("loaded")
        stored = nc.alloc_semaphore("stored")
        constants = nc.alloc_semaphore("second_constants")
        PS = ctx.enter_context(nc.psum_tensor("ps", [P, 8, 512], F32))
        turn = [0]

        def stage():
            turn[0] += 1
            return Names(pools[turn[0] % 2]), pools[(turn[0] + 1) % 2]

        WR = (sb("ring", [P, RING, CW]), sb("highs", [P, PARTS, CW], F32R), sb("lows", [P, PARTS, CW], F32R),
              arrived, used, hi_made, lo_made)
        mods = sb("mods", [P, LAYERS, 96])
        XH, XL = sb("x_high", [P, DK, T], F32R)[:, :, :], sb("x_low", [P, DK, T], F32R)[:, :, :]
        with ExitStack() as one:
            first(nc, one, A, PS, XH, XL, WR, mods, stage, loaded)
        with ExitStack() as two:
            second(nc, two, A, PS, XH, XL, WR, mods, stage, constants, stored)


def clear(sp, sems):
    for s in sems:
        sp.sem_clear(s)


def attention(nc, stage, PS, ident, causal, heads, dv, rows, blocks, query, key, value, nkeys, scale, out,
              probs, probsT, small, part):
    S, other = stage()
    units = [(h, q) for h in range(heads) for q in range(blocks)]
    wide = max(nkeys) > 512
    nbuf = len(probs)

    def turns(q):
        return (nkeys[q] + 511) // 512

    before = [0]
    for h, q in units:
        before.append(before[-1] + turns(q))
    stats = small.rearrange("p (s u) -> p s u", s=4)

    def scores(i, q):
        a = 2 * (i % 2) if wide else i % 4
        return PS[:, a:a + 2, :].rearrange("p b n -> p (b n)")[:, 0:nkeys[q]] if wide else PS[:, a, 0:nkeys[q]]

    sbuf = 2 if wide else 4

    def finish(act, h):
        act.wait_ge(S("product"), h + 1)
        nc.scalar.activation(out(h), PS[part(h):part(h) + dv, 6 + h % 2, 0:blocks * P], ACT.Copy).then_inc(S("out"), 1)

    with nc.Block() as block:
        @block.sync
        def _(sp):
            clear(sp, other)

        @block.tensor
        def _(pe):
            def make_scores(i):
                h, q = units[i]
                if i >= sbuf:
                    pe.wait_ge(S("probs"), i - sbuf + 1)
                s = scores(i, q)
                for a in range(0, nkeys[q], 512):
                    b = min(a + 512, nkeys[q])
                    mm = nc.tensor.matmul(s[:, a:b], query(h)[:, q * P:(q + 1) * P], key(h)[:, a:b], start=True, stop=True)
                mm.then_inc(S("scores"), 1)

            def turn(i):
                h, q = units[i]
                pe.wait_ge(S("scaled"), i + 1)
                for j in range(turns(q)):
                    n = before[i] + j
                    if n >= 2:
                        pe.wait_ge(S("turned_out"), n - 1)
                    for kb in range(4 * j, min(4 * j + 4, nkeys[q] // P)):
                        mm = nc.tensor.transpose(PS[:, 4 + n % 2, (kb % 4) * P:(kb % 4 + 1) * P], probs[i % nbuf][:, kb * P:(kb + 1) * P], ident)
                    mm.then_inc(S("turned"), 1)

            def product(h):
                pe.wait_ge(S("turned_out"), before[blocks * (h + 1)])
                if h >= 2:
                    pe.wait_ge(S("out"), h - 1)
                top = nkeys[-1] // P
                for kb in range(top):
                    q0 = min(q for q in range(blocks) if nkeys[q] > kb * P)
                    mm = nc.tensor.matmul(PS[part(h):part(h) + dv, 6 + h % 2, q0 * P:blocks * P], value(h, kb), probsT[h % 2][:, kb, q0 * P:blocks * P],
                                          start=(kb == 0), stop=(kb == top - 1))
                mm.then_inc(S("product"), 1)

            lead = 2 if wide else 3
            for i in range(min(lead, len(units))):
                make_scores(i)
            for i in range(len(units)):
                if i + lead < len(units):
                    make_scores(i + lead)
                turn(i)
                if i and i % blocks == 0:
                    product(i // blocks - 1)
            product(heads - 1)

        @block.scalar
        def _(act):
            for i, (h, q) in enumerate(units):
                act.wait_ge(S("negmax"), i + 1)
                if i >= nbuf:
                    act.wait_ge(S("turned"), before[i - nbuf + 1])
                nc.scalar.activation(probs[i % nbuf][:, 0:nkeys[q]], scores(i, q), ACT.Exp, scale=scale, bias=stats[:, 1, i:i + 1],
                                     accum_out=stats[:, 2, i:i + 1]).then_inc(S("probs"), 1)
                if i >= 2 and (i - 2) % blocks == blocks - 1:
                    finish(act, (i - 2) // blocks)
            finish(act, heads - 1)

        @block.vector
        def _(dve):
            v = nc.vector

            def mask(i):
                h, q = units[i]
                dve.wait_ge(S("scores"), i + 1)
                if causal is not None:
                    s = scores(i, q)[:, q * P:(q + 1) * P]
                    v.tensor_tensor(s, s, causal, ALU.add).then_inc(S("causal"), 1)

            def maximum(i):
                h, q = units[i]
                if causal is not None:
                    dve.wait_ge(S("causal"), i + 1)
                v.tensor_reduce(stats[:, 0, i:i + 1], scores(i, q), AX_X, ALU.max).then_inc(S("max"), 1)

            def negate(i):
                dve.wait_ge(S("max"), i + 1)
                v.tensor_scalar(stats[:, 1, i:i + 1], stats[:, 0, i:i + 1], -scale, None, ALU.mult).then_inc(S("negmax"), 1)

            def invert(i):
                dve.wait_ge(S("probs"), i + 1)
                v.reciprocal(stats[:, 3, i:i + 1], stats[:, 2, i:i + 1]).then_inc(S("inverse"), 1)

            def normalise(i):
                h, q = units[i]
                dve.wait_ge(S("inverse"), i + 1)
                p = probs[i % nbuf][:, 0:nkeys[q]]
                v.tensor_scalar(p, p, stats[:, 3, i:i + 1], None, ALU.mult).then_inc(S("scaled"), 1)

            def turned_out(i):
                h, q = units[i]
                if q == 0 and h >= 2:
                    dve.wait_ge(S("product"), h - 1)
                for j in range(turns(q)):
                    n = before[i] + j
                    nb = min(4, nkeys[q] // P - 4 * j)
                    dve.wait_ge(S("turned"), n + 1)
                    v.tensor_copy(probsT[h % 2][:, 4 * j:4 * j + nb, q * P:(q + 1) * P],
                                  PS[:, 4 + n % 2, 0:nb * P].rearrange("p (k t) -> p k t", k=nb)).then_inc(S("turned_out"), 1)

            n = len(units)
            for i in range(n + 2):
                if i < n:
                    mask(i)
                if causal is None and i < n:
                    maximum(i)
                if 1 <= i <= n:
                    invert(i - 1)
                if causal is not None and i < n:
                    maximum(i)
                if causal is None and i < n:
                    negate(i)
                if 1 <= i <= n:
                    normalise(i - 1)
                if causal is not None and i < n:
                    negate(i)
                if i >= 2:
                    turned_out(i - 2)


def first(nc, ctx, A, PS, XH, XL, WR, mods, stage, loaded):
    def sb(name, shape, dt=F32):
        return ctx.enter_context(nc.sbuf_tensor(name, shape, dt))

    xh = XH.bitcast(F32)
    used = WR[4]
    cst = sb("cst", [P, NCST])
    par = sb("par", [P, NPAR])
    oneless = sb("oneless", [P, 4])
    chunk_decays = sb("chunk_decays", [P, 4 * NCH])
    rope = sb("rope", [P, 2, T])
    BR = sb("BR", [P, NB * WT, T])
    X = sb("X", [P, 48 * T])

    def C(name, n=1, k=0):
        a = CCOL[name] + k
        return cst[:, a:a + n]

    def par_col(name, k=0):
        a = PCOL[name] + k
        return par[:, a:a + 1]

    def XT(i, n=1, w=T):
        return X[:, i * T:(i + n) * T] if n == 1 else X[:, i * T:i * T + n * w].rearrange("p (n t) -> p n t", n=n)

    ident = C("ident", P)

    S, other = stage()
    with nc.Block() as block:
        @block.sync
        def _(sp):
            for k in range(0, DK, 2):
                sp.dma_start(X[:, (4 + k) * T:(6 + k) * T], A["xT"][:, k * T:(k + 2) * T]).then_inc(S(f"x_in{k}"), 16)
                if k == 0:
                    sp.dma_start(cst[:, :], A["cst1"]).then_inc(loaded, 16)
                    sp.dma_start(X[64:96, 0:T].bitcast(I32), A["pos"].partition_broadcast(32)).then_inc(loaded, 16)
            sp.wait_ge(loaded, 32)

        @block.vector
        def _(dve):
            count = [0]

            def link(ins):
                count[0] += 1
                ins.then_inc(S("angle_step"), 1)
                dve.wait_ge(S("angle_step"), count[0])

            two_pi = 2.0 * np.pi
            c1 = float(np.float32(6.28125))
            c2 = float(np.float32(round((two_pi - c1) * 2 ** 19) / 2 ** 19))
            c3 = float(np.float32(two_pi - c1 - c2))
            magic = float(1.5 * 2 ** 23)
            pos, ang, turns, cosr = (X[64:96, i * T:(i + 1) * T] for i in range(4))
            rows = slice(64, 96)
            freq = cst[rows, CCOL["freq"]:CCOL["freq"] + 1]
            sgn = cst[rows, CCOL["sign"]:CCOL["sign"] + 1]
            dve.wait_ge(loaded, 32)
            v = nc.vector
            link(v.tensor_copy(turns, pos.bitcast(I32)))
            link(v.tensor_scalar(ang, turns, freq, None, ALU.mult))
            link(v.tensor_scalar(pos, ang, 1.0 / two_pi, None, ALU.mult))
            link(v.tensor_scalar(turns, pos, magic, None, ALU.add))
            link(v.tensor_scalar(turns, turns, magic, None, ALU.subtract))
            for c in (c1, c2, c3):
                link(v.scalar_tensor_tensor(out=ang, in0=turns, scalar=-c, in1=ang, op0=ALU.mult, op1=ALU.add))
            link(v.tensor_scalar(cosr, ang, float(np.pi / 2), None, ALU.add))
            link(v.tensor_scalar(pos, cosr, float(np.pi), None, ALU.is_gt))
            link(v.scalar_tensor_tensor(out=cosr, in0=pos, scalar=-two_pi, in1=cosr, op0=ALU.mult, op1=ALU.add))
            top = float(np.float32(3.1415925))
            link(v.tensor_scalar(cosr, cosr, top, -top, ALU.min, ALU.max))
            link(v.tensor_scalar(ang, ang, top, -top, ALU.min, ALU.max))
            v.memset(oneless[:, :], 0.0).then_inc(S("angles"), 1)
            dve.wait_ge(S("sines"), 2)
            v.tensor_scalar(rope[rows, 1, :], rope[rows, 1, :], sgn, None, ALU.mult).then_inc(S("signed"), 1)

        @block.scalar
        def _(act):
            for k in range(DK):
                act.wait_ge(S(f"x_in{k // 2 * 2}"), 16)
                nc.scalar.activation(XH[:, k, :], XT(4 + k), ACT.Copy).then_inc(S("x_hi"), 1)
            act.wait_ge(S("angles"), 1)
            nc.scalar.activation(rope[64:96, 0, :], X[64:96, 3 * T:4 * T], ACT.Sin).then_inc(S("sines"), 1)
            nc.scalar.activation(rope[64:96, 1, :], X[64:96, T:2 * T], ACT.Sin).then_inc(S("sines"), 1)

        @block.gpsimd
        def _(pool):
            for k in range(DK):
                pool.wait_ge(S("x_hi"), k + 1)
                nc.gpsimd.tensor_tensor(XL[:, k, :], XT(4 + k), xh[:, k, :], ALU.subtract).then_inc(S("x_lo"), 1)

    with nc.Fori(0, LAYERS) as layer:
        stream = Stream(WR, lambda n: A["w1"][bass.ds(layer, 1), n, :, :].rearrange("l p c -> p (l c)"), SPLIT1)

        def gemm(pe, bank, n, rhs, done, m=P, base=0, wait_bank=None):
            stream.wait(pe, n)
            for k in range(DK):
                mm = nc.tensor.matmul(PS[base:base + m, bank, 0:rhs.shape[2]], tile_of(stream.chunk(n), k)[:, 0:m],
                                      rhs[:, k, :], start=(k == 0), stop=(k == DK - 1))
                if k == 0 and n:
                    mm.then_inc(used, 1)
            mm.then_inc(done, 1)

        def gemm3(pe, bank, n, xh, xl, done):
            stream.wait_split(pe, n)
            for k in range(DK):
                mm = three(nc, PS[:, bank, :], tile_of(stream.high(n), k), tile_of(stream.low(n), k), xh[:, k, :], xl[:, k, :],
                           k == 0, k == DK - 1, used if k == 0 and n else None)
            mm.then_inc(done, 1)

        n0 = FIRST["rwkv"]
        praw = X[:, 30 * T:30 * T + 13 * 513].rearrange("p (c t) -> p c t", c=13)
        M = XT(0, 13)
        S, other = stage()
        with nc.Block() as block:
            @block.sync
            def _(sp):
                clear(sp, other)
                sp.dma_start(par[:, :], A["par1"][bass.ds(layer, 1), :, :].rearrange("l p c -> p (l c)")).then_inc(S("par"), 16)
                stream.send(sp, n0 + RW_TILES + RING - 1)
                sp.wait_ge(S("par"), 16)

            @block.tensor
            def _(pe):
                for t in range(RW_TILES):
                    if t >= 4:
                        pe.wait_ge(S("evicted"), t - 3)
                    gemm3(pe, t % 4, n0 + t, XH, XL, S("product"))

            @block.scalar
            def _(act):
                stream.hi(nc, act, n0 + PARTS)
                for t in range(RW_TILES):
                    act.wait_ge(S("product"), t + 1)
                    nc.scalar.activation(praw[:, t, 1:T + 1], PS[:, t % 4, :], ACT.Copy).then_inc(S("evicted"), 1)
                    stream.hi(nc, act, n0 + min(t + 3, RW_TILES + 1))

            @block.gpsimd
            def _(pool):
                stream.lo(nc, pool, n0 + RW_TILES + 1)

            @block.vector
            def _(dve):
                v = nc.vector
                v.memset(praw[:, :, 0:1], 0.0).then_inc(S("zeroed"), 1)
                dve.wait_ge(S("zeroed"), 1)
                dve.wait_ge(S("par"), 16)
                v.tensor_scalar(oneless[:, :], par[:, PCOL["k_a"]:PCOL["k_a"] + 4], -1.0, 1.0, ALU.mult, ALU.add).then_inc(S("oneless"), 1)
                for t in range(RW_TILES):
                    dve.wait_ge(S("evicted"), t + 1)
                    v.tensor_tensor(XT(13 + t % 4), praw[:, t, 0:T], praw[:, t, 1:T + 1], ALU.subtract).then_inc(S("diff"), 1)
                    dve.wait_ge(S("diff"), t + 1)
                    v.scalar_tensor_tensor(out=M[:, t, :], in0=XT(13 + t % 4), scalar=par_col("mu", t),
                                           in1=praw[:, t, 1:T + 1], op0=ALU.mult, op1=ALU.add).then_inc(S("mixed"), 1)


        SG, LC = XT(13, 4), XT(17, 4)
        AA, TH = XT(21, 4), XT(25)
        PP = X[:, 26 * T:26 * T + 4 * NCH * 65].rearrange("p (c j t) -> p c j t", c=4, j=NCH)
        PI = XT(31, 4)
        KK, TMP = XT(35, 4), XT(39, 4)
        AR = BR[:, 0:8, :].rearrange("p a t -> p (a t)").rearrange("p (c q x t) -> p c q x t", c=4, q=4, x=2)
        BT, KT = BR[:, 8:12, :], BR[:, 12:16, :]
        S, other = stage()
        with nc.Block() as block:
            @block.sync
            def _(sp):
                clear(sp, other)

            @block.tensor
            def _(pe):
                w2a2 = par[:, PCOL["w2a2"]:PCOL["w2a2"] + 512]
                pe.wait_ge(S("tanh"), 1)
                for c in range(4):
                    nc.tensor.matmul(PS[:, c, :], w2a2[0:64, c * P:(c + 1) * P], TH[0:64, :], start=True, stop=True).then_inc(S("lora"), 1)
                for c in range(4):
                    nc.tensor.matmul(PS[:, 4 + c, :], w2a2[64:128, c * P:(c + 1) * P], M[64:128, 12, :], start=True, stop=True).then_inc(S("lora"), 1)
                for c in range(4):
                    pe.wait_ge(S("ksq"), c + 1)
                    pe.wait_ge(S("gates"), 4)
                    nc.tensor.matmul(PS[:, c, :], C("head_ones", P), TMP[:, c, :], start=True, stop=True).then_inc(S("knorm2"), 1)
                for c in range(4):
                    pe.wait_ge(S("rkr"), c + 1)
                    pe.wait_ge(S("gates"), 8)
                    nc.tensor.matmul(PS[:, 4 + c, :], C("head_ones", P), TMP[:, c, :], start=True, stop=True).then_inc(S("bonus_sum"), 1)

            @block.gpsimd
            def _(pool):
                for c in range(4):
                    pool.wait_ge(S("decays"), 2 * c + 2)
                    pool.wait_ge(S("kmod"), c + 1)
                    nc.gpsimd.tensor_tensor(KT[:, c, :], M[:, 4 + c, :], PI[:, c, :], ALU.mult).then_inc(S("k_tilde"), 1)
                    pool.wait_ge(S("b0"), c + 1)
                    nc.gpsimd.tensor_tensor(BT[:, c, :], AA[:, c, :], PI[:, c, :], ALU.mult).then_inc(S("b_tilde"), 1)

            @block.scalar
            def _(act):
                a = nc.scalar
                a.activation(TH[0:64, :], M[0:64, 12, :], ACT.Tanh).then_inc(S("tanh"), 1)
                for c in range(4):
                    act.wait_ge(S("lora"), c + 1)
                    a.activation(SG[:, c, :], PS[:, c, :], ACT.Sigmoid, bias=par_col("w0", c)).then_inc(S("gates"), 1)
                for c in range(4):
                    act.wait_ge(S("lora"), 4 + c + 1)
                    a.activation(AA[:, c, :], PS[:, 4 + c, :], ACT.Sigmoid, bias=par_col("a0", c)).then_inc(S("gates"), 1)
                for c in range(4):
                    act.wait_ge(S("kraw"), c + 1)
                    a.activation(TMP[:, c, :], KK[:, c, :], ACT.Square).then_inc(S("ksq"), 1)
                for c in range(4):
                    act.wait_ge(S("kfloor"), c + 1)
                    a.activation(TMP[:, c, :], TMP[:, c, :], ACT.Ln).then_inc(S("klog"), 1)
                for c in range(4):
                    act.wait_ge(S("klog"), c + 1)
                    act.wait_ge(S("kmod"), c + 1)
                    a.activation(SG[:, c, :], TMP[:, c, :], ACT.Exp, scale=-0.5).then_inc(S("kinv"), 1)
                for c in range(4):
                    act.wait_ge(S("cum"), c + 1)
                    a.activation(PP[:, c, :, 1:65], LC[:, c, :].rearrange("p (j t) -> p j t", j=NCH), ACT.Exp, scale=-EXPH).then_inc(S("decays"), 1)
                    a.activation(PI[:, c, :], LC[:, c, :], ACT.Exp, scale=EXPH).then_inc(S("decays"), 1)

            @block.vector
            def _(dve):
                v = nc.vector
                v.memset(PP[:, :, :, 0:1], 1.0).then_inc(S("first_decay"), 1)
                for c in range(4):
                    v.tensor_scalar(KK[:, c, :], M[:, 4 + c, :], par_col("k_k", c), None, ALU.mult).then_inc(S("kraw"), 1)
                for c in range(4):
                    dve.wait_ge(S("gates"), c + 1)
                    v.tensor_tensor_scan(LC[:, c, :], C("reset", T), SG[:, c, :], 0.0, ALU.mult, ALU.add).then_inc(S("cum"), 1)
                for c in range(4):
                    dve.wait_ge(S("gates"), 4 + c + 1)
                    dve.wait_ge(S("cum"), c + 1)
                    v.tensor_scalar(SG[:, c, :], AA[:, c, :], par_col("k_a", c), oneless[:, c:c + 1], ALU.mult, ALU.add).then_inc(S("kscale"), 1)
                for c in range(4):
                    dve.wait_ge(S("kscale"), c + 1)
                    v.tensor_tensor(M[:, 4 + c, :], M[:, 4 + c, :], SG[:, c, :], ALU.mult).then_inc(S("kmod"), 1)
                for c in range(4):
                    dve.wait_ge(S("knorm2"), c + 1)
                    v.tensor_scalar(TMP[:, c, :], PS[:, c, :], 1e-24, None, ALU.max).then_inc(S("kfloor"), 1)
                for c in range(4):
                    dve.wait_ge(S("kinv"), c + 1)
                    v.tensor_tensor(KK[:, c, :], KK[:, c, :], SG[:, c, :], ALU.mult).then_inc(S("kk"), 1)
                for c in range(4):
                    dve.wait_ge(S("kinv"), 4)
                    dve.wait_ge(S("kmod"), c + 1)
                    v.scalar_tensor_tensor(out=TMP[:, c, :], in0=M[:, c, :], scalar=par_col("r_k", c), in1=M[:, 4 + c, :],
                                           op0=ALU.mult, op1=ALU.mult).then_inc(S("rkr"), 1)
                for c in range(4):
                    dve.wait_ge(S("kk"), c + 1)
                    v.tensor_tensor(AA[:, c, :], AA[:, c, :], KK[:, c, :], ALU.mult).then_inc(S("b0"), 1)
                for c in range(4):
                    dve.wait_ge(S("decays"), 2 * c + 2)
                    dve.wait_ge(S("first_decay"), 1)
                    dve.wait_ge(S("b0"), c + 1)
                    for q in range(4):
                        xa = 1 - q % 2
                        before = PP[:, c, 2 * q:2 * q + 2, 0:64]
                        upto = PP[:, c, 2 * q:2 * q + 2, 1:65]
                        sl = slice(q * P, (q + 1) * P)
                        v.scalar_tensor_tensor(out=AR[:, c, q, xa, :].rearrange("p (j t) -> p j t", j=2),
                                               in0=KK[:, c, sl].rearrange("p (j t) -> p j t", j=2), scalar=-1.0,
                                               in1=before, op0=ALU.mult, op1=ALU.mult).then_inc(S("done"), 1)
                        v.tensor_tensor(AR[:, c, q, 1 - xa, :].rearrange("p (j t) -> p j t", j=2),
                                        M[:, c, sl].rearrange("p (j t) -> p j t", j=2), upto, ALU.mult).then_inc(S("done"), 1)
                for c in range(4):
                    dve.wait_ge(S("bonus_sum"), c + 1)
                    dve.wait_ge(S("done"), 8 * (c + 1))
                    v.tensor_tensor(M[:, c, :], PS[:, 4 + c, :], M[:, 8 + c, :], ALU.mult).then_inc(S("bonus"), 1)


        BON = M[:, 0:4, :]
        VF = M[:, 8:12, :]
        TB, TK, TV = XT(12, 4), XT(16, 4), XT(4, 4)
        GBX = X[:, 42 * T:48 * T].rearrange("p (x h t) -> p h x t", x=3, h=8)
        GK2 = [X[:, a * T:(a + 4) * T].rearrange("p (h x t) -> p h x t", h=8, x=2) for a in (32, 20)]
        DT2 = [X[:, a * T:(a + 2) * T].rearrange("p (h t) -> p h t", h=8) for a in (36, 30)]
        DD, XX, MK = (X[:, a * T:(a + 2) * T].rearrange("p (h t) -> p h t", h=8) for a in (38, 40, 10))
        PC = chunk_decays[:, :].rearrange("p (c j) -> p c j", c=4)
        ST, SN = (XT(i).rearrange("p (c v) -> p c v", c=4) for i in (24, 9))
        ZS, US = XT(25), XT(8)
        S, other = stage()
        with nc.Block() as block:
            @block.sync
            def _(sp):
                clear(sp, other)

            @block.tensor
            def _(pe):
                for i in range(12):
                    src = (BT, KT, VF)[i // 4]
                    if i >= 4:
                        pe.wait_ge(S("tok"), i - 3)
                    for c in range(4):
                        mm = nc.tensor.transpose(PS[:, i % 4, c * P:(c + 1) * P], src[:, c, (i % 4) * P:(i % 4 + 1) * P], ident)
                    mm.then_inc(S("turned"), 1)

            @block.scalar
            def _(act):
                for i in range(12):
                    act.wait_ge(S("turned"), i + 1)
                    dst = (TB, TK, TV)[i // 4]
                    nc.scalar.activation(dst[:, i % 4, :], PS[:, i % 4, :], ACT.Copy).then_inc(S("tok"), 1)

            @block.vector
            def _(dve):
                nc.vector.tensor_copy(PC, PP[:, :, :, 64]).then_inc(S("pc"), 1)
                nc.vector.memset(XT(24), 0.0).then_inc(S("pc"), 1)
                nc.vector.memset(ZS, 0.0).then_inc(S("pc"), 1)
                dve.wait_ge(S("turned"), 12)
                nc.vector.memset(US, 0.0).then_inc(S("pc"), 1)

        YY = XT(26, 4)
        def interleaved(prepare, level, z, u, state):
            prepare(0)
            for lv in range(1, 6):
                level(0, lv)
            for q in range(4):
                ahead = q + 1 < 4
                if ahead:
                    prepare(q + 1)
                for lv, step in enumerate((lambda: z(q, 0), lambda: u(q, 0), lambda: state(q, 0), lambda: z(q, 1), lambda: u(q, 1)), 1):
                    step()
                    if ahead:
                        level(q + 1, lv)
                state(q, 1)

        def nothing(q, j):
            pass

        def md_bank(lv, g):
            return lv % 2 if g == 0 else 1 - lv % 2

        def dxT_bank(g):
            return 7 if g else 2

        def dx_bank(lv, g):
            return lv % 2 if g else 3

        S, other = stage()
        with nc.Block() as block:
            @block.sync
            def _(sp):
                clear(sp, other)

            @block.tensor
            def _(pe):
                def prepare(q):
                    GR, xa = slice(q * P, (q + 1) * P), 1 - q % 2
                    if q:
                        pe.wait_ge(S("invT"), 12 * q)
                    for g in range(2):
                        for which, src in ((0, BT), (1, KT)):
                            for half in range(2):
                                i = 4 * g + 2 * which + half
                                if i >= 4:
                                    pe.wait_ge(S("masked"), 8 * q + i - 3)
                                for hh in range(2):
                                    h = 4 * g + 2 * hh + half
                                    c, b = h // 2, 64 * (h % 2)
                                    mm = nc.tensor.matmul(PS[:, i % 4, hh * 256:(hh + 1) * 256], src[b:b + 64, c, GR],
                                                          AR[b:b + 64, c, q, :, :], start=True, stop=True)
                                mm.then_inc(S("gram"), 1)
                    for g in range(2):
                        if g:
                            pe.wait_ge(S("masked"), 8 * q + 5)
                        for hh in range(4):
                            h = 2 * hh + g
                            c, b = h // 2, 64 * (h % 2)
                            mm = nc.tensor.matmul(PS[:, 0 if g else 7, hh * P:(hh + 1) * P], AR[b:b + 64, c, q, xa, :], BT[b:b + 64, c, GR], start=True, stop=True)
                        mm.then_inc(S("gramM"), 1)
                    pe.wait_ge(S("masked"), 8 * q + 8)

                def level(q, lv):
                    DT = DT2[q % 2]
                    for g in range(2):
                        i = 2 * (lv - 1) + g
                        pe.wait_ge(S("level_mask"), 10 * q + i + 1)
                        pe.wait_ge(S("inv"), 10 * q + i + 1)
                        pe.wait_ge(S("invT"), 12 * q + i + 1)
                        for hh in range(4):
                            h = 2 * hh + g
                            mm = nc.tensor.matmul(PS[:, md_bank(lv, g), hh * P:(hh + 1) * P], MK[:, h, :], DD[:, h, :], start=True, stop=True)
                        mm.then_inc(S("md"), 1)
                    for g in range(2):
                        i = 2 * (lv - 1) + g
                        pe.wait_ge(S("x_out"), 10 * q + i + 1)
                        for hh in range(4):
                            h = 2 * hh + g
                            mm = nc.tensor.matmul(PS[:, dxT_bank(g), hh * P:(hh + 1) * P], XX[:, h, :], DT[:, h, :], start=True, stop=True)
                        mm.then_inc(S("dxT"), 1)
                        if lv < 5:
                            for hh in range(4):
                                h = 2 * hh + g
                                mm = nc.tensor.matmul(PS[:, dx_bank(lv, g), hh * P:(hh + 1) * P], DT[:, h, :], XX[:, h, :], start=True, stop=True)
                            mm.then_inc(S("dx"), 1)

                def z(q, j):
                    n, xa = 2 * q + j, 1 - q % 2
                    R = slice(64 * j, 64 * j + 64)
                    if n:
                        pe.wait_ge(S("state"), 2 * n)
                    for c in range(4):
                        pv = slice(c * P, (c + 1) * P)
                        nc.tensor.matmul(PS[R, 4, pv], AR[:, c, q, xa, R], ST[:, c, :], start=True, stop=False)
                        for h in (2 * c, 2 * c + 1):
                            hv = slice(h * 64, (h + 1) * 64)
                            mm = nc.tensor.matmul(PS[R, 4, hv], GK2[q % 2][:, h, xa, R], TV[:, q, hv], start=False, stop=(h % 2 == 1))
                    mm.then_inc(S("z"), 1)

                def u(q, j):
                    n = 2 * q + j
                    R = slice(64 * j, 64 * j + 64)
                    pe.wait_ge(S("invT"), 12 * (q + 1))
                    pe.wait_ge(S("z_out"), n + 1)
                    for h in range(8):
                        hv = slice(h * 64, (h + 1) * 64)
                        mm = nc.tensor.matmul(PS[R, 4, hv], DT2[q % 2][:, h, R], ZS[:, hv], start=True, stop=True)
                    mm.then_inc(S("u"), 1)

                def state(q, j):
                    n, xa = 2 * q + j, 1 - q % 2
                    R = slice(64 * j, 64 * j + 64)
                    pe.wait_ge(S("u_out"), n + 1)
                    if n:
                        pe.wait_ge(S("y_out"), n)
                    for c in range(4):
                        pv = slice(c * P, (c + 1) * P)
                        nc.tensor.matmul(PS[:, 5, pv], TB[R, q, pv], US[R, pv], start=True, stop=False)
                        mm = nc.tensor.matmul(PS[:, 5, pv], TK[R, q, pv], TV[R, q, pv], start=False, stop=True)
                    mm.then_inc(S("s_new"), 1)
                    for c in range(4):
                        nc.tensor.matmul(PS[:, 6, c * 64:(c + 1) * 64], ST[:, c, :], AR[:, c, q, 1 - xa, R], start=True, stop=False)
                        for h in (2 * c, 2 * c + 1):
                            hb = 64 * (h % 2)
                            hv = slice(h * 64, (h + 1) * 64)
                            o = PS[hb:hb + 64, 6, c * 64:(c + 1) * 64]
                            nc.tensor.matmul(o, US[:, hv], GBX[:, h, 2 * (q % 2), R], start=False, stop=False)
                            mm = nc.tensor.matmul(o, TV[:, q, hv], GK2[q % 2][:, h, 1 - xa, R], start=False, stop=True)
                    mm.then_inc(S("y"), 1)

                interleaved(prepare, level, z, u, state)

            @block.scalar
            def _(act):
                def level(q, lv):
                    for g in range(2):
                        i = 2 * (lv - 1) + g
                        act.wait_ge(S("md"), 10 * q + i + 1)
                        if lv > 1:
                            act.wait_ge(S("dxT"), 10 * q + i - 1)
                            act.wait_ge(S("dx"), 8 * q + i - 1)
                        nc.scalar.activation(XX[:, g::2, :], PS[:, md_bank(lv, g), :].rearrange("p (h t) -> p h t", h=4), ACT.Copy).then_inc(S("x_out"), 1)

                def state(q, j):
                    at = q * P + 64 * j
                    act.wait_ge(S("y"), 2 * q + j + 1)
                    nc.scalar.activation(YY[:, :, at:at + 64], PS[:, 6, 0:256].rearrange("p (c t) -> p c t", c=4), ACT.Copy).then_inc(S("y_out"), 1)

                interleaved(lambda q: None, level, nothing, nothing, state)

            @block.vector
            def _(dve):
                v = nc.vector
                idb = ident[:, None, :].to_broadcast([P, 4, P])

                def mask_of(name, k=0):
                    return C(name, P, k * P)[:, None, :].to_broadcast([P, 4, P])

                def prepare(q):
                    tri = C("tri", 256, P * (q % 2))[:, None, :].to_broadcast([P, 2, 256])
                    for g in range(2):
                        for which in range(2):
                            for half in range(2):
                                i = 4 * g + 2 * which + half
                                h = 4 * g + half
                                dve.wait_ge(S("gram"), 8 * q + i + 1)
                                if which:
                                    v.tensor_tensor(GK2[q % 2][:, h:h + 3:2, :, :].rearrange("p h x t -> p h (x t)"),
                                                    PS[:, i % 4, :].rearrange("p (h x) -> p h x", h=2), tri, ALU.mult).then_inc(S("masked"), 1)
                                else:
                                    v.tensor_tensor(GBX[:, h:h + 3:2, q % 2:q % 2 + 2, :], PS[:, i % 4, :].rearrange("p (h x t) -> p h x t", h=2, x=2),
                                                    tri.rearrange("p h (x t) -> p h x t", x=2), ALU.mult).then_inc(S("masked"), 1)
                    DT = DT2[q % 2]
                    for g in range(2):
                        hs = slice(g, 8, 2)
                        dve.wait_ge(S("gramM"), 2 * q + g + 1)
                        dve.wait_ge(S("masked"), 8 * q + 5 + g)
                        v.tensor_tensor(DD[:, hs, :], PS[:, 0 if g else 7, :].rearrange("p (h t) -> p h t", h=4), mask_of("m0"), ALU.mult).then_inc(S("d_low"), 1)
                        v.tensor_tensor(DT[:, hs, :], GBX[:, hs, 1, :], mask_of("lev"), ALU.mult).then_inc(S("dT_low"), 1)
                        v.tensor_tensor(MK[:, hs, :], GBX[:, hs, 1, :], mask_of("lev", 1), ALU.mult).then_inc(S("level_mask"), 1)
                        dve.wait_ge(S("dT_low"), 2 * q + g + 1)
                        dve.wait_ge(S("d_low"), 2 * q + g + 1)
                        v.tensor_tensor(DD[:, hs, :], DD[:, hs, :], idb, ALU.add).then_inc(S("inv"), 1)
                        v.tensor_tensor(DT[:, hs, :], DT[:, hs, :], idb, ALU.add).then_inc(S("invT"), 1)

                def level(q, lv):
                    DT = DT2[q % 2]
                    for g in range(2):
                        i = 2 * (lv - 1) + g
                        hs = slice(g, 8, 2)
                        if lv < 5:
                            dve.wait_ge(S("md"), 10 * q + i + 1)
                            v.tensor_tensor(MK[:, hs, :], GBX[:, hs, 1, :], mask_of("lev", lv + 1), ALU.mult).then_inc(S("level_mask"), 1)
                    for g in range(2):
                        i = 2 * (lv - 1) + g
                        hs = slice(g, 8, 2)
                        dve.wait_ge(S("dxT"), 10 * q + i + 1)
                        if lv < 5:
                            dve.wait_ge(S("dx"), 8 * q + i + 1)
                        v.tensor_tensor(DT[:, hs, :], DT[:, hs, :], PS[:, dxT_bank(g), :].rearrange("p (h t) -> p h t", h=4), ALU.add).then_inc(S("invT"), 1)
                        if lv < 5:
                            v.tensor_tensor(DD[:, hs, :], DD[:, hs, :], PS[:, dx_bank(lv, g), :].rearrange("p (h t) -> p h t", h=4), ALU.add).then_inc(S("inv"), 1)

                def z(q, j):
                    n, R = 2 * q + j, slice(64 * j, 64 * j + 64)
                    dve.wait_ge(S("z"), n + 1)
                    v.tensor_copy(ZS[R, :], PS[R, 4, :]).then_inc(S("z_out"), 1)

                def u(q, j):
                    n, R = 2 * q + j, slice(64 * j, 64 * j + 64)
                    dve.wait_ge(S("u"), n + 1)
                    v.tensor_copy(US[R, :], PS[R, 4, :]).then_inc(S("u_out"), 1)

                def state(q, j):
                    n = 2 * q + j
                    heads = [(slice(a, a + 64), slice(a, a + 64)) for a in (0, 64)]
                    new = PS[:, 5, :].rearrange("p (c v) -> p c v", c=4)
                    dve.wait_ge(S("s_new"), n + 1)
                    for rows, cols in heads:
                        v.tensor_tensor(SN[rows, :, cols], new[rows, :, cols], ST[rows, :, cols], ALU.add).then_inc(S("s_sum"), 1)
                    dve.wait_ge(S("y"), n + 1)
                    for k, (rows, cols) in enumerate(heads):
                        dve.wait_ge(S("s_sum"), 2 * n + k + 1)
                        v.tensor_tensor(ST[rows, :, cols], SN[rows, :, cols], PC[rows, :, n:n + 1].to_broadcast([64, 4, 64]), ALU.mult).then_inc(S("state"), 1)

                interleaved(prepare, level, z, u, state)

        Y0, YSQ, RV = XT(30, 4), XT(34, 4), XT(38, 4)
        n0 = FIRST["mla"]
        QL, QN = XT(4, 5), XT(9, 5)
        SQ, KP, RST = XT(14, 5), XT(19), XT(20, 2)
        KPR, ROT = XT(22), XT(23, 2)
        QH, KH, VV = XT(30, 8), XT(38, 8), XT(26, 4)
        pe_rows = slice(64, 96)
        S, other = stage()
        with nc.Block() as block:
            @block.sync
            def _(sp):
                clear(sp, other)
                stream.send(sp, n0 + 11 + RING - 1)

            @block.tensor
            def _(pe):
                for c in range(4):
                    nc.tensor.matmul(PS[:, 4 + c, :], C("head_ones", P), YY[:, c, :], start=True, stop=True).then_inc(S("rwkv_sum"), 1)
                for t in range(5):
                    if t == 3:
                        for c in range(4):
                            pe.wait_ge(S("rwkv_sq"), c + 1)
                            nc.tensor.matmul(PS[:, 4 + c, :], C("head_ones", P), YSQ[:, c, :], start=True, stop=True).then_inc(S("rwkv_sumsq"), 1)
                    if t == 4:
                        pe.wait_ge(S("rwkv_log"), 4)
                    gemm3(pe, t, n0 + t, XH, XL, S("latent"))
                gemm3(pe, 5, n0 + 5, XH, XL, S("latent"))
                pe.wait_ge(S("kpe"), 1)
                nc.tensor.matmul(PS[64:96, 6, :], cst[64:96, CCOL["swap"]:CCOL["swap"] + 32], KP[pe_rows, :], start=True, stop=True).then_inc(S("swapped"), 1)
                for t in range(5):
                    pe.wait_ge(S("sq"), t + 1)
                    pe.wait_ge(S("evicted"), t + 1)
                    bank = 0 if t < 3 else 1
                    mm = nc.tensor.matmul(PS[:, bank, :], C("ones", P), SQ[:, t, :], start=t in (0, 3), stop=t in (2, 4))
                    if t in (2, 4):
                        mm.then_inc(S("sumsq"), 1)
                pe.wait_ge(S("normed"), 5)
                for h in range(8):
                    n = n0 + 6 + h // 3
                    if h % 3 == 0:
                        stream.wait(pe, n)
                    if h >= 2:
                        pe.wait_ge(S("q_out"), h - 1)
                    for k in range(3):
                        mm = nc.tensor.matmul(PS[0:96, 2 + h % 2, :], stream.chunk(n)[:, (h % 3) * 288 + k * 96:(h % 3) * 288 + (k + 1) * 96],
                                              QN[:, k, :], start=(k == 0), stop=(k == 2))
                        if h % 3 == 0 and k == 0:
                            mm.then_inc(used, 1)
                    mm.then_inc(S("q"), 1)
                n = n0 + 9
                stream.wait(pe, n)
                for h in range(8):
                    pe.wait_ge(S("q_out"), h + 1)
                    if h >= 2:
                        pe.wait_ge(S("q_rot"), h - 1)
                    nc.tensor.matmul(PS[pe_rows, 6 + h % 2, :], cst[64:96, CCOL["swap"]:CCOL["swap"] + 32], QH[pe_rows, h, :],
                                     start=True, stop=True).then_inc(S("q_swapped"), 1)
                    if h >= 2:
                        pe.wait_ge(S("k_out"), h - 1)
                    for k in range(2):
                        mm = nc.tensor.matmul(PS[0:64, 4 + h % 2, :], stream.chunk(n)[:, h * 128 + k * 64:h * 128 + (k + 1) * 64],
                                              QN[:, 3 + k, :], start=(k == 0), stop=(k == 1))
                        if h == 0 and k == 0:
                            mm.then_inc(used, 1)
                    mm.then_inc(S("k"), 1)
                n = n0 + 10
                stream.wait(pe, n)
                pe.wait_ge(S("rms"), 2)
                for q in range(4):
                    if q >= 2:
                        pe.wait_ge(S("v_out"), q - 1)
                    for k in range(2):
                        mm = nc.tensor.matmul(PS[:, q % 2, :], QN[:, 3 + k, q * P:(q + 1) * P], stream.chunk(n)[:, k * 512:(k + 1) * 512],
                                              start=(k == 0), stop=(k == 1))
                        if q == 0 and k == 0:
                            mm.then_inc(used, 1)
                    mm.then_inc(S("v"), 1)

            @block.scalar
            def _(act):
                a = nc.scalar
                stream.hi(nc, act, n0 + PARTS)
                for c in range(4):
                    act.wait_ge(S("rwkv_centred"), c + 1)
                    a.activation(YSQ[:, c, :], Y0[:, c, :], ACT.Square).then_inc(S("rwkv_sq"), 1)
                for t in range(5):
                    if t == 3:
                        for c in range(4):
                            act.wait_ge(S("rwkv_sumsq"), c + 1)
                            a.activation(YSQ[:, c, :], PS[:, 4 + c, :], ACT.Ln, scale=1.0 / HD, bias=C("eps", 1, 0)).then_inc(S("rwkv_log"), 1)
                        for c in range(4):
                            act.wait_ge(S("rwkv_log"), c + 1)
                            a.activation(RV[:, c, :], YSQ[:, c, :], ACT.Exp, scale=-0.5).then_inc(S("rwkv_rstd"), 1)
                    act.wait_ge(S("latent"), t + 1)
                    a.activation(QL[:, t, :], PS[:, t, :], ACT.Copy).then_inc(S("evicted"), 1)
                    a.activation(SQ[:, t, :], PS[:, t, :], ACT.Square).then_inc(S("sq"), 1)
                    stream.hi(nc, act, n0 + min(t + 3, 6))
                for c in range(4):
                    act.wait_ge(S("rwkv_normed"), c + 1)
                    a.activation(YY[:, c, :], Y0[:, c, :], ACT.Identity, scale=par_col("lnx_g", c), bias=par_col("lnx_b", c)).then_inc(S("rwkv_affine"), 1)
                act.wait_ge(S("latent"), 6)
                a.activation(KP[pe_rows, :], PS[pe_rows, 5, :], ACT.Copy).then_inc(S("kpe"), 1)
                for i, width in enumerate((384, 256)):
                    act.wait_ge(S("sumsq"), i + 1)
                    a.activation(RST[:, i, :], PS[:, i, :], ACT.Ln, scale=1.0 / width, bias=C("eps", 1, 1)).then_inc(S("log"), 1)
                for i in range(2):
                    act.wait_ge(S("log"), i + 1)
                    a.activation(RST[:, i, :], RST[:, i, :], ACT.Exp, scale=-0.5).then_inc(S("rms"), 1)
                act.wait_ge(S("rwkv_branch"), 4)
                for h in range(8):
                    act.wait_ge(S("q"), h + 1)
                    a.activation(QH[0:96, h, :], PS[0:96, 2 + h % 2, :], ACT.Copy).then_inc(S("q_out"), 1)
                for h in range(8):
                    act.wait_ge(S("k"), h + 1)
                    a.activation(KH[0:64, h, :], PS[0:64, 4 + h % 2, :], ACT.Copy).then_inc(S("k_out"), 1)
                for q in range(4):
                    act.wait_ge(S("v"), q + 1)
                    a.activation(VV[:, q, :], PS[:, q % 2, :], ACT.Copy).then_inc(S("v_out"), 1)
                stream.hi(nc, act, n0 + 11 + 1)

            @block.vector
            def _(dve):
                v = nc.vector
                for c in range(4):
                    dve.wait_ge(S("rwkv_sum"), c + 1)
                    v.scalar_tensor_tensor(out=Y0[:, c, :], in0=PS[:, 4 + c, :], scalar=-1.0 / HD, in1=YY[:, c, :], op0=ALU.mult, op1=ALU.add).then_inc(S("rwkv_centred"), 1)
                for c in range(4):
                    dve.wait_ge(S("rwkv_rstd"), c + 1)
                    v.tensor_tensor(Y0[:, c, :], Y0[:, c, :], RV[:, c, :], ALU.mult).then_inc(S("rwkv_normed"), 1)
                for c in range(4):
                    dve.wait_ge(S("rwkv_affine"), c + 1)
                    v.tensor_tensor(BR[:, c, :], YY[:, c, :], BON[:, c, :], ALU.add).then_inc(S("rwkv_branch"), 1)
                cos, sin = rope[pe_rows, 0, :], rope[pe_rows, 1, :]
                dve.wait_ge(S("kpe"), 1)
                v.tensor_tensor(KPR[pe_rows, :], KP[pe_rows, :], cos, ALU.mult).then_inc(S("kp_cos"), 1)
                dve.wait_ge(S("swapped"), 1)
                v.tensor_tensor(ROT[pe_rows, 0, :], PS[pe_rows, 6, :], sin, ALU.mult).then_inc(S("kp_sin"), 1)
                dve.wait_ge(S("kp_sin"), 1)
                v.tensor_tensor(KPR[pe_rows, :], KPR[pe_rows, :], ROT[pe_rows, 0, :], ALU.add).then_inc(S("kp_rot"), 1)
                for t in range(5):
                    dve.wait_ge(S("rms"), 1 if t < 3 else 2)
                    dve.wait_ge(S("evicted"), t + 1)
                    v.scalar_tensor_tensor(out=QN[:, t, :], in0=QL[:, t, :], scalar=par_col("q_norm", t), in1=RST[:, 0 if t < 3 else 1, :],
                                           op0=ALU.mult, op1=ALU.mult).then_inc(S("normed"), 1)
                dve.wait_ge(S("kp_rot"), 1)
                for h in range(8):
                    i = h % 2
                    dve.wait_ge(S("q_swapped"), h + 1)
                    if h >= 2:
                        dve.wait_ge(S("q_done"), h - 1)
                    v.tensor_tensor(ROT[pe_rows, i, :], PS[pe_rows, 6 + i, :], sin, ALU.mult).then_inc(S("q_rot"), 1)
                    v.tensor_tensor(QH[pe_rows, h, :], QH[pe_rows, h, :], cos, ALU.mult).then_inc(S("q_cos"), 1)
                    dve.wait_ge(S("q_cos"), h + 1)
                    v.tensor_tensor(QH[pe_rows, h, :], QH[pe_rows, h, :], ROT[pe_rows, i, :], ALU.add).then_inc(S("q_done"), 1)

            @block.gpsimd
            def _(pool):
                stream.lo(nc, pool, n0 + 6)
                pool.wait_ge(S("kp_rot"), 1)
                pool.wait_ge(S("rwkv_branch"), 4)
                for h in range(8):
                    nc.gpsimd.tensor_copy(KH[pe_rows, h, :], KPR[pe_rows, :]).then_inc(S("kp_copied"), 1)
                pool.wait_ge(S("kp_copied"), 8)
                stream.lo(nc, pool, n0 + 11 + 1)

        attention(nc, stage, PS, ident, C("causal", P), heads=8, dv=64, rows=96, blocks=4,
                  query=lambda h: QH[0:96, h, :], key=lambda h: KH[0:96, h, :],
                  value=lambda h, kb: VV[:, kb, h * 64:(h + 1) * 64], nkeys=[128, 256, 384, 512],
                  scale=96.0 ** -0.5, out=lambda h: BR[64 * (h % 2):64 * (h % 2) + 64, 4 + h // 2, :],
                  probs=[XT(0), XT(1), XT(2)], probsT=[XT(4, 4), XT(8, 4)], small=XT(14), part=lambda h: 64 * (h % 2))

        n0, nx, ng = FIRST["conv"], FIRST["xattn"], FIRST["gates"]
        H0 = X[:, 0:4 * (T + TAPS - 1)].rearrange("p (c t) -> p c t", c=4)
        SGM, ACC, Y0, SQ, RST = XT(5, 4), XT(9, 4), XT(13, 4), XT(17, 4), XT(21)
        QX, KX, VX = XT(22, 4), X[:, 26 * T:28 * T].rearrange("p (h t) -> p h t", h=4), XT(28, 2)
        memT = XT(44, 8, MEM)
        GNOW, GLATER = XT(30, 4), XT(34, 8)
        S, other = stage()
        with nc.Block() as block:
            @block.sync
            def _(sp):
                clear(sp, other)
                sp.dma_start(X[:, 44 * T:48 * T], A["memT"]).then_inc(S("mem"), 16)
                stream.send(sp, ng + 16 + RING - 1)
                sp.wait_ge(S("mem"), 16)

            @block.tensor
            def _(pe):
                for t in range(8):
                    gemm3(pe, t, n0 + t, XH, XL, S("u"))
                pe.wait_ge(S("mem"), 16)
                for t in range(8):
                    if t < 4:
                        pe.wait_ge(S("gate"), t + 1)
                    else:
                        pe.wait_ge(S("evicted"), t - 3)
                    if t < 4:
                        gemm3(pe, 4 + t % 4, nx + t, XH, XL, S("product"))
                    else:
                        gemm(pe, 4 + t % 4, nx + t, memT[:, :, :], S("product"))
                pe.wait_ge(S("glu"), 4)
                for kc in range(4):
                    n = nx + 8 + kc
                    stream.wait(pe, n)
                    for q in range(2):
                        for k in range(2):
                            mm = nc.tensor.matmul(PS[:, 2 + q, :], memT[:, 2 * kc + k, q * P:(q + 1) * P], stream.chunk(n)[:, k * 512:(k + 1) * 512],
                                                  start=(kc == 0 and k == 0), stop=(kc == 3 and k == 1))
                            if q == 0 and k == 0:
                                mm.then_inc(used, 1)
                        if kc == 3:
                            mm.then_inc(S("product"), 1)
                for t in range(16):
                    if t < 4:
                        pe.wait_ge(S("evicted"), 5 + t)
                    else:
                        pe.wait_ge(S("silu"), t - 3)
                    gemm3(pe, 4 + t % 4, ng + t, XH, XL, S("gate_product"))
                for c in range(4):
                    pe.wait_ge(S("conv"), c + 1)
                    mm = nc.tensor.matmul(PS[:, 0, :], C("ones", P), ACC[:, c, :], start=(c == 0), stop=(c == 3))
                mm.then_inc(S("sum"), 1)
                for c in range(4):
                    pe.wait_ge(S("sq"), c + 1)
                    mm = nc.tensor.matmul(PS[:, 1, :], C("ones", P), SQ[:, c, :], start=(c == 0), stop=(c == 3))
                mm.then_inc(S("sumsq"), 1)

            @block.scalar
            def _(act):
                a = nc.scalar
                stream.hi(nc, act, n0 + 7)
                for c in range(4):
                    act.wait_ge(S("u"), 4 + c + 1)
                    a.activation(SGM[:, c, :], PS[:, 4 + c, :], ACT.Sigmoid).then_inc(S("gate"), 1)
                    stream.hi(nc, act, n0 + 8 + c)
                for t in range(10):
                    if t < 2:
                        stream.hi(nc, act, n0 + 11 + t)
                    if t == 9:
                        stream.hi(nc, act, ng + 1)
                    act.wait_ge(S("product"), t + 1)
                    dst, src = ((QX[:, t, :], PS[:, 4 + t % 4, :]) if t < 4 else (KX[:, t - 4, :], PS[:, 4 + t % 4, 0:MEM]) if t < 8
                                else (VX[:, t - 8, :], PS[:, 2 + t - 8, :]))
                    a.activation(dst, src, ACT.Copy).then_inc(S("evicted"), 1)
                stream.hi(nc, act, ng + 2)
                for t in range(16):
                    act.wait_ge(S("gate_product"), t + 1)
                    if 4 <= t < 8:
                        act.wait_ge(S("gated"), t - 3)
                    a.activation(GNOW[:, t % 4, :] if t < 8 else GLATER[:, t - 8, :], PS[:, 4 + t % 4, :], ACT.Silu).then_inc(S("silu"), 1)
                    stream.hi(nc, act, ng + min(t + 3, 16 + 1))
                for c in range(4):
                    act.wait_ge(S("centred"), c + 1)
                    a.activation(SQ[:, c, :], Y0[:, c, :], ACT.Square).then_inc(S("sq"), 1)
                act.wait_ge(S("sumsq"), 1)
                a.activation(RST, PS[:, 1, :], ACT.Ln, scale=1.0 / W, bias=C("eps", 1, 2)).then_inc(S("log"), 1)
                act.wait_ge(S("log"), 1)
                a.activation(RST, RST, ACT.Exp, scale=-0.5).then_inc(S("rstd"), 1)
                for c in range(4):
                    act.wait_ge(S("normed"), c + 1)
                    a.activation(BR[:, 8 + c, :], Y0[:, c, :], ACT.Silu, scale=par_col("cln_g", c), bias=par_col("cln_b", c)).then_inc(S("branch"), 1)

            @block.vector
            def _(dve):
                v = nc.vector
                v.memset(H0[:, :, 0:TAPS - 1], 0.0).then_inc(S("pad"), 1)
                for c in range(4):
                    dve.wait_ge(S("gate"), c + 1)
                    v.tensor_tensor(H0[:, c, TAPS - 1:], PS[:, c, :], SGM[:, c, :], ALU.mult).then_inc(S("glu"), 1)
                dve.wait_ge(S("pad"), 1)
                dve.wait_ge(S("glu"), 4)
                for tap in range(TAPS):
                    for c in range(4):
                        w = par_col("conv_w", c * TAPS + tap)
                        if tap == 0:
                            ins = v.tensor_scalar(ACC[:, c, :], H0[:, c, 0:T], w, par_col("conv_b", c), ALU.mult, ALU.add)
                        else:
                            dve.wait_ge(S("tap"), 4 * (tap - 1) + c + 1)
                            ins = v.scalar_tensor_tensor(out=ACC[:, c, :], in0=H0[:, c, tap:tap + T], scalar=w, in1=ACC[:, c, :],
                                                         op0=ALU.mult, op1=ALU.add)
                        ins.then_inc(S("conv") if tap == TAPS - 1 else S("tap"), 1)
                dve.wait_ge(S("sum"), 1)
                dve.wait_ge(S("conv"), 4)
                for c in range(4):
                    v.scalar_tensor_tensor(out=Y0[:, c, :], in0=PS[:, 0, :], scalar=-1.0 / W, in1=ACC[:, c, :], op0=ALU.mult, op1=ALU.add).then_inc(S("centred"), 1)
                dve.wait_ge(S("rstd"), 1)
                dve.wait_ge(S("centred"), 4)
                for c in range(4):
                    dve.wait_ge(S("sq"), c + 1)
                    v.tensor_tensor(Y0[:, c, :], Y0[:, c, :], RST, ALU.mult).then_inc(S("normed"), 1)

            @block.gpsimd
            def _(pool):
                stream.lo(nc, pool, ng + 2)
                for t in range(16):
                    if t < 8:
                        pool.wait_ge(S("silu"), t + 1)
                        nc.gpsimd.tensor_tensor(BR[:, t, :], BR[:, t, :], GNOW[:, t % 4, :], ALU.mult).then_inc(S("gated"), 1)
                    stream.lo(nc, pool, ng + min(t + 3, 16 + 1))

        attention(nc, stage, PS, ident, None, heads=4, dv=128, rows=128, blocks=4,
                  query=lambda h: QX[:, h, :], key=lambda h: KX[:, h, :],
                  value=lambda h, kb: VX[:, kb, h * P:(h + 1) * P], nkeys=[256] * 4,
                  scale=128.0 ** -0.5, out=lambda h: BR[:, 12 + h, :],
                  probs=[XT(0), XT(1), XT(2)], probsT=[XT(4, 4), XT(8, 4)], small=XT(14), part=lambda h: 0)

        n0 = FIRST["merge"]
        MG = XT(12, 8)

        def gate_chunk(i):
            return n0 + 6 * (i // 4) + 3 * (i % 4 // 2) + 1 + i % 2
        AD = X[:, 4 * T:4 * T + 96].rearrange("p (m c) -> p m c", c=2)
        CB = X[:, 30 * T:34 * T].rearrange("p (c k) -> p c k", c=2)
        PROD = X[:, 28 * T:30 * T]

        def rows_of(t):
            return X[:, (20 + 2 * (t % 4)) * T:(22 + 2 * (t % 4)) * T]

        S, other = stage()
        with nc.Block() as block:
            @block.sync
            def _(sp):
                clear(sp, other)
                for c in range(2):
                    sp.dma_start(CB[:, c, :], A["cond"][c].partition_broadcast(P)).then_inc(S("cond"), 16)
                for t in range(48):
                    stream.send(sp, n0 + t + RING)
                    if t >= 4:
                        sp.wait_ge(S("ada"), 2 * (t - 3))
                    sp.dma_start(rows_of(t), A["ada"][bass.ds(layer, 1), t, :, :].rearrange("l p c -> p (l c)")).then_inc(S(f"rows{t % 4}"), 16)

            @block.tensor
            def _(pe):
                for m in range(8):
                    for n in range(4):
                        i = 4 * m + n
                        o = n0 + 6 * m + 3 * (n // 2)
                        if i >= 4:
                            pe.wait_ge(S("weighted"), i - 3)
                        if n % 2 == 0:
                            stream.wait(pe, o)
                        bank = 4 + i % 4
                        if n % 2 == 0:
                            for nn in (n, n + 1):
                                if 4 * m + nn >= 4:
                                    pe.wait_ge(S("weighted"), 4 * m + nn - 3)
                                if m == 0 and nn >= 2:
                                    pe.wait_ge(S("gated"), 4 * (nn - 1))
                                for k in range(4):
                                    mm = nc.tensor.matmul(PS[:, 4 + (4 * m + nn) % 4, :], stream.chunk(o)[:, (nn % 2) * 512 + k * P:(nn % 2) * 512 + (k + 1) * P],
                                                          BR[:, 4 * nn + k, :], start=(k == 0), stop=(k == 3))
                                    if nn == n and k == 0:
                                        mm.then_inc(used, 1)
                                mm.then_inc(S("product"), 1)
                        if i >= 4:
                            pe.wait_ge(S("gate"), i - 3)
                        gemm3(pe, i % 4, gate_chunk(i), XH, XL, S("gate_product"))

            @block.scalar
            def _(act):
                stream.hi(nc, act, gate_chunk(1) + 1)
                act.wait_ge(S("cond"), 32)
                nc.scalar.activation(CB, CB, ACT.Silu).then_inc(S("silu_c"), 1)
                for i in range(32):
                    act.wait_ge(S("gate_product"), i + 1)
                    if i >= 4:
                        act.wait_ge(S("weighted"), i - 3)
                    nc.scalar.activation(XT(i % 4), PS[:, i % 4, :], ACT.Sigmoid, bias=par_col("b_gate", 8 * (i % 4) + i // 4)).then_inc(S("gate"), 1)
                    stream.hi(nc, act, min(gate_chunk(i + 2) + 1, n0 + 48))

            @block.vector
            def _(dve):
                v = nc.vector
                for i in range(32):
                    m, n = i // 4, i % 4
                    dve.wait_ge(S("gate"), i + 1)
                    dve.wait_ge(S("product"), i + 1)
                    dst = MG[:, m, :] if n == 0 else XT(8 + i % 4)
                    if i >= 4 and n:
                        dve.wait_ge(S("merged"), 3 * m - 3 + n)
                    v.tensor_tensor(dst, PS[:, 4 + i % 4, :], XT(i % 4), ALU.mult).then_inc(S("weighted"), 1)
                    if n:
                        dve.wait_ge(S("weighted"), i + 1)
                        if n > 1:
                            dve.wait_ge(S("merged"), 3 * m + n - 1)
                        v.tensor_tensor(MG[:, m, :], MG[:, m, :], XT(8 + i % 4), ALU.add).then_inc(S("merged"), 1)
                    if i == 0:
                        dve.wait_ge(S("silu_c"), 1)
                    for t in range(min(48, 48 * i // 28), min(48, 48 * (i + 1) // 28)):
                        dve.wait_ge(S(f"rows{t % 4}"), 16 * (t // 4 + 1))
                        for c in range(2):
                            if 2 * t + c:
                                dve.wait_ge(S("ada"), 2 * t + c)
                            v.tensor_tensor_reduce(PROD, rows_of(t), CB[:, c, :], 1.0, 0.0, ALU.mult, ALU.add, AD[:, t, c:c + 1]).then_inc(S("ada"), 1)
                dve.wait_ge(S("ada"), 96)
                v.tensor_copy(mods[:, bass.ds(layer, 1), :].rearrange("p l m -> p (l m)"), X[:, 4 * T:4 * T + 96]).then_inc(S("mods"), 1)

            @block.gpsimd
            def _(pool):
                stream.lo(nc, pool, gate_chunk(1) + 1)
                for t in range(8):
                    nc.gpsimd.tensor_tensor(BR[:, 8 + t, :], BR[:, 8 + t, :], GLATER[:, t, :], ALU.mult).then_inc(S("gated"), 1)
                    if t == 3:
                        stream.lo(nc, pool, gate_chunk(2) + 1)
                stream.lo(nc, pool, n0 + 48)

        n0 = FIRST["out"]
        RR, SQ, RST = XT(0, 8), XT(8, 8), XT(16)
        S, other = stage()
        with nc.Block() as block:
            @block.sync
            def _(sp):
                clear(sp, other)
                stream.send(sp, n0 + 8)

            @block.tensor
            def _(pe):
                for t in range(8):
                    if t >= 4:
                        pe.wait_ge(S("residual"), t - 3)
                    gemm(pe, t % 4, n0 + t, MG, S("product"))
                for t in range(8):
                    pe.wait_ge(S("residual"), t + 1)
                    mm = nc.tensor.matmul(PS[:, 4, :], C("ones", P), RR[:, t, :], start=(t == 0), stop=(t == 7))
                mm.then_inc(S("sum"), 1)
                for t in range(8):
                    pe.wait_ge(S("sq"), t + 1)
                    mm = nc.tensor.matmul(PS[:, 5, :], C("ones", P), SQ[:, t, :], start=(t == 0), stop=(t == 7))
                mm.then_inc(S("sumsq"), 1)

            @block.scalar
            def _(act):
                a = nc.scalar
                for t in range(8):
                    act.wait_ge(S("centred"), t + 1)
                    a.activation(SQ[:, t, :], RR[:, t, :], ACT.Square).then_inc(S("sq"), 1)
                act.wait_ge(S("sumsq"), 1)
                a.activation(RST, PS[:, 5, :], ACT.Ln, scale=1.0 / D, bias=C("eps", 1, 2)).then_inc(S("log"), 1)
                act.wait_ge(S("log"), 1)
                a.activation(RST, RST, ACT.Exp, scale=-0.5).then_inc(S("rstd"), 1)
                for t in range(8):
                    act.wait_ge(S("normed"), t + 1)
                    a.activation(SQ[:, t, :], RR[:, t, :], ACT.Identity, scale=par_col("ln_g", t), bias=par_col("ln_b", t)).then_inc(S("x_new"), 1)

            @block.gpsimd
            def _(pool):
                for t in range(0, 6, 2):
                    pool.wait_ge(S("x_high"), t + 1)
                    nc.gpsimd.tensor_tensor(XL[:, t, :], SQ[:, t, :], xh[:, t, :], ALU.subtract).then_inc(S("x_low_pool"), 1)

            @block.vector
            def _(dve):
                v = nc.vector
                for t in range(8):
                    dve.wait_ge(S("product"), t + 1)
                    v.scalar_tensor_tensor(out=RR[:, t, :], in0=xh[:, t, :], scalar=DEEP_ALPHA, in1=PS[:, t % 4, :], op0=ALU.mult, op1=ALU.add).then_inc(S("residual_high"), 1)
                    dve.wait_ge(S("residual_high"), t + 1)
                    v.scalar_tensor_tensor(out=RR[:, t, :], in0=XL[:, t, :].bitcast(F32), scalar=DEEP_ALPHA, in1=RR[:, t, :], op0=ALU.mult, op1=ALU.add).then_inc(S("residual"), 1)
                dve.wait_ge(S("sum"), 1)
                for t in range(8):
                    v.scalar_tensor_tensor(out=RR[:, t, :], in0=PS[:, 4, :], scalar=-1.0 / D, in1=RR[:, t, :], op0=ALU.mult, op1=ALU.add).then_inc(S("centred"), 1)
                dve.wait_ge(S("rstd"), 1)
                for t in range(8):
                    dve.wait_ge(S("sq"), t + 1)
                    v.tensor_tensor(RR[:, t, :], RR[:, t, :], RST, ALU.mult).then_inc(S("normed"), 1)

                def low(t):
                    if t % 2 or t == 6:
                        dve.wait_ge(S("x_high"), t + 1)
                        v.tensor_tensor(XL[:, t, :], SQ[:, t, :], xh[:, t, :], ALU.subtract).then_inc(S("x_low"), 1)

                for t in range(8):
                    dve.wait_ge(S("x_new"), t + 1)
                    v.tensor_copy(XH[:, t, :], SQ[:, t, :]).then_inc(S("x_high"), 1)
                    if t:
                        low(t - 1)
                low(7)

        S, other = stage()
        with nc.Block() as block:
            @block.sync
            def _(sp):
                clear(sp, other)
                clear(sp, WR[3])
                clear(sp, WR[4:])


CKV = CTX + T
FF = 2816
FT = FF // P
XB = T + 16
PCOL2 = {}
_at = 0
for _name, _n in (("g_mix", 8), ("g_ffn", 8), ("b_ada", 48), ("q_gain", 1), ("k_gain", 1), ("pool_scale", 2),
                  ("w_pool", 256), ("w_four", 256)):
    PCOL2[_name] = _at
    _at += _n
NPAR2 = _at
CCOL2 = {}
_at = 0
for _name, _n in (("ident", 128), ("head_ones", 128), ("ones", 128), ("swap", 128), ("eps", 1), ("cos", T), ("sin", T), ("cs64", 256),
                  ("count_x", 2 * T), ("count_c", 2 * CTX)):
    CCOL2[_name] = _at
    _at += _n
NCST2 = _at
FH = FT // 2
STAGE_CHUNKS2 = (("in", 11), ("out", 8), ("up0", 2 * FH), ("down0", FH), ("up1", 2 * FH), ("down1", FH))
FIRST2 = {}
_at = 0
for _name, _n in STAGE_CHUNKS2:
    FIRST2[_name] = _at
    _at += _n
NCHUNK2 = _at


def second(nc, ctx, A, PS, XH, XL, WR, mods, stage, constants, stored):
    def sb(name, shape, dt=F32):
        return ctx.enter_context(nc.sbuf_tensor(name, shape, dt))

    cst = sb("cst2", [P, NCST2])
    par = sb("par2", [P, NPAR2])
    cT = sb("cT", [P, DK, CTX])
    mod = sb("mod", [P, 48, 2])
    gain = sb("gain", [P, 2, 8, 2])
    xT = sb("xT", [P, DK, T])

    def C(name, n=1, k=0):
        a = CCOL2[name] + k
        return cst[:, a:a + n]

    def par_col(name, k=0, n=1):
        a = PCOL2[name] + k
        return par[:, a:a + n]

    def tiles_of(X, i, n=1, w=T):
        a = X[:, i * T:i * T + n * w]
        return a if n == 1 else a.rearrange("p (n t) -> p n t", n=n)

    ident = C("ident", P)
    eps = C("eps")
    early = CCOL2["cos"]
    SH1, SC1, GA1, SH2, SC2, GA2 = (8 * i for i in range(6))

    S, other = stage()
    with nc.Block() as block:
        @block.sync
        def _(sp):
            clear(sp, other)
            sp.dma_start(cst[:, 0:early], A["cst2"][:, 0:early]).then_inc(S("in"), 16)
            sp.dma_start(cT[:, :, :].rearrange("p k t -> p (k t)"), A["ctxT"]).then_inc(S("in"), 16)
            sp.dma_start(cst[:, early:NCST2], A["cst2"][:, early:NCST2]).then_inc(constants, 16)
            sp.wait_ge(S("in"), 32)

        @block.vector
        def _(dve):
            for t in range(0, DK, 2):
                nc.vector.tensor_tensor(xT[:, t:t + 2, :], XH[:, t:t + 2, :].bitcast(F32), XL[:, t:t + 2, :].bitcast(F32), ALU.add).then_inc(S("x_whole"), 1)

    for layer in range(LAYERS):
        update = layer < LAYERS - 1
        stream = Stream(WR, lambda n: A["w2"][layer, n, :, :], list(range(NCHUNK2)))
        used = WR[4]
        room = ExitStack()
        mixed = room.enter_context(nc.sbuf_tensor(f"mixed{layer}", [P, 12 * T], F32))
        lower = ExitStack()
        Y = lower.enter_context(nc.sbuf_tensor(f"tiles{layer}", [P, 32 * T], F32))
        above = ExitStack()
        HC, HCL = (above.enter_context(nc.sbuf_tensor(f"context_{part}{layer}", [P, DK, CTX], F32R))[:, :, :] for part in ("high", "low"))

        def XT(i, n=1, w=T):
            return tiles_of(Y, i, n, w)

        streams = [dict(name="x", n=T, src=xT, h=XH, l=XL, k=0, bank=0), dict(name="c", n=CTX, src=cT, h=HC, l=HCL, k=1, bank=4)]

        def mark(n, first):
            return used if n and first else None

        def gemm(pe, n, outs, ready=None):
            stream.wait_split(pe, n)
            for i, (ps, high, low, done) in enumerate(outs):
                for k in range(DK):
                    if ready is not None:
                        ready(pe, full[i], k)
                    mm = three(nc, ps, tile_of(stream.high(n), k), tile_of(stream.low(n), k), high[:, k, :], low[:, k, :],
                               k == 0, k == DK - 1, mark(n, i == 0 and k == 0))
                mm.then_inc(done, 1)

        S, other = stage()
        with nc.Block() as block:
            @block.sync
            def _(sp):
                clear(sp, other)
                sp.dma_start(par[:, :], A["par2"][layer]).then_inc(S("par"), 16)
                stream.send(sp, RING)
                sp.wait_ge(S("par"), 16)

            @block.vector
            def _(dve):
                v = nc.vector
                dve.wait_ge(S("par"), 16)
                v.tensor_tensor(mod[:, :, :], mods[:, layer, :].rearrange("p (m c) -> p m c", m=48),
                                par_col("b_ada", 0, 48)[:, :, None].to_broadcast([P, 48, 2]), ALU.add).then_inc(S("mod"), 1)
                dve.wait_ge(S("mod"), 1)
                for i, (sc, g) in enumerate(((SC1, "g_mix"), (SC2, "g_ffn"))):
                    v.tensor_scalar(gain[:, i, :, :], mod[:, sc:sc + 8, :], 1.0, None, ALU.add).then_inc(S("one_plus"), 1)
                dve.wait_ge(S("one_plus"), 2)
                for i, (sc, g) in enumerate(((SC1, "g_mix"), (SC2, "g_ffn"))):
                    v.tensor_tensor(gain[:, i, :, :], gain[:, i, :, :], par_col(g, 0, 8)[:, :, None].to_broadcast([P, 8, 2]), ALU.mult).then_inc(S("gain"), 1)

        class Norm:

            def __init__(self, S, which, shift, sts, scratch):
                self.S, self.which, self.shift, self.sts = S, which, shift, sts
                self.slots = {"x": tiles_of(scratch, 0, 4), "c": tiles_of(scratch, 4, 4, CTX)}
                self.inverse = {"x": tiles_of(scratch, 6), "c": tiles_of(scratch, 7)[:, 0:CTX]}

            def tensor(self, pe):
                for s in self.sts:
                    nm, n = s["name"], s["n"]
                    for t in range(DK):
                        pe.wait_ge(self.S("sq" + nm), t + 1)
                        nc.tensor.matmul(PS[:, s["bank"], 0:n], C("ones", P), self.slots[nm][:, t % 4, :], start=(t == 0), stop=(t == DK - 1)).then_inc(self.S("summed" + nm), 1)

            def scalar(self, act, upto):
                a, S = nc.scalar, self.S

                def squares(s, tiles):
                    nm = s["name"]
                    for t in tiles:
                        if t >= 4:
                            act.wait_ge(S("summed" + nm), t - 3)
                        a.activation(self.slots[nm][:, t % 4, :], s["src"][:, t, :], ACT.Square).then_inc(S("sq" + nm), 1)

                def deviation(s):
                    nm, n = s["name"], s["n"]
                    act.wait_ge(S("summed" + nm), DK)
                    a.activation(self.inverse[nm], PS[:, s["bank"], 0:n], ACT.Ln, scale=1.0 / D, bias=eps).then_inc(S("log" + nm), 1)
                    act.wait_ge(S("log" + nm), 1)
                    a.activation(self.inverse[nm], self.inverse[nm], ACT.Exp, scale=-0.5).then_inc(S("rstd" + nm), 1)

                def shifted(s):
                    nm = s["name"]
                    for t in range(DK):
                        act.wait_ge(S("normed" + nm), t + 1)
                        a.activation(s["h"][:, t, :], self.slots[nm][:, t % 4, :], ACT.Identity, bias=mod[:, self.shift + t, s["k"]:s["k"] + 1]).then_inc(S("h" + nm), 1)

                x, others = self.sts[0], self.sts[1:]
                squares(x, range(DK))
                for s in others:
                    squares(s, range(4))
                deviation(x)
                stream.hi(nc, act, upto)
                for s in others:
                    squares(s, range(4, DK))
                shifted(x)
                for s in others:
                    deviation(s)
                    shifted(s)

            def vector(self, dve):
                S = self.S
                for s in self.sts:
                    nm = s["name"]

                    def normed(t):
                        if t >= 4:
                            dve.wait_ge(S("l" + nm), t - 3)
                        nc.vector.scalar_tensor_tensor(out=self.slots[nm][:, t % 4, :], in0=s["src"][:, t, :], scalar=gain[:, self.which, t, s["k"]:s["k"] + 1],
                                                       in1=self.inverse[nm], op0=ALU.mult, op1=ALU.mult).then_inc(S("normed" + nm), 1)

                    dve.wait_ge(S("rstd" + nm), 1)
                    for t in range(4):
                        normed(t)
                    for t in range(DK):
                        dve.wait_ge(S("h" + nm), t + 1)
                        nc.vector.scalar_tensor_tensor(out=s["l"][:, t, :], in0=self.slots[nm][:, t % 4, :], scalar=mod[:, self.shift + t, s["k"]:s["k"] + 1],
                                                       in1=s["h"][:, t, :].bitcast(F32), op0=ALU.add, op1=ALU.subtract).then_inc(S("l" + nm), 1)
                        if t + 4 < DK:
                            normed(t + 4)

            def ready(self, pe, s, k):
                pe.wait_ge(self.S("l" + s["name"]), k + 1)

        n0 = FIRST2["in"]
        def padded(at, n):
            return Y[:, at:at + 2 * (n + 16)].rearrange("p (c t) -> p c t", c=2)

        QR, KR, FO, VV = XT(0, 4), XT(4, 2), XT(13, 2), XT(16, 6, P)
        QRc, KRc, FOc = XT(6, 4, CTX), XT(8, 2, CTX), XT(15, 2, CTX)
        PL, PLc = padded(9 * T, T), padded(9 * T + 2 * XB, CTX)
        tiles = [("q", i) for i in range(4)] + [("k", i) for i in range(2)] + [("v", 0)] + [("p", i) for i in range(2)] + [("f", i) for i in range(2)]
        plan = {"x": tiles, "c": tiles if update else [t for t in tiles if t[0] in "kv"]}
        where = {"x": {"q": QR, "k": KR, "f": FO, "p": PL[:, :, 8:8 + T], "v": VV[:, 2:6, :]},
                 "c": {"q": QRc, "k": KRc, "f": FOc, "p": PLc[:, :, 8:8 + CTX], "v": VV[:, 0:2, :]}}
        KA = XT(18, 2, CKV)
        QN, QNc = XT(21, 4), XT(25, 4, CTX)
        MX, MXc = tiles_of(mixed, 0, 8), tiles_of(mixed, 8, 8, CTX)
        items = [(QR[:, i, :], T, "q_gain", QN[:, i, :], True) for i in range(4)]
        items += [(KR[:, i, :], T, "k_gain", KA[:, i, CTX:CKV], True) for i in range(2)]
        items += [(KRc[:, i, :], CTX, "k_gain", KA[:, i, 0:CTX], False) for i in range(2)]
        if update:
            items += [(QRc[:, i, :], CTX, "q_gain", QNc[:, i, :], False) for i in range(4)]
        def scratch(i):
            n = items[i][1]
            return mixed[:, i * T:(i + 1) * T] if i < 6 else mixed[:, 6 * T + (i - 6) * CTX:6 * T + (i - 6) * CTX + n]

        S, other = stage()
        norm = Norm(S, 0, SH1, streams, Y[:, 18 * T:26 * T])
        with nc.Block() as block:
            @block.sync
            def _(sp):
                clear(sp, other)
                stream.send(sp, n0 + 11 + RING - 1)
                if layer == 0:
                    sp.wait_ge(constants, 16)

            @block.tensor
            def _(pe):
                def head_sums():
                    for i, (raw, n, g, dst, turn) in enumerate(items):
                        pe.wait_ge(S("sq"), i + 1)
                        if i >= 2:
                            pe.wait_ge(S("log"), i - 1)
                        nc.tensor.matmul(PS[:, 2 + i % 2, 0:n], C("head_ones", P), scratch(i), start=True, stop=True).then_inc(S("sumsq"), 1)

                def turns():
                    for i in range(6):
                        pe.wait_ge(S("normed"), i + 1)
                        if i >= 2:
                            pe.wait_ge(S("sin"), i - 1)
                        nc.tensor.matmul(PS[:, 6 + i % 2, :], C("swap", P), items[i][0], start=True, stop=True).then_inc(S("swapped"), 1)

                norm.tensor(pe)
                for j, t in enumerate(tiles):
                    if j == 7:
                        head_sums()
                    if j == 9:
                        turns()
                    n = n0 + j
                    stream.wait_split(pe, n)
                    first = True
                    for s in streams:
                        if t not in plan[s["name"]]:
                            continue
                        i = plan[s["name"]].index(t)
                        if i >= 2:
                            pe.wait_ge(S("evicted" + s["name"]), i - 1)
                        bank = s["bank"] + i % 2
                        if t[0] != "v":
                            for k in range(DK):
                                if i == 0:
                                    norm.ready(pe, s, k)
                                mm = three(nc, PS[:, bank, 0:s["n"]], tile_of(stream.high(n), k), tile_of(stream.low(n), k),
                                           s["h"][:, k, :], s["l"][:, k, :], k == 0, k == DK - 1, mark(n, first))
                                first = False
                        else:
                            for q in range(s["n"] // P):
                                for k in range(DK):
                                    mm = three(nc, PS[:, bank, q * P:(q + 1) * P], s["h"][:, k, q * P:(q + 1) * P], s["l"][:, k, q * P:(q + 1) * P],
                                               tile_of(stream.high(n), k), tile_of(stream.low(n), k), k == 0, k == DK - 1, mark(n, first))
                                    first = False
                        mm.then_inc(S("product" + s["name"]), 1)

            @block.vector
            def _(dve):
                v = nc.vector

                def rotate(i):
                    dst = items[i][3]
                    dve.wait_ge(S("normed"), i + 1)
                    if i >= 2:
                        dve.wait_ge(S("rotated"), i - 1)
                    v.tensor_tensor(XT(27 + i % 2), items[i][0], C("cos", T), ALU.mult).then_inc(S("cos"), 1)
                    dve.wait_ge(S("swapped"), i + 1)
                    v.tensor_tensor(XT(29 + i % 2), PS[:, 6 + i % 2, :], C("sin", T), ALU.mult).then_inc(S("sin"), 1)
                    dve.wait_ge(S("cos"), i + 1)
                    dve.wait_ge(S("sin"), i + 1)
                    v.tensor_tensor(dst, XT(27 + i % 2), XT(29 + i % 2), ALU.add).then_inc(S("rotated"), 1)

                norm.vector(dve)
                if layer == 0:
                    dve.wait_ge(constants, 16)
                for i, (raw, n, g, dst, turn) in enumerate(items):
                    dve.wait_ge(S("rstd"), i + 1)
                    v.scalar_tensor_tensor(out=raw if turn else dst, in0=raw, scalar=par_col(g), in1=scratch(i),
                                           op0=ALU.mult, op1=ALU.mult).then_inc(S("normed"), 1)
                for i in range(6):
                    rotate(i)

            @block.scalar
            def _(act):
                def head_squares():
                    act.wait_ge(S("evictedx"), 6)
                    act.wait_ge(S("evictedc"), 6 if update else 2)
                    for i, (raw, n, g, dst, turn) in enumerate(items):
                        nc.scalar.activation(scratch(i), raw, ACT.Square).then_inc(S("sq"), 1)

                def head_deviations():
                    for i, (raw, n, g, dst, turn) in enumerate(items):
                        act.wait_ge(S("sumsq"), i + 1)
                        nc.scalar.activation(scratch(i), PS[:, 2 + i % 2, 0:n], ACT.Ln, scale=1.0 / HD, bias=eps).then_inc(S("log"), 1)
                    for i in range(len(items)):
                        act.wait_ge(S("log"), i + 1)
                        nc.scalar.activation(scratch(i), scratch(i), ACT.Exp, scale=-0.5).then_inc(S("rstd"), 1)

                norm.scalar(act, n0 + PARTS)
                for j, t in enumerate(tiles):
                    for s in streams:
                        if t not in plan[s["name"]]:
                            continue
                        i = plan[s["name"]].index(t)
                        act.wait_ge(S("product" + s["name"]), i + 1)
                        dst = where[s["name"]][t[0]]
                        src = PS[:, s["bank"] + i % 2, 0:s["n"]]
                        if t[0] == "v":
                            src = src.rearrange("p (q c) -> p q c", c=P)
                        else:
                            dst = dst[:, t[1], :]
                        nc.scalar.activation(dst, src, ACT.Copy).then_inc(S("evicted" + s["name"]), 1)
                    if j == 6:
                        head_deviations()
                    stream.hi(nc, act, n0 + min(j + 3, 11 + 1))
                    if j == 5:
                        head_squares()

            @block.gpsimd
            def _(pool):
                stream.lo(nc, pool, n0 + 11 + 1)

        above.close()
        above = ExitStack()
        Z = above.enter_context(nc.sbuf_tensor(f"more_tiles{layer}", [P, 9 * T], F32))

        full = streams if update else streams[:1]
        DFT = Z[:, 0:8 * T].rearrange("p (q c t) -> p q c t", q=4, c=2)
        U = {"x": dict(p=PL, f=FO, mx=MX, dft=DFT, norm=1.0, g=Y[:, 27 * T:31 * T], f2=XT(7, 2), cnt=C("count_x", 2 * T).rearrange("p (c t) -> p c t", c=2)),
             "c": dict(p=PLc, f=FOc, mx=MXc, dft=DFT[:, :, :, 0:T:2], norm=float(np.sqrt(2.0)), g=Y[:, 5 * T:7 * T], f2=XT(31, 2, CTX), cnt=C("count_c", 2 * CTX).rearrange("p (c t) -> p c t", c=2))}
        S, other = stage()
        with nc.Block() as block:
            @block.sync
            def _(sp):
                clear(sp, other)
                sp.dma_start(Z[:, 0:8 * T], A["dft"]).then_inc(S("dft"), 16)
                sp.wait_ge(S("dft"), 16)

            @block.gpsimd
            def _(pool):
                g = nc.gpsimd
                done = [0]

                def link(ins):
                    done[0] += 1
                    ins.then_inc(S("pool_step"), 1)
                    pool.wait_ge(S("pool_step"), done[0])

                for s in full:
                    u, n = U[s["name"]], s["n"]
                    w = n + 16
                    s2, s4, s8, mean = (Y[:, i * XB:i * XB + w] for i in range(4))
                    link(g.memset(u["p"][:, :, 0:8], 0.0))
                    link(g.memset(u["p"][:, :, 8 + n:16 + n], 0.0))
                    for c in range(2):
                        src = u["p"][:, c, :]
                        link(g.tensor_tensor(s2[:, 1:w], src[:, 0:w - 1], src[:, 1:w], ALU.add))
                        link(g.tensor_tensor(s4[:, 2:w - 2], s2[:, 1:w - 3], s2[:, 3:w - 1], ALU.add))
                        lo, hi = s2[0:64, 8:8 + n], s4[64:128, 8:8 + n]
                        if c:
                            link(g.tensor_tensor(s8[:, 4:w - 4], s4[:, 2:w - 6], s4[:, 6:w - 2], ALU.add))
                            link(g.tensor_tensor(s2[64:128, 8:8 + n], s8[64:128, 4:4 + n], s8[64:128, 12:12 + n], ALU.add))
                            lo, hi = s8[0:64, 8:8 + n], s2[64:128, 8:8 + n]
                        link(g.tensor_tensor(mean[0:64, 0:n], lo, u["cnt"][0:64, c, :], ALU.mult))
                        link(g.tensor_tensor(mean[64:128, 0:n], hi, u["cnt"][64:128, c, :], ALU.mult))
                        link(g.tensor_tensor(src[:, 8:8 + n], mean[:, 0:n], src[:, 8:8 + n], ALU.subtract))
                    g.memset(mean[:, 0:1], 0.0).then_inc(S("d" + s["name"]), 1)

            @block.tensor
            def _(pe):
                for s in full:
                    nm, n, b = s["name"], s["n"], s["bank"]
                    u, nq = U[nm], s["n"] // P
                    for q in range(nq):
                        if q >= 2:
                            pe.wait_ge(S("g" + nm), q - 1)
                        for c in range(2):
                            mm = nc.tensor.matmul(PS[:, b + q % 2, c * 256:(c + 1) * 256], u["f"][:, c, q * P:(q + 1) * P], C("cs64", 256), start=True, stop=True)
                        mm.then_inc(S("gp" + nm), 1)
                    pe.wait_ge(S("dft"), 16)
                    pe.wait_ge(S("g" + nm), nq)
                    gg = u["g"].rearrange("p (q c x j) -> p q c x j", q=nq, c=2, x=2)
                    for c in range(2):
                        for q in range(nq):
                            for x in range(2):
                                mm = nc.tensor.matmul(PS[:, b + c, 0:n], gg[:, q, c, x, :], u["dft"][:, q, x, :], start=(q == 0 and x == 0), stop=(q == nq - 1 and x == 1))
                        mm.then_inc(S("f" + nm), 1)
                    for c in range(2):
                        pe.wait_ge(S("f_out" + nm), c + 1)
                        nc.tensor.matmul(PS[:, b + 2 + c, 0:n], par_col("w_four", c * P, P), u["f2"][:, c, :], start=True, stop=True).then_inc(S("y" + nm), 1)
                for s in full:
                    nm, n, b = s["name"], s["n"], s["bank"]
                    for c in range(2):
                        pe.wait_ge(S("d" + nm), 1)
                        pe.wait_ge(S("y_out" + nm), c + 1)
                        nc.tensor.matmul(PS[:, b + 2 + c, 0:n], par_col("w_pool", c * P, P), U[nm]["p"][:, c, 8:8 + n], start=True, stop=True).then_inc(S("pooled" + nm), 1)

            @block.scalar
            def _(act):
                a = nc.scalar
                for s in full:
                    nm, n, b = s["name"], s["n"], s["bank"]
                    u, nq = U[nm], s["n"] // P
                    for q in range(nq):
                        act.wait_ge(S("gp" + nm), q + 1)
                        a.activation(u["g"][:, q * T:(q + 1) * T], PS[:, b + q % 2, :], ACT.Copy).then_inc(S("g" + nm), 1)
                    for c in range(2):
                        act.wait_ge(S("f" + nm), c + 1)
                        a.activation(u["f2"][:, c, :], PS[:, b + c, 0:n], ACT.Copy, scale=u["norm"]).then_inc(S("f_out" + nm), 1)
                    for c in range(2):
                        act.wait_ge(S("y" + nm), c + 1)
                        a.activation(u["mx"][:, 6 + c, :], PS[:, b + 2 + c, 0:n], ACT.Copy).then_inc(S("y_out" + nm), 1)
                for s in full:
                    nm, n, b = s["name"], s["n"], s["bank"]
                    for c in range(2):
                        act.wait_ge(S("pooled" + nm), c + 1)
                        a.activation(U[nm]["mx"][:, 4 + c, :], PS[:, b + 2 + c, 0:n], ACT.Copy, scale=par_col("pool_scale", c)).then_inc(S("pool_out"), 1)

        def half(h):
            return slice(64 * (h % 2), 64 * (h % 2) + 64)

        attention(nc, stage, PS, ident, None, heads=8, dv=64, rows=64, blocks=T // P,
                  query=lambda h: QN[half(h), h // 2, :], key=lambda h: KA[half(h), h // 4, :],
                  value=lambda h, kb: VV[:, kb, (h // 4) * 64:(h // 4) * 64 + 64], nkeys=[CKV] * (T // P),
                  scale=HD ** -0.5, out=lambda h: MX[half(h), h // 2, :],
                  probs=[Y[:, a:a + CKV] for a in (12 * T, 12 * T + CKV, 27 * T)], probsT=[XT(0, 6), XT(6, 6)], small=XT(29), part=lambda h: 64 * (h % 2))
        if update:
            attention(nc, stage, PS, ident, None, heads=8, dv=64, rows=64, blocks=CTX // P,
                      query=lambda h: QNc[half(h), h // 2, :], key=lambda h: KA[half(h), h // 4, 0:CTX],
                      value=lambda h, kb: VV[:, kb, (h // 4) * 64:(h // 4) * 64 + 64], nkeys=[CTX] * (CTX // P),
                      scale=HD ** -0.5, out=lambda h: MXc[half(h), h // 2, :],
                      probs=[XT(a)[:, 0:CTX] for a in (12, 13, 14)], probsT=[XT(0, 2), XT(6, 2)], small=XT(29), part=lambda h: 64 * (h % 2))

        def project(first, kt, rhs, gate, split=()):
            S, other = stage()
            chunks = kt
            with nc.Block() as block:
                @block.sync
                def _(sp):
                    clear(sp, other)
                    stream.send(sp, min(first + chunks + RING - 1, NCHUNK2))

                @block.tensor
                def _(pe):
                    for m in range(8):
                        if m >= 4:
                            for s in full:
                                pe.wait_ge(S("added" + s["name"]), m - 3)
                        for k in range(kt):
                            n, b = first + (m * kt + k) // 8, (m * kt + k) % 8
                            if b == 0:
                                stream.wait_split(pe, n)
                            for i, s in enumerate(full):
                                if split and m == 0:
                                    pe.wait_ge(S("low"), len(full) * k + i + 1)
                                high, low = rhs[s["name"]]
                                mm = three(nc, PS[:, s["bank"] + m % 4, 0:s["n"]], tile_of(stream.high(n), b), tile_of(stream.low(n), b),
                                           high[:, k, :], low[:, k, :], k == 0, k == kt - 1, mark(n, i == 0 and b == 0))
                                if k == kt - 1:
                                    mm.then_inc(S("product" + s["name"]), 1)

                @block.scalar
                def _(act):
                    for x, high, low in split:
                        nc.scalar.activation(high, x, ACT.Copy).then_inc(S("high"), 1)
                    stream.hi(nc, act, min(first + chunks + 1, NCHUNK2))

                @block.gpsimd
                def _(pool):
                    stream.lo(nc, pool, min(first + chunks + 1, NCHUNK2))

                @block.vector
                def _(dve):
                    for i, (x, high, low) in enumerate(split):
                        dve.wait_ge(S("high"), i + 1)
                        nc.vector.tensor_tensor(low, x, high.bitcast(F32), ALU.subtract).then_inc(S("low"), 1)
                    for m in range(8):
                        for s in full:
                            dve.wait_ge(S("product" + s["name"]), m + 1)
                            nc.vector.scalar_tensor_tensor(out=s["src"][:, m, :], in0=PS[:, s["bank"] + m % 4, 0:s["n"]], scalar=mod[:, gate + m, s["k"]:s["k"] + 1],
                                                           in1=s["src"][:, m, :], op0=ALU.mult, op1=ALU.add).then_inc(S("added" + s["name"]), 1)

        above.close()
        lower.close()
        with nc.sbuf_tensor(f"mixed_parts{layer}", [P, 24 * T], F32R) as parts:
            MH, ML, MHc, MLc = tiles_of(parts, 0, 8), tiles_of(parts, 8, 8), tiles_of(parts, 16, 8, CTX), tiles_of(parts, 20, 8, CTX)
            split = []
            for k in range(DK):
                split += [(MX[:, k, :], MH[:, k, :], ML[:, k, :]), (MXc[:, k, :], MHc[:, k, :], MLc[:, k, :])][:len(full)]
            project(FIRST2["out"], 8, {"x": (MH, ML), "c": (MHc, MLc)}, GA1, split)
        room.close()

        HC, HCL = (room.enter_context(nc.sbuf_tensor(f"context_again_{part}{layer}", [P, DK, CTX], F32R))[:, :, :] for part in ("high", "low"))
        streams[1].update(h=HC, l=HCL)
        hidden = room.enter_context(nc.sbuf_tensor(f"hidden_parts{layer}", [P, 33 * T], F32R))
        scratch = room.enter_context(nc.sbuf_tensor(f"hidden_scratch{layer}", [P, 8 * T], F32))
        FFN = {"x": (tiles_of(hidden, 0, FH), tiles_of(hidden, 11, FH)),
               "c": (tiles_of(hidden, 22, 2 * FH, CTX)[:, 0:FH, :], tiles_of(hidden, 22, 2 * FH, CTX)[:, FH:2 * FH, :])}
        SG = {"x": tiles_of(scratch, 0, 2), "c": tiles_of(scratch, 4, 2, CTX)}
        PR = {"x": tiles_of(scratch, 2, 2), "c": tiles_of(scratch, 5, 2, CTX)}
        for part in range(2):
            n0 = FIRST2[f"up{part}"]
            S, other = stage()
            norm = None if part else Norm(S, 1, SH2, full, scratch)
            with nc.Block() as block:
                @block.sync
                def _(sp):
                    clear(sp, other)
                    stream.send(sp, n0 + 2 * FH + RING - 1)

                @block.tensor
                def _(pe):
                    if norm is not None:
                        norm.tensor(pe)
                    for t in range(FH):
                        if t >= 2:
                            for s in full:
                                pe.wait_ge(S("act" + s["name"]), t - 1)
                        for j in range(2):
                            gemm(pe, n0 + 2 * t + j, [(PS[:, s["bank"] + 2 * (t % 2) + j, 0:s["n"]], s["h"], s["l"], S(("gate", "up")[j] + s["name"])) for s in full],
                                 norm.ready if norm is not None and t == j == 0 else None)

                @block.scalar
                def _(act):
                    def high(t):
                        for s in full:
                            act.wait_ge(S("act" + s["name"]), t + 1)
                            nc.scalar.activation(FFN[s["name"]][0][:, t, :], PR[s["name"]][:, t % 2, :], ACT.Copy).then_inc(S("high" + s["name"]), 1)

                    if norm is not None:
                        norm.scalar(act, n0 + 1)
                    stream.hi(nc, act, n0 + PARTS)
                    for t in range(FH):
                        for s in full:
                            act.wait_ge(S("gate" + s["name"]), t + 1)
                            if t >= 2:
                                act.wait_ge(S("act" + s["name"]), t - 1)
                            nc.scalar.activation(SG[s["name"]][:, t % 2, :], PS[:, s["bank"] + 2 * (t % 2), 0:s["n"]], ACT.Silu).then_inc(S("silu" + s["name"]), 1)
                        stream.hi(nc, act, n0 + 2 * t + 3)
                        if t:
                            high(t - 1)
                        stream.hi(nc, act, n0 + min(2 * t + 4, 2 * FH + 1))
                    high(FH - 1)

                @block.gpsimd
                def _(pool):
                    def low(t):
                        for s in full:
                            pool.wait_ge(S("high" + s["name"]), t + 1)
                            nc.gpsimd.tensor_tensor(FFN[s["name"]][1][:, t, :], PR[s["name"]][:, t % 2, :], FFN[s["name"]][0][:, t, :].bitcast(F32), ALU.subtract).then_inc(S("low" + s["name"]), 1)

                    for t in range(FH):
                        stream.lo(nc, pool, n0 + 2 * t + 3)
                        if t:
                            low(t - 1)
                        stream.lo(nc, pool, n0 + min(2 * t + 4, 2 * FH + 1))
                    low(FH - 1)

                @block.vector
                def _(dve):
                    if norm is not None:
                        norm.vector(dve)
                    for t in range(FH):
                        for s in full:
                            dve.wait_ge(S("silu" + s["name"]), t + 1)
                            dve.wait_ge(S("up" + s["name"]), t + 1)
                            if t >= 2:
                                dve.wait_ge(S("low" + s["name"]), t - 1)
                            nc.vector.tensor_tensor(PR[s["name"]][:, t % 2, :], PS[:, s["bank"] + 2 * (t % 2) + 1, 0:s["n"]], SG[s["name"]][:, t % 2, :], ALU.mult).then_inc(S("act" + s["name"]), 1)

            project(FIRST2[f"down{part}"], FH, FFN, GA2)
        room.close()

        S, other = stage()
        with nc.Block() as block:
            @block.sync
            def _(sp):
                clear(sp, other)
                clear(sp, WR[3])
                clear(sp, WR[4:])

    S, other = stage()
    with nc.Block() as block:
        @block.sync
        def _(sp):
            sp.dma_start(A["out"], xT[:, :, :].rearrange("p k t -> p (k t)")).then_inc(stored, 16)
            sp.wait_ge(stored, 16)


def blocks(w, m=P):
    k = w.shape[0] // P
    return w.reshape(k, P, w.shape[1]).transpose(1, 0, 2).reshape(P, -1)


def fill(a):
    out = np.zeros((P, CW), np.float32)
    out[:, :a.shape[1]] = a
    return out


OFF = {}
_at = 0
for _name, _n in (("rw", 1664), ("rw_g", 512), ("q_lat", 384), ("kv_lat", 256), ("k_pe", 32), ("mla_g", 512),
                  ("conv_u", 1024), ("conv_g", 512), ("xq", 512), ("xg", 512), ("merge", 4096)):
    OFF[_name] = _at
    _at += _n


def chunks1(I, l):
    w = I["w_in"][l]

    def cols(name, t, n=P):
        a = OFF[name] + t * P
        return blocks(w[:, a:a + n])

    out = [cols("rw", t) for t in range(13)]
    out += [cols("q_lat", t) for t in range(3)] + [cols("kv_lat", t) for t in range(2)]
    kpe = np.zeros((D, P), np.float32)
    kpe[:, 64:96] = w[:, OFF["k_pe"]:OFF["k_pe"] + 32]
    out.append(blocks(kpe))
    uq = I["mla_w_uq"][l]
    heads = [blocks(uq[:, h * 96:(h + 1) * 96]) for h in range(8)]
    for a in (0, 3, 6):
        out.append(fill(np.concatenate(heads[a:a + 3], 1)))
    ukv = I["mla_w_ukv"][l].reshape(256, 8, 128)
    out.append(np.concatenate([blocks(ukv[:, h, :64]) for h in range(8)], 1))
    out.append(blocks(ukv[:, :, 64:].reshape(256, 512)))
    out += [cols("conv_u", t) for t in range(8)]
    out += [cols("xq", t) for t in range(4)]
    mk = I["xattn_w_mem_kv"][l]
    out += [blocks(mk[:, t * P:(t + 1) * P]) for t in range(4)]
    out += [blocks(mk[k * 256:(k + 1) * 256, 512:]) for k in range(4)]
    for name in ("rw_g", "mla_g", "conv_g", "xg"):
        out += [cols(name, t) for t in range(4)]
    ob = I["w_o_branch"][l]
    for m in range(8):
        o = [blocks(ob[n][:, m * P:(m + 1) * P]) for n in range(4)]
        g = [cols("merge", 8 * n + m) for n in range(4)]
        out += [np.concatenate(o[0:2], 1), g[0], g[1], np.concatenate(o[2:4], 1), g[2], g[3]]
    out += [blocks(I["w_out"][l][:, m * P:(m + 1) * P]) for m in range(8)]
    return np.stack(out)


def colsof(v):
    return v.reshape(-1, P).T


def params1(I, l):
    out = np.zeros((P, NPAR), np.float32)

    def put(name, a):
        out[:, PCOL[name]:PCOL[name] + a.shape[1]] = a

    put("b_gate", colsof(I["b_gate"][l].reshape(-1)))
    for name, key in (("mu", "rwkv_mu"), ("w0", "rwkv_w0"), ("a0", "rwkv_a0"), ("k_k", "rwkv_k_k"), ("k_a", "rwkv_k_a"),
                      ("lnx_g", "rwkv_lnx_g"), ("lnx_b", "rwkv_lnx_b"), ("q_norm", "mla_q_norm"), ("kv_norm", "mla_kv_norm"),
                      ("conv_b", "conv_b"), ("cln_g", "conv_ln_g"), ("cln_b", "conv_ln_b"), ("ln_g", "ln_g"), ("ln_b", "ln_b")):
        put(name, colsof(I[key][l]))
    put("r_k", colsof(I["rwkv_r_k"][l].reshape(-1)))
    put("conv_w", I["conv_w"][l].reshape(TAPS, WT, P).transpose(2, 1, 0).reshape(P, WT * TAPS))
    put("w2a2", np.concatenate([I["rwkv_w2"][l], I["rwkv_a2"][l]], 0))
    return out


def consts1():
    out = np.zeros((P, NCST), np.float32)

    def put(name, a, k=0):
        out[:, CCOL[name] + k:CCOL[name] + k + a.shape[1]] = a

    i = np.arange(P)
    row, col = i[:, None], i[None, :]
    put("ident", np.eye(P, dtype=np.float32))
    put("head_ones", (row // 64 == col // 64).astype(np.float32))
    put("ones", np.ones((P, P), np.float32))
    same = row // 64 == col // 64
    put("tri", (same & (row <= col)).astype(np.float32))
    put("tri", (same & (row < col)).astype(np.float32), P)
    put("tri", (same & (row <= col)).astype(np.float32), 2 * P)
    for lv in range(6):
        n = 1 << lv
        low = (row // (2 * n) == col // (2 * n)) & ((row // n) % 2 == 1) & ((col // n) % 2 == 0)
        if lv == 0:
            put("m0", low.astype(np.float32))
        put("lev", low.T.astype(np.float32), lv * P)
    put("causal", np.where(col > row, -1e30, 0.0).astype(np.float32))
    for a in range(32):
        out[64 + (a + 16) % 32, CCOL["swap"] + a] = 1.0
    inv = (np.float32(10000.0) ** (-np.arange(0, 32, 2, dtype=np.float32) / np.float32(32))).astype(np.float32)
    out[64:96, CCOL["freq"]] = np.concatenate([inv, inv])
    out[64:80, CCOL["sign"]] = -1.0
    out[80:96, CCOL["sign"]] = 1.0
    for k, e in enumerate((64e-5, 1e-6, 1e-5, 0.0)):
        out[:, CCOL["eps"] + k] = e
    put("reset", np.broadcast_to((np.arange(T) % CH != 0).astype(np.float32), (P, T)))
    return out


def turned(a):
    return np.ascontiguousarray(a.T.reshape(DK, P, -1).transpose(1, 0, 2).reshape(P, -1))


def layouts(I):
    return {
        "xT": turned(I["x"][0]),
        "memT": turned(I["mem"][0]),
        "pos": np.ascontiguousarray(I["positions"].reshape(T)),
        "cst1": consts1(),
        "par1": np.stack([params1(I, l) for l in range(LAYERS)]),
        "w1": np.stack([chunks1(I, l) for l in range(LAYERS)]),
    }


def pair_diag(w):
    out = np.zeros((P, P), np.float32)
    out[:64, :64], out[64:, 64:] = w[0], w[1]
    return out


def chunks2(I, l):
    w = I["w_in_2"][l]
    out = [blocks(w[:, t * P:(t + 1) * P]) for t in range(4)]
    for g in range(2):
        k = w[:, 512 + 64 * g:512 + 64 * g + 64]
        out.append(blocks(np.concatenate([k, k], 1)))
    out += [blocks(w[:, a:a + P]) for a in (640, 768, 896, 1024, 1152)]
    out += [blocks(I["w_out_2"][l][:, m * P:(m + 1) * P]) for m in range(8)]
    gu = I["w_gate_up_2"][l]
    dn = I["w_down_2"][l]
    for part in range(2):
        for t in range(part * FH, (part + 1) * FH):
            out += [blocks(gu[:, t * P:(t + 1) * P]), blocks(gu[:, FF + t * P:FF + (t + 1) * P])]
        rows = dn[part * FH * P:(part + 1) * FH * P]
        down = np.concatenate([blocks(rows[:, m * P:(m + 1) * P]) for m in range(8)], 1)
        out += [down[:, a:a + CW] for a in range(0, down.shape[1], CW)]
    return np.stack(out)


def params2(I, l):
    out = np.zeros((P, NPAR2), np.float32)

    def put(name, a, k=0):
        out[:, PCOL2[name] + k:PCOL2[name] + k + a.shape[1]] = a

    put("g_mix", colsof(I["g_mix_2"][l]))
    put("g_ffn", colsof(I["g_ffn_2"][l]))
    put("b_ada", colsof(I["b_ada_2"][l]))
    for name in ("q_gain", "k_gain"):
        g = I[name + "_2"][l]
        put(name, np.concatenate([g, g])[:, None])
    put("pool_scale", colsof(I["pool_scale_2"][l]))
    for c in range(2):
        put("w_pool", pair_diag(I["w_pool_2"][l][2 * c:2 * c + 2]), c * P)
        put("w_four", pair_diag(I["w_four_2"][l][2 * c:2 * c + 2]), c * P)
    return out


def dft(n):
    i = np.arange(n)
    a = 2.0 * np.pi * ((i[:, None] * i[None, :]) % n) / n
    both = np.stack([np.cos(a), -np.sin(a)], 1) / np.sqrt(n * 64.0)
    return both.reshape(n // P, P, 2, n).transpose(1, 0, 2, 3).reshape(P, -1).astype(np.float32)


def counts(n):
    t = np.arange(n)
    out = np.zeros((P, 2, n), np.float32)
    for g, w in enumerate((2, 4, 8, 16)):
        lo, hi = np.clip(t - w // 2, 0, n), np.clip(t + w - w // 2, 0, n)
        out[64 * (g % 2):64 * (g % 2) + 64, g // 2, :] = (1.0 / (hi - lo)).astype(np.float32)
    return out.reshape(P, -1)


def consts2():
    out = np.zeros((P, NCST2), np.float32)

    def put(name, a):
        out[:, CCOL2[name]:CCOL2[name] + a.shape[1]] = a

    i = np.arange(P)
    row, col = i[:, None], i[None, :]
    put("ident", np.eye(P, dtype=np.float32))
    put("head_ones", (row // 64 == col // 64).astype(np.float32))
    put("ones", np.ones((P, P), np.float32))
    put("swap", (row == (col ^ 16)).astype(np.float32))
    t = np.arange(T)
    freqs = (np.float32(10000.0) ** (-np.arange(16, dtype=np.float32) / np.float32(16))).astype(np.float32)
    place = np.stack([t // 64, t % 64]).astype(np.float32)
    r = i % 64
    ang = (place[r // 32] * freqs[r % 16][:, None]).astype(np.float32).astype(np.float64)
    put("cos", np.cos(ang).astype(np.float32))
    put("sin", (np.sin(ang) * np.where((r // 16) % 2, 1.0, -1.0)[:, None]).astype(np.float32))
    j = np.arange(64)
    a = 2.0 * np.pi * ((j[:, None] * j[None, :]) % 64) / 64
    put("cs64", np.concatenate([pair_diag(np.stack([f, f])) for f in (np.cos(a), np.sin(a))], 1).astype(np.float32))
    put("count_x", counts(T))
    put("count_c", counts(CTX))
    out[:, CCOL2["eps"]] = 1e-6
    return out


def layouts2(I):
    return {
        "ctxT": turned(I["ctx_2"][0]),
"cond": np.ascontiguousarray(np.stack([I["c_2"].reshape(D), I["c_ctx_2"].reshape(D)])),
        "ada": np.stack([I["w_ada_2"][l].T.reshape(48, P, D) for l in range(LAYERS)]),
        "cst2": consts2(),
        "par2": np.stack([params2(I, l) for l in range(LAYERS)]),
        "dft": dft(T),
        "w2": np.stack([chunks2(I, l) for l in range(LAYERS)]),
    }


_INS = ["x", "mem", "positions", "w_in", "b_gate", "rwkv_mu", "rwkv_w0", "rwkv_w2", "rwkv_a0", "rwkv_a2", "rwkv_k_k",
        "rwkv_k_a", "rwkv_r_k", "rwkv_lnx_g", "rwkv_lnx_b", "mla_q_norm", "mla_w_uq", "mla_kv_norm", "mla_w_ukv",
        "conv_w", "conv_b", "conv_ln_g", "conv_ln_b", "xattn_w_mem_kv", "w_o_branch", "w_out", "ln_g", "ln_b", "c_2",
        "ctx_2", "c_ctx_2", "w_ada_2", "b_ada_2", "g_mix_2", "g_ffn_2", "w_in_2", "q_gain_2", "k_gain_2", "w_pool_2",
        "pool_scale_2", "w_four_2", "w_out_2", "w_gate_up_2", "w_down_2"]


def kernel(**inputs):
    import concourse.bacc as bacc
    from concourse.bass_utils import run_bass_kernel_spmd as run

    I = {name: np.asarray(inputs[name]) for name in _INS}
    nc = bacc.Bacc("TRN2", target_bir_lowering=False, num_devices=1)
    arrays, A = {}, {}
    for name, a in {**layouts(I), **layouts2(I)}.items():
        a = np.ascontiguousarray(a)
        arrays[f"in_{name}"] = a
        A[name] = nc.dram_tensor(f"in_{name}", a.shape, mybir.dt.from_np(a.dtype), kind="ExternalInput").ap()
    A["out"] = nc.dram_tensor("out_0", (P, DK * T), F32, kind="ExternalOutput").ap()
    build(nc, A)
    r = run(nc, [arrays], core_ids=[0])
    got = r.results[0]["out_0"]
    return np.ascontiguousarray(got.reshape(P, DK, T).transpose(2, 1, 0).reshape(1, T, D))
```
